# Optimizing a Trainium2 kernel written in Bass

```python
import math
import jax
import jax.numpy as jnp
from jax import lax
import numpy as np
import jax, jax.numpy as jnp

D_MODEL = 1024
BATCH = 1
SEQ = 256
DEPTH = 2

N_MIXERS = 4
F32 = jnp.float32
ROPE_THETA = 10000.0
DEEPNORM_ALPHA = (2.0 * DEPTH) ** 0.25
DEEPNORM_BETA = (8.0 * DEPTH) ** -0.25
LN_EPS = 1e-5
NEG_INF = -1e30
D_FF = ((8 * D_MODEL + 3 * 256 - 1) // (3 * 256)) * 256

RWKV_HEAD_DIM = 64
RWKV_HEADS = D_MODEL // RWKV_HEAD_DIM
RWKV_LORA_DECAY = 64
RWKV_LORA_ICLR = 64
RWKV_LORA_GATE = 128
RWKV_GN_EPS = 64e-5
GDN_HEAD_DIM = 128
GDN_HEADS = D_MODEL // GDN_HEAD_DIM
GDN_CONV = 4
GDN_CHUNK = 64
GDN_QKV = 3 * GDN_HEADS * GDN_HEAD_DIM
GDN_PROJ = 4 * GDN_HEADS * GDN_HEAD_DIM + 2 * GDN_HEADS
DIFF_HEADS = 8
DIFF_HEAD_DIM = D_MODEL // (2 * DIFF_HEADS)
ATTN_Q_BLOCK = 128
SWA_HEAD_DIM = 64
SWA_Q_HEADS = D_MODEL // SWA_HEAD_DIM
SWA_KV_HEADS = SWA_Q_HEADS // 8
SWA_WINDOW = 128
SWA_QKV = (SWA_Q_HEADS + 2 * SWA_KV_HEADS) * SWA_HEAD_DIM


def _layer_norm(x, g, b):
    xf = x.astype(F32)
    mu = jnp.mean(xf, -1, keepdims=True)
    var = jnp.mean(jnp.square(xf - mu), -1, keepdims=True)
    return ((xf - mu) * lax.rsqrt(var + LN_EPS) * g + b).astype(x.dtype)

def _rms_norm(x, g, eps):
    xf = x.astype(F32)
    return xf * lax.rsqrt(jnp.mean(xf * xf, -1, keepdims=True) + eps) * g

def _l2norm(x, eps=1e-6):
    xf = x.astype(F32)
    return (xf * lax.rsqrt(jnp.sum(xf * xf, -1, keepdims=True) + eps)).astype(x.dtype)

def _rope(x, pos):
    d = x.shape[-1]
    inv = ROPE_THETA ** (-jnp.arange(0, d, 2, dtype=F32) / d)
    ang = pos.astype(F32)[:, None] * inv[None, :]
    cos = jnp.cos(ang)[None, :, None, :]
    sin = jnp.sin(ang)[None, :, None, :]
    x1, x2 = jnp.split(x.astype(F32), 2, axis=-1)
    return jnp.concatenate([x1 * cos - x2 * sin, x2 * cos + x1 * sin], -1).astype(x.dtype)

def _token_shift(x):
    return jnp.pad(x, ((0, 0), (1, 0), (0, 0)))[:, :-1]

def _causal_depthwise_conv(x, w):
    K, C = w.shape
    return lax.conv_general_dilated(x, w[:, None, :].astype(x.dtype), window_strides=(1,),
                                    padding=[(K - 1, 0)], dimension_numbers=('NWC', 'WIO', 'NWC'),
                                    feature_group_count=C)

def _rwkv7_mixer(u, mu, w_rkv, w0, w1, w2, a0, a1, a2, g1, g2, k_k, k_a, r_k, gn_g, gn_b, w_out):
    B, T, D = u.shape
    H, N = RWKV_HEADS, RWKV_HEAD_DIM
    xx = _token_shift(u) - u
    lerp = lambda i: u + xx * mu[i]
    r = lerp(0) @ w_rkv[0]
    k = lerp(1) @ w_rkv[1]
    v = lerp(2) @ w_rkv[2]
    w_log = -jax.nn.softplus(-(w0 + jnp.tanh(lerp(3) @ w1) @ w2)) - 0.5
    a = jax.nn.sigmoid(a0 + (lerp(4) @ a1) @ a2)
    g = jax.nn.sigmoid(lerp(5) @ g1) @ g2
    heads = lambda t: t.reshape(B, T, H, N)
    kk = _l2norm(heads(k * k_k))
    k = k * (1 + (a - 1) * k_a)
    r, k, v, a = heads(r), heads(k), heads(v), heads(a)
    decay = jnp.exp(-jnp.exp(heads(w_log).astype(F32)))
    tm = lambda t: jnp.moveaxis(t.astype(F32), 1, 0)

    def step(S, inp):
        r_t, k_t, v_t, w_t, a_t, b_t = inp
        sa = jnp.einsum('bhvk,bhk->bhv', S, a_t)
        S = S * w_t[:, :, None, :] + sa[..., None] * b_t[:, :, None, :] + v_t[..., None] * k_t[:, :, None, :]
        return S, jnp.einsum('bhvk,bhk->bhv', S, r_t)

    S0 = jnp.zeros((B, H, N, N), F32)
    _, y = lax.scan(step, S0, (tm(r), tm(k), tm(v), jnp.moveaxis(decay, 1, 0), tm(-kk), tm(kk * a)))
    y = jnp.moveaxis(y, 0, 1)
    mean = jnp.mean(y, -1, keepdims=True)
    var = jnp.mean(jnp.square(y - mean), -1, keepdims=True)
    y = ((y - mean) * lax.rsqrt(var + RWKV_GN_EPS)).reshape(B, T, D) * gn_g + gn_b
    bonus = jnp.sum((r * k * r_k).astype(F32), -1, keepdims=True) * v.astype(F32)
    y = (y + bonus.reshape(B, T, D)).astype(u.dtype)
    return (y * g) @ w_out

def _chunk_gated_delta_rule(q, k, v, g, beta):
    B, T, H, dk = q.shape
    dv = v.shape[-1]
    C = GDN_CHUNK
    n = T // C
    chunks = lambda t: jnp.moveaxis(t.astype(F32).reshape(B, n, C, H, -1), 3, 1)
    q, k, v = chunks(q), chunks(k), chunks(v)
    beta = chunks(beta[..., None])
    gc = jnp.cumsum(chunks(g[..., None])[..., 0], axis=-1)
    k_beta, v_beta = k * beta, v * beta
    idx = jnp.arange(C)
    causal = idx[:, None] >= idx[None, :]
    strict = idx[:, None] > idx[None, :]
    decay = jnp.exp(jnp.where(causal, gc[..., :, None] - gc[..., None, :], -jnp.inf))
    L = jnp.where(strict, jnp.einsum('bhnid,bhnjd->bhnij', k_beta, k) * decay, 0.0)
    eye = jnp.eye(C, dtype=F32)
    tinv = lax.linalg.triangular_solve(eye + L, jnp.broadcast_to(eye, L.shape), left_side=True, lower=True)
    u_c = tinv @ v_beta
    w_c = tinv @ (k_beta * jnp.exp(gc)[..., None])
    a_intra = jnp.where(causal, jnp.einsum('bhnid,bhnjd->bhnij', q, k) * decay, 0.0)
    q_dec = q * jnp.exp(gc)[..., None]
    k_dec = k * jnp.exp(gc[..., -1:] - gc)[..., None]
    g_last = jnp.exp(gc[..., -1])

    def step(S, inp):
        q_i, k_i, u_i, w_i, a_i, gl = inp
        v_new = u_i - w_i @ S
        o = q_i @ S + a_i @ v_new
        S = S * gl[..., None, None] + jnp.einsum('bhck,bhcv->bhkv', k_i, v_new)
        return S, o

    xs = tuple(jnp.moveaxis(t, 2, 0) for t in (q_dec, k_dec, u_c, w_c, a_intra, g_last))
    _, o = lax.scan(step, jnp.zeros((B, H, dk, dv), F32), xs)
    return jnp.transpose(o, (1, 0, 3, 2, 4)).reshape(B, T, H, dv)

def _gated_deltanet_mixer(u, w_in, conv_w, a_log, dt_bias, norm_g, w_out):
    B, T, _ = u.shape
    H, d = GDN_HEADS, GDN_HEAD_DIM
    hd = H * d
    proj = u @ w_in
    qkv = jax.nn.silu(_causal_depthwise_conv(proj[..., :3 * hd], conv_w))
    z = proj[..., 3 * hd:4 * hd].reshape(B, T, H, d)
    b_in = proj[..., 4 * hd:4 * hd + H]
    a_in = proj[..., 4 * hd + H:]
    q = _l2norm(qkv[..., :hd].reshape(B, T, H, d)) * d ** -0.5
    k = _l2norm(qkv[..., hd:2 * hd].reshape(B, T, H, d))
    v = qkv[..., 2 * hd:].reshape(B, T, H, d)
    beta = jax.nn.sigmoid(b_in.astype(F32))
    g = -jnp.exp(a_log.astype(F32)) * jax.nn.softplus(a_in.astype(F32) + dt_bias)
    o = _chunk_gated_delta_rule(q, k, v, g, beta)
    o = _rms_norm(o, norm_g, 1e-6) * jax.nn.silu(z.astype(F32))
    return o.reshape(B, T, hd).astype(u.dtype) @ w_out

def _diff_attention_mixer(u, pos, w_in, lam_p, subln_g, w_out, lam_init):
    B, T, D = u.shape
    H, d, Qb = DIFF_HEADS, DIFF_HEAD_DIM, ATTN_Q_BLOCK
    proj = u @ w_in
    q = _rope(proj[..., :D].reshape(B, T, 2 * H, d), pos) * d ** -0.5
    k = _rope(proj[..., D:2 * D].reshape(B, T, 2 * H, d), pos)
    v = proj[..., 2 * D:].reshape(B, T, H, 2 * d)
    lp = lam_p.astype(F32)
    lam = jnp.exp(jnp.sum(lp[0] * lp[1])) - jnp.exp(jnp.sum(lp[2] * lp[3])) + lam_init
    nb = T // Qb
    qb = jnp.moveaxis(q.reshape(B, nb, Qb, 2 * H, d), 1, 0)
    kf, vf = k.astype(F32), v.astype(F32)
    kpos = jnp.arange(T)

    def block(args):
        q_blk, i = args
        s = jnp.einsum('bqhd,bkhd->bhqk', q_blk.astype(F32), kf)
        qpos = i * Qb + jnp.arange(Qb)
        s = jnp.where(kpos[None, :] <= qpos[:, None], s, NEG_INF)
        p = jax.nn.softmax(s, axis=-1).reshape(B, H, 2, Qb, T)
        attn = p[:, :, 0] - lam * p[:, :, 1]
        return jnp.einsum('bhqk,bkhe->bqhe', attn, vf)

    o = lax.map(block, (qb, jnp.arange(nb)))
    o = jnp.moveaxis(o, 0, 1).reshape(B, T, H, 2 * d)
    o = _rms_norm(o, subln_g, 1e-5) * (1.0 - lam_init)
    return o.reshape(B, T, D).astype(u.dtype) @ w_out

def _swa_sink_mixer(u, pos, w_qkv, b_qkv, sinks, w_out, b_out):
    B, T, _ = u.shape
    Hq, Hkv, d, W = SWA_Q_HEADS, SWA_KV_HEADS, SWA_HEAD_DIM, SWA_WINDOW
    G = Hq // Hkv
    nb = T // W
    proj = u @ w_qkv + b_qkv
    q = _rope(proj[..., :Hq * d].reshape(B, T, Hq, d), pos) * d ** -0.5
    k = _rope(proj[..., Hq * d:(Hq + Hkv) * d].reshape(B, T, Hkv, d), pos)
    v = proj[..., (Hq + Hkv) * d:].reshape(B, T, Hkv, d)
    qb = q.astype(F32).reshape(B, nb, W, Hkv, G, d)

    def band(t):
        tb = t.astype(F32).reshape(B, nb, W, Hkv, d)
        prev = jnp.pad(tb, ((0, 0), (1, 0), (0, 0), (0, 0), (0, 0)))[:, :-1]
        return jnp.concatenate([prev, tb], axis=2)

    kb, vb = band(k), band(v)
    s = jnp.einsum('bnqhgd,bnkhd->bnhgqk', qb, kb)
    qi = jnp.arange(W)[:, None]
    kj = jnp.arange(2 * W)[None, :]
    rel = W + qi - kj
    in_window = (rel >= 0) & (rel < W)
    key_pos = jnp.arange(nb)[:, None] * W + jnp.arange(2 * W)[None, :] - W
    valid = in_window[None, :, :] & (key_pos >= 0)[:, None, :]
    s = jnp.where(valid[None, :, None, None], s, NEG_INF)
    sink = sinks.astype(F32).reshape(Hkv, G)[None, None, :, :, None, None]
    m = jnp.maximum(jnp.max(s, -1, keepdims=True), sink)
    p = jnp.exp(s - m)
    p = p / (jnp.sum(p, -1, keepdims=True) + jnp.exp(sink - m))
    o = jnp.einsum('bnhgqk,bnkhd->bnqhgd', p, vb).reshape(B, T, Hq * d)
    return o.astype(u.dtype) @ w_out + b_out

def _count(m):
    return len(range(m, DEPTH, N_MIXERS))

def first_inputs(seed: int = 0) -> dict:
    key = jax.random.key(seed)
    keys = iter(jax.random.split(key, 48))

    def nrm(shape, std):
        return jax.random.normal(next(keys), shape, F32) * std

    def unif(shape, lo, hi):
        return jax.random.uniform(next(keys), shape, F32, lo, hi)

    D = D_MODEL
    nA, nB, nC, nD = (_count(m) for m in range(N_MIXERS))
    beta = DEEPNORM_BETA
    gdn_hd = GDN_HEADS * GDN_HEAD_DIM
    swa_hd = SWA_Q_HEADS * SWA_HEAD_DIM
    dt = jnp.exp(unif((nB, GDN_HEADS), math.log(1e-3), math.log(1e-1)))
    return {
        'x': nrm((BATCH, SEQ, D), 1.0),
        'c': nrm((BATCH, D), 1.0),
        'ada_w': nrm((DEPTH, D, 6 * D), 0.1 * D ** -0.5),
        'ada_b': nrm((DEPTH, 6 * D), 0.02),
        'ln_g': 1.0 + nrm((DEPTH, 2, D), 0.02),
        'ln_b': nrm((DEPTH, 2, D), 0.02),
        'ffn_w_in': nrm((DEPTH, D, 2 * D_FF), D ** -0.5),
        'ffn_w_out': nrm((DEPTH, D_FF, D), beta * D_FF ** -0.5),
        'rwkv_mu': unif((nA, 6, D), 0.0, 1.0),
        'rwkv_w_rkv': nrm((nA, 3, D, D), D ** -0.5),
        'rwkv_w0': unif((nA, D), -6.0, 1.0),
        'rwkv_w1': nrm((nA, D, RWKV_LORA_DECAY), D ** -0.5),
        'rwkv_w2': nrm((nA, RWKV_LORA_DECAY, D), 0.5 * RWKV_LORA_DECAY ** -0.5),
        'rwkv_a0': nrm((nA, D), 0.1),
        'rwkv_a1': nrm((nA, D, RWKV_LORA_ICLR), D ** -0.5),
        'rwkv_a2': nrm((nA, RWKV_LORA_ICLR, D), 0.5 * RWKV_LORA_ICLR ** -0.5),
        'rwkv_g1': nrm((nA, D, RWKV_LORA_GATE), D ** -0.5),
        'rwkv_g2': nrm((nA, RWKV_LORA_GATE, D), RWKV_LORA_GATE ** -0.5),
        'rwkv_k_k': 1.0 + nrm((nA, D), 0.1),
        'rwkv_k_a': 1.0 + nrm((nA, D), 0.1),
        'rwkv_r_k': nrm((nA, RWKV_HEADS, RWKV_HEAD_DIM), 0.1),
        'rwkv_gn_g': 1.0 + nrm((nA, D), 0.02),
        'rwkv_gn_b': nrm((nA, D), 0.02),
        'rwkv_w_out': nrm((nA, D, D), beta * D ** -0.5),
        'gdn_w_in': nrm((nB, D, GDN_PROJ), D ** -0.5),
        'gdn_conv': nrm((nB, GDN_CONV, GDN_QKV), GDN_CONV ** -0.5),
        'gdn_a_log': jnp.log(unif((nB, GDN_HEADS), 1.0, 16.0)),
        'gdn_dt_bias': dt + jnp.log(-jnp.expm1(-dt)),
        'gdn_norm_g': 1.0 + nrm((nB, GDN_HEAD_DIM), 0.02),
        'gdn_w_out': nrm((nB, gdn_hd, D), beta * gdn_hd ** -0.5),
        'diff_w_in': nrm((nC, D, 3 * D), D ** -0.5),
        'diff_lambda': nrm((nC, 4, DIFF_HEAD_DIM), 0.1),
        'diff_subln_g': 1.0 + nrm((nC, 2 * DIFF_HEAD_DIM), 0.02),
        'diff_w_out': nrm((nC, D, D), beta * D ** -0.5),
        'swa_w_qkv': nrm((nD, D, SWA_QKV), D ** -0.5),
        'swa_b_qkv': nrm((nD, SWA_QKV), 0.02),
        'swa_sinks': nrm((nD, SWA_Q_HEADS), 1.0),
        'swa_w_out': nrm((nD, swa_hd, D), beta * swa_hd ** -0.5),
        'swa_b_out': nrm((nD, D), 0.02),
    }

def first_block(x, c, ada_w, ada_b, ln_g, ln_b, ffn_w_in, ffn_w_out,
              rwkv_mu, rwkv_w_rkv, rwkv_w0, rwkv_w1, rwkv_w2, rwkv_a0, rwkv_a1, rwkv_a2,
              rwkv_g1, rwkv_g2, rwkv_k_k, rwkv_k_a, rwkv_r_k, rwkv_gn_g, rwkv_gn_b, rwkv_w_out,
              gdn_w_in, gdn_conv, gdn_a_log, gdn_dt_bias, gdn_norm_g, gdn_w_out,
              diff_w_in, diff_lambda, diff_subln_g, diff_w_out,
              swa_w_qkv, swa_b_qkv, swa_sinks, swa_w_out, swa_b_out):
    T = x.shape[1]
    pos = jnp.arange(T)
    cond = jax.nn.silu(c)
    for i in range(DEPTH):
        mod = (cond @ ada_w[i] + ada_b[i])[:, None, :]
        sh1, sc1, ga1, sh2, sc2, ga2 = jnp.split(mod, 6, axis=-1)
        u = x * (1 + sc1) + sh1
        m, j = i % N_MIXERS, i // N_MIXERS
        if m == 0:
            y = _rwkv7_mixer(u, rwkv_mu[j], rwkv_w_rkv[j], rwkv_w0[j], rwkv_w1[j], rwkv_w2[j],
                             rwkv_a0[j], rwkv_a1[j], rwkv_a2[j], rwkv_g1[j], rwkv_g2[j],
                             rwkv_k_k[j], rwkv_k_a[j], rwkv_r_k[j], rwkv_gn_g[j], rwkv_gn_b[j],
                             rwkv_w_out[j])
        elif m == 1:
            y = _gated_deltanet_mixer(u, gdn_w_in[j], gdn_conv[j], gdn_a_log[j], gdn_dt_bias[j],
                                      gdn_norm_g[j], gdn_w_out[j])
        elif m == 2:
            lam_init = 0.8 - 0.6 * math.exp(-0.3 * i)
            y = _diff_attention_mixer(u, pos, diff_w_in[j], diff_lambda[j], diff_subln_g[j],
                                      diff_w_out[j], lam_init)
        else:
            y = _swa_sink_mixer(u, pos, swa_w_qkv[j], swa_b_qkv[j], swa_sinks[j], swa_w_out[j],
                                swa_b_out[j])
        x = _layer_norm(DEEPNORM_ALPHA * x + (1 + ga1) * y, ln_g[i, 0], ln_b[i, 0])
        u = x * (1 + sc2) + sh2
        gate, up = jnp.split(u @ ffn_w_in[i], 2, axis=-1)
        y = (jax.nn.silu(gate) * up) @ ffn_w_out[i]
        x = _layer_norm(DEEPNORM_ALPHA * x + (1 + ga2) * y, ln_g[i, 1], ln_b[i, 1])
    return x


N_META = 16
BLOCK = 128
SSD_HEADS = 8
SSD_HEAD_DIM = 64
SSD_D = SSD_HEADS * SSD_HEAD_DIM
SSD_GROUPS = 2
SSD_STATE = 64
SSD_CONV = 4
SSD_CONV_DIM = SSD_D + 2 * SSD_GROUPS * SSD_STATE
FOX_HEADS = 4
FOX_HEAD_DIM = 64
FOX_D = FOX_HEADS * FOX_HEAD_DIM
MLA_HEADS = 4
MLA_Q_LORA = 256
MLA_KV_LORA = 128
MLA_NOPE = 64
MLA_ROPE = 32
MLA_V = 64
MLA_D = MLA_HEADS * MLA_V
D_MIX = SSD_D + FOX_D + MLA_D
IN_SIZES = [SSD_D, SSD_CONV_DIM, SSD_HEADS,
            FOX_D, FOX_D, FOX_D, FOX_HEADS,
            MLA_Q_LORA, MLA_KV_LORA, MLA_ROPE]
N_IN = sum(IN_SIZES)
IN_SPLITS = [int(s) for s in np.cumsum(IN_SIZES)[:-1]]
D_FF_2 = 2816
ALPHA = (2 * DEPTH) ** 0.25
BETA = (8 * DEPTH) ** -0.25
EPS = 1e-5


def layer_norm(x, g, b):
    xf = x.astype(jnp.float32)
    mu = jnp.mean(xf, -1, keepdims=True)
    var = jnp.mean(jnp.square(xf - mu), -1, keepdims=True)
    return ((xf - mu) * lax.rsqrt(var + EPS) * g + b).astype(x.dtype)

def rms_norm(x, g):
    xf = x.astype(jnp.float32)
    y = xf * lax.rsqrt(jnp.mean(jnp.square(xf), -1, keepdims=True) + EPS)
    return (y * g).astype(x.dtype)

def swiglu(x, w_gate, w_up, w_down):
    return (jax.nn.silu(x @ w_gate) * (x @ w_up)) @ w_down

def rope(x, cos, sin):
    x1, x2 = jnp.split(x.astype(jnp.float32), 2, axis=-1)
    return jnp.concatenate([x1 * cos - x2 * sin, x2 * cos + x1 * sin], -1).astype(x.dtype)

def block_edges(total):
    return sorted(set([0] + list(range(N_META, total, BLOCK)) + [total]))

def blocked_causal_attention(logits_fn, v):
    total = v.shape[1]
    outs = []
    edges = block_edges(total)
    for q0, q1 in zip(edges[:-1], edges[1:]):
        s = logits_fn(q0, q1).astype(jnp.float32)
        causal = jnp.arange(q1)[None, :] <= jnp.arange(q0, q1)[:, None]
        s = jnp.where(causal, s, -jnp.inf)
        p = jax.nn.softmax(s, axis=-1).astype(v.dtype)
        outs.append(jnp.einsum('bhqk,bkhd->bqhd', p, v[:, :q1]))
    return jnp.concatenate(outs, axis=1)

def causal_depthwise_conv(x, w, bias):
    out = lax.conv_general_dilated(
        x, w[:, None, :], window_strides=(1,), padding=[(SSD_CONV - 1, 0)],
        dimension_numbers=('NWC', 'WIO', 'NWC'), feature_group_count=x.shape[-1])
    return out + bias

def ssd_chunked(x, dt, A, Bm, Cm):
    b, l, h, p = x.shape
    n = Bm.shape[-1]
    nc = l // BLOCK
    x = x.reshape(b, nc, BLOCK, h, p)
    dt = dt.reshape(b, nc, BLOCK, h)
    Bm = Bm.reshape(b, nc, BLOCK, h, n)
    Cm = Cm.reshape(b, nc, BLOCK, h, n)
    a = jnp.moveaxis(dt * A, -1, 1)
    a_cum = jnp.cumsum(a, axis=-1)
    xdt = x * dt[..., None]
    idx = jnp.arange(BLOCK)
    causal = idx[:, None] >= idx[None, :]
    seg = jnp.exp(jnp.where(causal, a_cum[..., :, None] - a_cum[..., None, :], -jnp.inf))
    cb = jnp.einsum('bclhn,bcshn->bhcls', Cm, Bm)
    y_diag = jnp.einsum('bhcls,bcshp->bclhp', cb * seg, xdt)
    decay_states = jnp.exp(a_cum[..., -1:] - a_cum)
    states = jnp.einsum('bclhn,bhcl,bclhp->bchpn', Bm, decay_states, xdt)
    chunk_decay = jnp.exp(a_cum[..., -1])

    def step(s, inp):
        st, dec = inp
        return s * dec[..., None, None] + st, s

    init = jnp.zeros((b, h, p, n), x.dtype)
    _, prev = lax.scan(step, init, (jnp.moveaxis(states, 1, 0), jnp.moveaxis(chunk_decay, 2, 0)))
    prev = jnp.moveaxis(prev, 0, 1)
    y_off = jnp.einsum('bclhn,bchpn,bhcl->bclhp', Cm, prev, jnp.exp(a_cum))
    return (y_diag + y_off).reshape(b, l, h, p)

def ssd_mixer(z, xbc, dt_raw, conv_w, conv_b, dt_bias, a_log, d_skip, norm_g):
    b, L, _ = xbc.shape
    f32 = jnp.float32
    xbc = jax.nn.silu(causal_depthwise_conv(xbc, conv_w, conv_b)).astype(f32)
    xs, Bm, Cm = jnp.split(xbc, [SSD_D, SSD_D + SSD_GROUPS * SSD_STATE], axis=-1)
    xs = xs.reshape(b, L, SSD_HEADS, SSD_HEAD_DIM)
    rep = SSD_HEADS // SSD_GROUPS
    Bm = jnp.repeat(Bm.reshape(b, L, SSD_GROUPS, SSD_STATE), rep, axis=2)
    Cm = jnp.repeat(Cm.reshape(b, L, SSD_GROUPS, SSD_STATE), rep, axis=2)
    dt = jax.nn.softplus(dt_raw.astype(f32) + dt_bias.astype(f32))
    A = -jnp.exp(a_log.astype(f32))
    pad = (-L) % BLOCK
    padf = lambda t: jnp.pad(t, ((0, 0), (pad, 0)) + ((0, 0),) * (t.ndim - 2))
    y = ssd_chunked(padf(xs), padf(dt), A, padf(Bm), padf(Cm))[:, pad:]
    y = y + d_skip.astype(f32)[:, None] * xs
    y = y.reshape(b, L, SSD_D) * jax.nn.silu(z.astype(f32))
    y = rms_norm(y.reshape(b, L, SSD_GROUPS, SSD_D // SSD_GROUPS), 1.0).reshape(b, L, SSD_D) * norm_g
    return y.astype(z.dtype)

def fox_mixer(q, k, v, f_raw, f_b):
    b, L, _ = q.shape
    q = q.reshape(b, L, FOX_HEADS, FOX_HEAD_DIM)
    k = k.reshape(b, L, FOX_HEADS, FOX_HEAD_DIM)
    v = v.reshape(b, L, FOX_HEADS, FOX_HEAD_DIM)
    log_f = jax.nn.log_sigmoid(f_raw.astype(jnp.float32) + f_b.astype(jnp.float32))
    c = jnp.cumsum(log_f, axis=1).transpose(0, 2, 1)
    scale = FOX_HEAD_DIM ** -0.5

    def logits(q0, q1):
        s = jnp.einsum('bqhd,bkhd->bhqk', q[:, q0:q1], k[:, :q1]).astype(jnp.float32) * scale
        return s + (c[:, :, q0:q1, None] - c[:, :, None, :q1])

    return blocked_causal_attention(logits, v).reshape(b, L, FOX_D)

def mla_mixer(cq, ckv, k_rope, q_norm_g, w_uq, kv_norm_g, w_ukv, cos, sin):
    b, L, _ = cq.shape
    qh = (rms_norm(cq, q_norm_g) @ w_uq).reshape(b, L, MLA_HEADS, MLA_NOPE + MLA_ROPE)
    q_nope, q_rope = qh[..., :MLA_NOPE], qh[..., MLA_NOPE:]
    q_rope = rope(q_rope, cos[None, :, None, :], sin[None, :, None, :])
    kv = (rms_norm(ckv, kv_norm_g) @ w_ukv).reshape(b, L, MLA_HEADS, MLA_NOPE + MLA_V)
    k_nope, v = kv[..., :MLA_NOPE], kv[..., MLA_NOPE:]
    k_rope = rope(k_rope, cos[None], sin[None])
    scale = (MLA_NOPE + MLA_ROPE) ** -0.5

    def logits(q0, q1):
        s = jnp.einsum('bqhd,bkhd->bhqk', q_nope[:, q0:q1], k_nope[:, :q1])
        s = s + jnp.einsum('bqhr,bkr->bhqk', q_rope[:, q0:q1], k_rope[:, :q1])
        return s * scale

    return blocked_causal_attention(logits, v).reshape(b, L, MLA_D)

def second_inputs(seed: int = 0) -> dict:
    key = jax.random.key(seed)
    ks = iter(jax.random.split(key, 48))
    f32 = jnp.float32
    Dm, F, NL = D_MODEL, D_FF_2, DEPTH

    def nrm(shape, scale):
        return jax.random.normal(next(ks), shape, f32) * scale

    def gain(shape):
        return 1.0 + nrm(shape, 0.02)

    u = jax.random.uniform(next(ks), (NL, SSD_HEADS), f32)
    dt0 = jnp.exp(u * (np.log(0.1) - np.log(0.001)) + np.log(0.001))
    dt_bias = dt0 + jnp.log(-jnp.expm1(-dt0))
    a_log = jnp.log(jax.random.uniform(next(ks), (NL, SSD_HEADS), f32, 1.0, 16.0))
    return {
        "x": nrm((BATCH, SEQ, Dm), 1.0),
        "meta": nrm((N_META, Dm), 1.0),
        "ffn1_w_gate": nrm((NL, Dm, F), Dm ** -0.5),
        "ffn1_w_up": nrm((NL, Dm, F), Dm ** -0.5),
        "ffn1_w_down": nrm((NL, F, Dm), F ** -0.5 * BETA),
        "ln1_g": gain((NL, Dm)),
        "ln1_b": nrm((NL, Dm), 0.02),
        "w_in": nrm((NL, Dm, N_IN), Dm ** -0.5),
        "conv_w": nrm((NL, SSD_CONV, SSD_CONV_DIM), SSD_CONV ** -0.5),
        "conv_b": nrm((NL, SSD_CONV_DIM), 0.02),
        "dt_bias": dt_bias,
        "a_log": a_log,
        "d_skip": gain((NL, SSD_HEADS)),
        "ssd_norm_g": gain((NL, SSD_D)),
        "fox_f_b": 3.0 + nrm((NL, FOX_HEADS), 0.5),
        "mla_q_norm_g": gain((NL, MLA_Q_LORA)),
        "mla_w_uq": nrm((NL, MLA_Q_LORA, MLA_HEADS * (MLA_NOPE + MLA_ROPE)), MLA_Q_LORA ** -0.5),
        "mla_kv_norm_g": gain((NL, MLA_KV_LORA)),
        "mla_w_ukv": nrm((NL, MLA_KV_LORA, MLA_HEADS * (MLA_NOPE + MLA_V)), MLA_KV_LORA ** -0.5),
        "w_out": nrm((NL, D_MIX, Dm), D_MIX ** -0.5 * BETA),
        "ln2_g": gain((NL, Dm)),
        "ln2_b": nrm((NL, Dm), 0.02),
        "ffn2_w_gate": nrm((NL, Dm, F), Dm ** -0.5),
        "ffn2_w_up": nrm((NL, Dm, F), Dm ** -0.5),
        "ffn2_w_down": nrm((NL, F, Dm), F ** -0.5 * BETA),
        "ln3_g": gain((NL, Dm)),
        "ln3_b": nrm((NL, Dm), 0.02),
    }

def second_block(x, meta, ffn1_w_gate, ffn1_w_up, ffn1_w_down, ln1_g, ln1_b, w_in,
              conv_w, conv_b, dt_bias, a_log, d_skip, ssd_norm_g, fox_f_b,
              mla_q_norm_g, mla_w_uq, mla_kv_norm_g, mla_w_ukv, w_out, ln2_g, ln2_b,
              ffn2_w_gate, ffn2_w_up, ffn2_w_down, ln3_g, ln3_b):
    b = x.shape[0]
    h = jnp.concatenate([jnp.broadcast_to(meta[None].astype(x.dtype), (b, N_META, D_MODEL)), x], axis=1)
    total = h.shape[1]
    pos = jnp.arange(total, dtype=jnp.float32)
    inv_freq = 1.0 / (ROPE_THETA ** (jnp.arange(0, MLA_ROPE, 2, dtype=jnp.float32) / MLA_ROPE))
    ang = pos[:, None] * inv_freq[None, :]
    cos, sin = jnp.cos(ang), jnp.sin(ang)

    for l in range(DEPTH):
        h = layer_norm(ALPHA * h + 0.5 * swiglu(h, ffn1_w_gate[l], ffn1_w_up[l], ffn1_w_down[l]),
                       ln1_g[l], ln1_b[l])
        proj = h @ w_in[l]
        (z, xbc, dt_raw, fq, fk, fv, f_raw, cq, ckv, k_rope) = jnp.split(proj, IN_SPLITS, axis=-1)
        y_ssd = ssd_mixer(z, xbc, dt_raw, conv_w[l], conv_b[l], dt_bias[l], a_log[l],
                          d_skip[l], ssd_norm_g[l])
        y_fox = fox_mixer(fq, fk, fv, f_raw, fox_f_b[l])
        y_mla = mla_mixer(cq, ckv, k_rope, mla_q_norm_g[l], mla_w_uq[l], mla_kv_norm_g[l],
                          mla_w_ukv[l], cos, sin)
        mix = jnp.concatenate([y_ssd, y_fox.astype(h.dtype), y_mla.astype(h.dtype)], axis=-1) @ w_out[l]
        h = layer_norm(ALPHA * h + mix, ln2_g[l], ln2_b[l])
        h = layer_norm(ALPHA * h + 0.5 * swiglu(h, ffn2_w_gate[l], ffn2_w_up[l], ffn2_w_down[l]),
                       ln3_g[l], ln3_b[l])
    return h[:, N_META:]


def setup_inputs(seed=0):
    out = dict(first_inputs(seed))
    for name, value in second_inputs(seed + 1).items():
        if name != "x":
            out[name + "_2"] = value
    return out


def reference(
    x, c, ada_w, ada_b, ln_g, ln_b, ffn_w_in, ffn_w_out, rwkv_mu, rwkv_w_rkv, rwkv_w0, rwkv_w1,
    rwkv_w2, rwkv_a0, rwkv_a1, rwkv_a2, rwkv_g1, rwkv_g2, rwkv_k_k, rwkv_k_a, rwkv_r_k,
    rwkv_gn_g, rwkv_gn_b, rwkv_w_out, gdn_w_in, gdn_conv, gdn_a_log, gdn_dt_bias, gdn_norm_g,
    gdn_w_out, diff_w_in, diff_lambda, diff_subln_g, diff_w_out, swa_w_qkv, swa_b_qkv,
    swa_sinks, swa_w_out, swa_b_out, meta_2, ffn1_w_gate_2, ffn1_w_up_2, ffn1_w_down_2, ln1_g_2,
    ln1_b_2, w_in_2, conv_w_2, conv_b_2, dt_bias_2, a_log_2, d_skip_2, ssd_norm_g_2, fox_f_b_2,
    mla_q_norm_g_2, mla_w_uq_2, mla_kv_norm_g_2, mla_w_ukv_2, w_out_2, ln2_g_2, ln2_b_2,
    ffn2_w_gate_2, ffn2_w_up_2, ffn2_w_down_2, ln3_g_2, ln3_b_2,
):
    x = first_block(
        x, c, ada_w, ada_b, ln_g, ln_b, ffn_w_in, ffn_w_out, rwkv_mu, rwkv_w_rkv, rwkv_w0,
        rwkv_w1, rwkv_w2, rwkv_a0, rwkv_a1, rwkv_a2, rwkv_g1, rwkv_g2, rwkv_k_k, rwkv_k_a,
        rwkv_r_k, rwkv_gn_g, rwkv_gn_b, rwkv_w_out, gdn_w_in, gdn_conv, gdn_a_log, gdn_dt_bias,
        gdn_norm_g, gdn_w_out, diff_w_in, diff_lambda, diff_subln_g, diff_w_out, swa_w_qkv,
        swa_b_qkv, swa_sinks, swa_w_out, swa_b_out,
    )
    return second_block(
        x, meta_2, ffn1_w_gate_2, ffn1_w_up_2, ffn1_w_down_2, ln1_g_2, ln1_b_2, w_in_2,
        conv_w_2, conv_b_2, dt_bias_2, a_log_2, d_skip_2, ssd_norm_g_2, fox_f_b_2,
        mla_q_norm_g_2, mla_w_uq_2, mla_kv_norm_g_2, mla_w_ukv_2, w_out_2, ln2_g_2, ln2_b_2,
        ffn2_w_gate_2, ffn2_w_up_2, ffn2_w_down_2, ln3_g_2, ln3_b_2,
    )


_drawn_inputs = setup_inputs


def setup_inputs(seed=0):
    import zlib

    import numpy as np

    out = dict(_drawn_inputs(seed))
    spreads = {}
    factors = {'rwkv_w1': 8.0,
     'rwkv_w2': 8.0,
     'rwkv_a0': 5.752,
     'rwkv_k_k': 4.178,
     'rwkv_gn_g': 8.0,
     'rwkv_gn_b': 8.0,
     'gdn_norm_g': 8.0,
     'conv_b_2': 6.205,
     'd_skip_2': 8.0,
     'ssd_norm_g_2': 7.804,
     'fox_f_b_2': 27.984,
     'mla_q_norm_g_2': 8.0,
     'mla_kv_norm_g_2': 8.0}
    for name, (base, spread) in spreads.items():
        noise = np.random.default_rng([zlib.crc32(name.encode()), seed]).standard_normal(out[name].shape)
        drawn = base * np.exp(spread * noise) if base else spread * noise
        out[name] = jnp.asarray(drawn.astype(out[name].dtype))
    for name, factor in factors.items():
        out[name] = (out[name] * factor).astype(out[name].dtype)
    return out
```

```python
from contextlib import ExitStack

import numpy as np

import concourse.bass as bass
from concourse import mybir

ALU = mybir.AluOpType
ACT = mybir.ActivationFunctionType
F32 = mybir.dt.float32
AX_X = mybir.AxisListType.X

P = 128
D = 1024
DT = D // P
SEQ = 256
META = 16
TALL = META + SEQ
DEPTH = 2
ALPHA = (2.0 * DEPTH) ** 0.25
FF = 2816
FT = FF // P
BLOCKS = 16
RING = 8
SLOTS = 10
EPS_LN = 1e-5
NEG = -1e30
DECAY_SCALE = float(np.exp(-0.5))
BANKS = 8


def _dense(name, layer, n_tiles, k_tiles):
    return [(name, layer, n, k) for n in range(n_tiles) for k in range(k_tiles)]


def manifest():
    m = []
    for i in range(DEPTH):
        m += _dense("ada", i, 48, 8)
    m += _dense("rwkv_k", 0, 8, 8)
    m += _dense("w1a1", 0, 1, 8)
    m += _dense("w2a2", 0, 8, 1)
    m += _dense("rwkv_r", 0, 8, 8)
    m += _dense("rwkv_v", 0, 8, 8)
    m += _dense("g1", 0, 1, 8)
    m += _dense("g2", 0, 8, 1)
    m += _dense("rwkv_out", 0, 8, 8)
    for n in range(FT):
        m += [("ffn_in", 0, n, k) for k in range(8)] + [("ffn_in", 0, FT + n, k) for k in range(8)]
    m += _dense("ffn_out", 0, 8, FT)
    m += [("gdn_ba", 0, 0, 0)]
    m += _dense("gdn_in", 0, 32, 8)
    m += _dense("gdn_out", 0, 8, 8)
    for n in range(FT):
        m += [("ffn_in", 1, n, k) for k in range(8)] + [("ffn_in", 1, FT + n, k) for k in range(8)]
    m += _dense("ffn_out", 1, 8, FT)
    for i in range(DEPTH):
        for f in (1, 2):
            for n in range(FT):
                m += [(f"gate{f}", i, n, k) for k in range(8)] + [(f"up{f}", i, n, k) for k in range(8)]
            m += _dense(f"down{f}", i, 8, FT)
            if f == 1:
                m += [("dtf", i, 0, 0)]
                m += _dense("mix_in", i, 19, 8)
                m += _dense("kr", i, 2, 8)
                m += _dense("uq", i, 4, 2)
                m += _dense("ukv", i, 4, 1)
                m += _dense("mix_out", i, 8, 8)
    return m


def param_columns():
    cols, at = {}, 0

    def add(name, n):
        nonlocal at
        cols[name] = at
        at += n

    for i in range(DEPTH):
        add(f"ada_b{i}", 48)
        for s in range(2):
            add(f"ln_g{i}{s}", 8)
            add(f"ln_b{i}{s}", 8)
    add("mu", 48)
    for n in ("w0", "a0", "k_k", "k_a", "r_k", "gn_g", "gn_b"):
        add(n, 8)
    add("gdn_conv", 4 * 24)
    add("gdn_norm", 1)
    add("gdn_alog", 1)
    add("gdn_dtb", 1)
    for i in range(DEPTH):
        for s in (1, 2, 3):
            add(f"ln{s}_g{i}", 8)
            add(f"ln{s}_b{i}", 8)
        add(f"conv_w{i}", 4 * 6)
        add(f"conv_b{i}", 6)
        add(f"dtb{i}", 1)
        add(f"alog{i}", 1)
        add(f"dskip{i}", 4)
        add(f"ssd_g{i}", 4)
        add(f"mlaq{i}", 2)
        add(f"mlakv{i}", 1)
    cols["_n"] = at
    return cols


def constants():
    parts, cols, at = [], {}, 0

    def add(name, a):
        nonlocal at
        a = np.asarray(a, np.float32)
        full = np.zeros((P, a.shape[1]), np.float32)
        full[: a.shape[0]] = a
        cols[name] = at
        at += a.shape[1]
        parts.append(full)

    i = np.arange(P)
    r, c = i[:, None], i[None, :]
    add("ident", r == c)
    add("ones", np.ones((P, P)))
    chunk = r // 64 == c // 64
    add("strict64", (r < c) & chunk)
    add("incl64", (r <= c) & chunk)
    add("nstrict", -1.0 * (r < c))
    add("later_neg", NEG * (r > c))
    add("key_neg", NEG * (c > r))
    lv = [(r // 2 ** (l + 1) == c // 2 ** (l + 1)) & (r // 2**l % 2 == 1) & (c // 2**l % 2 == 0) for l in range(7)]
    add("level0T", lv[0].T)
    for l in range(1, 7):
        add(f"level{l}", lv[l])
    add("hsel", np.concatenate([(np.arange(16)[None, :] == 2 * j + r // 64) for j in range(8)], 1))
    add("hselT", np.concatenate([(np.arange(16)[:, None] == 2 * j + c // 64) for j in range(8)], 1))
    add("sel12", np.concatenate([np.repeat(np.arange(12)[:, None] == h, P, 1) for h in range(12)], 1))
    add("mean", np.full((P, P), 1.0 / D))
    add("sign12", np.where(np.arange(12) < 8, 1.0, -1.0)[:, None])
    add("hsel8", np.concatenate([np.repeat(np.arange(8)[None, :] == j, P, 0) for j in range(8)], 1))
    add("reset64", np.broadcast_to((np.arange(SEQ) % 64 != 0)[None, :], (P, SEQ)))
    add("half", np.stack([i < 64, i >= 64], 1))
    add("half_fox", 64.0**-0.5 * np.stack([i < 64, i >= 64], 1))
    add("half_mla", 96.0**-0.5 * np.stack([i < 64, i >= 64], 1))
    add("quarter_mla", 96.0**-0.5 * np.stack([i // 32 == q for q in range(4)], 1))
    freq = (10000.0 ** (-np.arange(0, 32, 2, dtype=np.float32) / 32)).astype(np.float32)
    ang = (freq[i % 16][:, None] * np.arange(TALL, dtype=np.float32)[None, :]).astype(np.float32)
    add("cos", np.cos(ang))
    add("sin", np.sin(ang) * np.where(i % 32 < 16, -1.0, 1.0)[:, None])
    cols["_n"] = at
    return cols, np.concatenate(parts, 1)


class Counts:

    def __init__(self):
        self.sent, self.taken, self.last = {}, {}, None

    def sig(self, sem):
        self.sent[sem] = self.sent.get(sem, 0) + 1
        self.last = (sem, self.sent[sem])
        return sem

    def nth(self, sem, n=1):
        self.taken[sem] = self.taken.get(sem, 0) + n
        return self.taken[sem]


def first_and_second_block(nc, stream, params, consts, xin, cin, meta, out):
    M = manifest()
    PC = param_columns()
    CC, _ = constants()
    nv, na, ng = nc.vector, nc.scalar, nc.gpsimd

    with ExitStack() as ctx:
        def sb(name, shape):
            return ctx.enter_context(nc.sbuf_tensor(name, shape, F32))

        def sem(name):
            return ctx.enter_context(nc.semaphore(name))

        ring = sb("ring", [P, RING, BLOCKS, P])
        arena = sb("arena", [P, SLOTS, DT, TALL])
        par = sb("par", [P, PC["_n"]])
        con = sb("con", [P, CC["_n"]])
        cond = sb("cond", [P, DT])
        mods = sb("mods", [P, DEPTH, 48])
        mod1 = sb("mod1", [P, DEPTH, 48])
        lnc = sb("lnc", [P, 10, 4, DT])
        small = sb("small", [P, 3, TALL])
        silu_t = sb("silu_t", [P, 2, TALL])
        XX = sb("XX", [P, 4, 2, P])
        ZZ = sb("ZZ", [P, 4, P])
        TOK = sb("TOK", [P, 2, 3, P])
        AZ = sb("AZ", [P, 2, 2, P])
        PP = sb("PP", [P, 4, P])
        cols = sb("cols", [P, 64])
        TC = sb("TC", [P, 3, 24])[:, :, :]
        prob_even = sb("prob_even", [P, 3, TALL])[:, :, :]
        WL = sb("WL", [P, DT, 4])[:, :, :]
        bank = [ctx.enter_context(nc.psum_tensor(f"bank{b}", [P, 512], F32)) for b in range(BANKS)]

        slab_loaded = [sem(f"slab_loaded{s}") for s in range(RING)]
        slab_used = sem("slab_used")
        inputs_loaded = sem("inputs_loaded")
        stored = sem("stored")
        output_ready = sem("output_ready")
        vstep, astep = sem("vector_step"), sem("scalar_step")
        full = {r: [sem(f"bank{b}_full_for_{r}") for b in range(BANKS)] for r in ("vector", "scalar")}
        full_for_vector, full_for_scalar = full["vector"], full["scalar"]
        free = {r: [sem(f"bank{b}_free_by_{r}") for b in range(BANKS)] for r in ("vector", "scalar")}
        cond_ready = sem("cond_ready")
        gate_full, silu_ready = sem("gate_full"), sem("silu_ready")
        up_full, hidden_ready = sem("up_full"), sem("hidden_ready")
        resid_ready = sem("resid_ready")
        centered, squared = sem("centered"), sem("squared")
        var_ready, std_ready = sem("var_ready"), sem("std_ready")
        normed, input_ready = sem("normed"), sem("input_ready")
        lerp_ready, lerp_used = sem("lerp_ready"), sem("lerp_used")
        v2p, a2p = sem("vector_result_for_tensor"), sem("scalar_result_for_tensor")
        v2a, a2v = sem("vector_result_for_scalar"), sem("scalar_result_for_vector")
        p2v = sem("tensor_done_for_vector")

        XAS, US = 0, 1

        def slot(i):
            return arena[:, i]

        def tl(i, j, T=SEQ, t0=0):
            return arena[:, i, j, t0:t0 + T]

        def pc(name, j=0, rows=P):
            return par[0:rows, PC[name] + j:PC[name] + j + 1]

        def cm(name, w=P, off=0, rows=P, r0=0):
            return con[r0:rows, CC[name] + off:CC[name] + off + w]

        ident = cm("ident")

        def hidden(f, T):
            return tl(2 + f // DT, f % DT, T)

        PK = (0, TALL, TALL + TALL - P)
        flat = lambda s, a, b: arena[:, s].rearrange("p j t -> p (j t)")[:, a:b]
        EX = flat(8, 0, 512).rearrange("p (n f) -> p n f", n=2)
        KB = flat(8, 512, 1024).rearrange("p (n f) -> p n f", n=2)
        DC = flat(8, 1024, 1536).rearrange("p (n f) -> p n f", n=4)
        DS = flat(8, 1536, 2048).rearrange("p (n f) -> p n f", n=4)
        XD = flat(6, 0, 1536).rearrange("p (n f) -> p n f", n=3)
        FV = flat(5, 4 * TALL, 4 * TALL + 768).rearrange("p (n f) -> p n f", n=3)
        MV = flat(3, 4 * TALL, 4 * TALL + 768).rearrange("p (n f) -> p n f", n=3)
        CB = flat(9, 0, 864).rearrange("p (g f) -> p g f", g=2)
        PKT = XX[:, :, :, :].rearrange("p a b f -> p (a b f)")[:, 0:864].rearrange("p (n f) -> p n f", n=2)

        def prob(h):
            return arena[:, 2, 4:7] if h % 2 else prob_even

        def decay_col(i, h, sn):
            return TC[0:sn, i, 12 + h:13 + h]

        GM = arena[:, 3].rearrange("p j t -> p (j t)")[:, 0:2048].rearrange("p (u f) -> p u f", u=4)

        def xview(T):
            return TALL - T

        norm_of = {"mixer": 0, "ffn": 1}


        block = ctx.enter_context(nc.Block())

        @block.sync
        def _(sp):
            slabs = -(-len(M) // BLOCKS)
            for dst, src in ((cond[:, :], cin), (par[:, :], params), (con[:, :], consts),
                             (arena[:, XAS, :, META:TALL], xin), (arena[:, US, :, 0:META], meta)):
                sp.dma_start(dst, src).then_inc(inputs_loaded, 16)
            for s in range(slabs):
                if s >= RING:
                    sp.wait_ge(slab_used, s - RING + 1)
                sp.dma_start(ring[:, s % RING], stream[s]).then_inc(slab_loaded[s % RING], 16)
            for half in range(2):
                js = slice(4 * half, 4 * half + 4)
                sp.wait_ge(output_ready, 4 * half + 4)
                sp.dma_start(out[:, js], arena[:, US, js, META:TALL]).then_inc(stored, 16)
            sp.wait_ge(stored, 32)

        @block.tensor
        def _(eng):
            pe = Counts()
            prev = [None] * BANKS
            at, owed = [0], []

            def freed(b):
                r = prev[b] or "vector"
                n = pe.nth(free[r][b], 1 if prev[b] else 0)
                prev[b] = None
                return free[r][b], n

            def mm(o, l, r, start=True, stop_=True, hold=False):
                ins = nc.tensor.matmul(o, l, r, start=start, stop=stop_, skip_group_check=True)
                if owed and not hold:
                    ins.then_inc(owed.pop(0), 1)
                return ins

            def transpose_to(o, x, rows=P, hold=False):
                ins = nc.tensor.transpose(o, x, con[0:rows, CC["ident"]:CC["ident"] + rows])
                if owed and not hold:
                    ins.then_inc(owed.pop(0), 1)
                return ins

            def closing(b, reader):
                prev[b] = reader
                return full[reader][b]

            def told(b, reader):
                return full[reader][b]

            def w(key):
                n = at[0]
                assert M[n] == key, (M[n], key)
                s = n // BLOCKS
                if n % BLOCKS == 0:
                    eng.wait_ge(slab_loaded[s % RING], 16 * (s // RING + 1))
                    if s:
                        owed.append(slab_used)
                at[0] += 1
                return ring[:, s % RING, n % BLOCKS, :]

            def project(name, layer, n_tiles, k_tiles, rhs, T, banks, reader, n0=0, ready=None, final=False, freed_by=None):
                for n in range(n_tiles):
                    b = banks[n % len(banks)]
                    eng.wait_ge(*freed(b))
                    for k in range(k_tiles):
                        if n == 0 and ready is not None:
                            eng.wait_ge(ready, pe.nth(ready))
                        m = mm(bank[b][:, 0:T], w((name, layer, n0 + n, k)), rhs(k), k == 0,
                               k == k_tiles - 1, hold=k == k_tiles - 1)
                        if k == k_tiles - 1:
                            m.then_inc(closing(b, reader), 1)
                    prev[b] = freed_by or reader
                if final:
                    prev[b] = None

            resid = {"base": 0, "got": 0}

            def residual(n):
                while resid["got"] < n:
                    eng.wait_ge(resid_ready, pe.nth(resid_ready))
                    resid["got"] += 1

            def out_projection(name, layer, k_tiles, rhs, T, n0=0):
                resid["got"] = 0
                for n in range(DT):
                    b = 6 + n % 2
                    eng.wait_ge(*freed(b))
                    residual(n - 1)
                    for k in range(k_tiles):
                        m = mm(bank[b][:, 0:T], w((name, layer, n, k)), rhs(k), k == 0, k == k_tiles - 1,
                               hold=k == k_tiles - 1)
                        if k == k_tiles - 1:
                            m.then_inc(full["vector"][b], 1)

            def norm(T):
                t0 = xview(T)
                eng.wait_ge(*freed(4))
                for j in range(DT):
                    residual(j + 1)
                    m = mm(bank[4][:, 0:T], cm("mean"), tl(XAS, j, T, t0), j == 0, j == DT - 1, hold=j == DT - 1)
                    if j == DT - 1:
                        m.then_inc(told(4, "vector"), 1)
                eng.wait_ge(*freed(5))
                for j in range(DT):
                    if j % 2 == 0:
                        eng.wait_ge(squared, pe.nth(squared))
                    m = mm(bank[5][:, 0:T], cm("mean"), tl(9, j, T), j == 0, j == DT - 1, hold=j == DT - 1)
                    if j == DT - 1:
                        m.then_inc(told(5, "vector"), 1)

            def ffn(name_g, name_u, name_d, layer, T, up0):
                t0 = xview(T)
                for b in range(4):
                    eng.wait_ge(*freed(b))
                for f in range(FT):
                    if f >= 2:
                        eng.wait_ge(hidden_ready, pe.nth(hidden_ready))
                    g, u = 2 * (f % 2), 2 * (f % 2) + 1
                    for k in range(DT):
                        if f == 0:
                            eng.wait_ge(input_ready, pe.nth(input_ready))
                        m = mm(bank[g][:, 0:T], w((name_g, layer, f, k)), tl(US, k, T, t0), k == 0, k == 7,
                               hold=k == 7)
                        if k == 7:
                            m.then_inc(gate_full, 1)
                    for k in range(DT):
                        m = mm(bank[u][:, 0:T], w((name_u, layer, up0 + f, k)), tl(US, k, T, t0), k == 0,
                               k == 7, hold=k == 7)
                        if k == 7:
                            m.then_inc(up_full, 1)
                eng.wait_ge(hidden_ready, pe.nth(hidden_ready, 2))
                out_projection(name_d, layer, FT, lambda k: hidden(k, T), T)

            def row_sums(src_slot, b, reader, sel, width, wait=None):
                eng.wait_ge(*freed(b))
                for j in range(DT):
                    m = mm(bank[b][0:width, 0:SEQ], cm(sel, width, width * j), tl(src_slot, j), j == 0,
                           j == 7, hold=j == 7)
                    if j == 7:
                        m.then_inc(told(b, reader), 1)

            def spread(rows, sel, nrows, banks, close=closing):
                for j in range(DT):
                    b = banks[j // 2]
                    if j % 2 == 0:
                        eng.wait_ge(*freed(b))
                    m = mm(bank[b][:, 256 * (j % 2):256 * (j % 2) + SEQ], cm(sel, P, P * j, nrows), rows,
                           True, True, hold=j % 2)
                    if j % 2:
                        m.then_inc(close(b, "vector"), 1)

            def inverse(levels):
                for b in range(4):
                    eng.wait_ge(*freed(b))
                for l in range(1, levels):
                    for p in range(2):
                        eng.wait_ge(v2p, pe.nth(v2p))
                        for u in (2 * p, 2 * p + 1):
                            m = mm(bank[p][:, P * (u % 2):P * (u % 2) + P], GM[:, u, 0:P], XX[:, u, 0], True,
                                   True, hold=u % 2)
                            if u % 2:
                                m.then_inc(told(p, "vector"), 1)
                    for p in range(2):
                        eng.wait_ge(v2p, pe.nth(v2p))
                        for u in (2 * p, 2 * p + 1):
                            o = 2 * P * (u % 2)
                            mm(bank[2 + p][:, o:o + P], XX[:, u, 1], ZZ[:, u], True, True)
                            m = mm(bank[2 + p][:, o + P:o + 2 * P], ZZ[:, u], XX[:, u, 1], True, True, hold=u % 2)
                            if u % 2:
                                m.then_inc(told(2 + p, "vector"), 1)

            eng.wait_ge(inputs_loaded, 80)
            eng.wait_ge(cond_ready, pe.nth(cond_ready))
            for i in range(DEPTH):
                for n in range(48):
                    for k in range(8):
                        m = mm(bank[i][:, n:n + 1], w(("ada", i, n, k)), cond[:, k:k + 1], k == 0, k == 7,
                               hold=n == 47 and k == 7)
                        if n == 47 and k == 7:
                            m.then_inc(closing(i, "vector"), 1)


            U = lambda k: tl(US, k, SEQ, META)
            L = [lambda k: tl(2, k), lambda k: tl(3, k)]
            B4 = [0, 1, 2, 3]
            project("rwkv_k", 0, 8, 8, L[0], SEQ, B4, "scalar", ready=lerp_ready)
            owed.append(lerp_used)
            eng.wait_ge(*freed(4))
            eng.wait_ge(*freed(5))
            for k in range(8):
                wk = w(("w1a1", 0, 0, k))
                eng.wait_ge(lerp_ready, pe.nth(lerp_ready))
                m = mm(bank[4][0:64, 0:SEQ], wk[:, 0:64], L[1](k), k == 0, k == 7, hold=k == 7)
                if k == 7:
                    m.then_inc(told(4, "scalar"), 1)
            owed.append(lerp_used)
            eng.wait_ge(lerp_ready, pe.nth(lerp_ready, 8))
            for k in range(8):
                wk = ring[:, ((at[0] - 8 + k) // BLOCKS) % RING, (at[0] - 8 + k) % BLOCKS, :]
                m = mm(bank[5][64:128, 0:SEQ], wk[:, 64:128], L[0](k), k == 0, k == 7, hold=k == 7)
                if k == 7:
                    m.then_inc(told(5, "scalar"), 1)
            owed.append(lerp_used)
            eng.wait_ge(a2p, pe.nth(a2p, 2))
            for n in range(8):
                wk = w(("w2a2", 0, n, 0))
                b = 2 * (n % 2)
                eng.wait_ge(*freed(b))
                mm(bank[b][:, 0:SEQ], wk[0:64, :], small[0:64, 0, 0:SEQ], True, True, hold=True).then_inc(closing(b, "scalar"), 1)
                eng.wait_ge(*freed(b + 1))
                mm(bank[b + 1][:, 0:SEQ], wk[64:128, :], small[64:128, 0, 0:SEQ], True, True, hold=True).then_inc(closing(b + 1, "scalar"), 1)
            project("rwkv_r", 0, 8, 8, L[1], SEQ, B4, "scalar", ready=lerp_ready)
            owed.append(lerp_used)
            project("rwkv_v", 0, 8, 8, L[0], SEQ, B4, "scalar", ready=lerp_ready)
            owed.append(lerp_used)
            project("g1", 0, 1, 8, L[1], SEQ, [4], "scalar", ready=lerp_ready, final=True)
            eng.wait_ge(a2p, pe.nth(a2p))
            project("g2", 0, 8, 1, lambda k: small[:, 1, 0:SEQ], SEQ, B4, "scalar", final=True)
            eng.wait_ge(a2p, pe.nth(a2p))
            row_sums(9, 4, "vector", "hsel", 16)
            eng.wait_ge(v2p, pe.nth(v2p))
            row_sums(3, 5, "scalar", "hsel", 16)
            eng.wait_ge(v2p, pe.nth(v2p))
            spread(small[0:16, 2, 0:SEQ], "hselT", 16, B4)

            for j in range(DT):
                if j == 0:
                    eng.wait_ge(v2p, pe.nth(v2p))
                for tau in range(2):
                    ts = slice(P * tau, P * tau + P)
                    b = 4 + tau
                    eng.wait_ge(*freed(b))
                    for n, s in enumerate((8, 4, 6, 5)):
                        m = transpose_to(bank[b][:, P * n:P * n + P], arena[:, s, j, ts], hold=n == 3)
                        if n == 3:
                            m.then_inc(told(b, "scalar"), 1)
                for u in range(4):
                    tau, e = u // 2, u % 2
                    ts = slice(P * tau, P * tau + P)
                    b = 6 + e
                    eng.wait_ge(*freed(b))
                    rows = slice(64 * e, 64 * e + 64)
                    ra = arena[rows, 5:8:2, j, ts]
                    mm(bank[b][:, 0:256], arena[rows, 6, j, ts], ra, True, True)
                    mm(bank[b][:, 256:512], arena[rows, 4, j, ts], ra, True, True, hold=True).then_inc(closing(b, "vector"), 1)
                for p in range(2):
                    eng.wait_ge(v2p, pe.nth(v2p))
                    eng.wait_ge(*freed(2 + p))
                    for u in (2 * p, 2 * p + 1):
                        m = transpose_to(bank[2 + p][:, P * (u % 2):P * (u % 2) + P], XX[:, u, 1], hold=u % 2)
                        if u % 2:
                            m.then_inc(told(2 + p, "vector"), 1)
                inverse(6)
                eng.wait_ge(a2p, pe.nth(a2p, 2))
                eng.wait_ge(v2p, pe.nth(v2p, 2))
                for tau in range(2):
                    b = 4 + tau
                    eng.wait_ge(*freed(b))
                    for e in range(2):
                        m = mm(bank[b][:, 64 * e:64 * e + 64], GM[:, 2 * tau + e, 256:384],
                               TOK[:, tau, 0, 64 * e:64 * e + 64], True, True, hold=e)
                        if e:
                            m.then_inc(told(b, "scalar"), 1)
                for tau in range(2):
                    eng.wait_ge(a2p, pe.nth(a2p))
                    b = 4 + tau
                    eng.wait_ge(*freed(b))
                    for e in range(2):
                        m = mm(bank[b][:, P * e:P * e + P], XX[:, 2 * tau + e, 1], AZ[:, tau, e], True, True, hold=e)
                        if e:
                            m.then_inc(told(b, "scalar"), 1)
                for tau in range(2):
                    eng.wait_ge(a2p, pe.nth(a2p))
                    b = tau
                    eng.wait_ge(*freed(b))
                    for e in range(2):
                        u, o = 2 * tau + e, slice(64 * e, 64 * e + 64)
                        mm(bank[b][o, 0:P], PP[:, u, 0:64], GM[:, u, P:2 * P], True, True)
                        mm(bank[b][o, P:2 * P], PP[:, u, 64:128], GM[:, u, P:2 * P], True, False)
                        m = mm(bank[b][o, P:2 * P], TOK[:, tau, 0, o], GM[:, u, 3 * P:4 * P], False, True, hold=e)
                        if e:
                            m.then_inc(closing(b, "vector"), 1)
                    for cc in range(2):
                        c = 2 * tau + cc
                        if c == 3:
                            continue
                        b = (2, 3, 6)[c]
                        eng.wait_ge(*freed(b))
                        rows = slice(64 * cc, 64 * cc + 64)
                        for e in range(2):
                            u, o = 2 * tau + e, slice(64 * e, 64 * e + 64)
                            mm(bank[b][o, 0:64], TOK[rows, tau, 2, o], PP[rows, u, 64:128], True, False)
                            m = mm(bank[b][o, 0:64], TOK[rows, tau, 1, o], TOK[rows, tau, 0, o], False, True,
                                   hold=e and c == 0)
                            if e and c == 0:
                                m.then_inc(closing(b, "vector"), 1)
                            if c:
                                m = mm(bank[b][o, 64:128], PP[rows, u, 0:64], TOK[rows, tau, 2, o], True,
                                       True, hold=e)
                                if e:
                                    m.then_inc(closing(b, "vector"), 1)
            for c in (1, 2):
                eng.wait_ge(v2p, pe.nth(v2p))
                eng.wait_ge(*freed(c))
                for j in range(DT):
                    m = mm(bank[c][:, 64 * j:64 * j + 64], arena[:, 9, j, P * (c - 1):P * c],
                           arena[:, 2, j, 192:256], True, True, hold=j == 7)
                    if j == 7:
                        m.then_inc(closing(c, "vector"), 1)
            eng.wait_ge(v2p, pe.nth(v2p))
            for j in range(DT):
                b = B4[j % 4]
                eng.wait_ge(*freed(b))
                if j >= 4:
                    eng.wait_ge(v2p, pe.nth(v2p))
                for c in (1, 2, 3):
                    m = mm(bank[b][:, 64 * c:64 * c + 64], arena[:, (3, 4, 6)[c - 1], j, 0:P],
                           tl(7, j)[:, 64 * c:64 * c + 64], True, True, hold=c == 3)
                    if c == 3:
                        m.then_inc(told(b, "vector"), 1)
            eng.wait_ge(v2p, pe.nth(v2p, 4))
            row_sums(5, 4, "scalar", "hsel", 16)
            eng.wait_ge(a2p, pe.nth(a2p))
            spread(small[0:16, 0, 0:SEQ], "hselT", 16, B4, told)
            eng.wait_ge(a2p, pe.nth(a2p))
            row_sums(3, 5, "vector", "hsel", 16)
            eng.wait_ge(v2p, pe.nth(v2p))
            spread(small[0:16, 2, 0:SEQ], "hselT", 16, B4)
            spread(small[0:16, 1, 0:SEQ], "hselT", 16, B4)
            eng.wait_ge(v2p, pe.nth(v2p))
            out_projection("rwkv_out", 0, 8, lambda k: tl(5, k), SEQ)
            norm(SEQ)
            ffn("ffn_in", "ffn_in", "ffn_out", 0, SEQ, FT)
            norm(SEQ)
            eng.wait_ge(*freed(4))
            eng.wait_ge(*freed(5))
            wk = w(("gdn_ba", 0, 0, 0))
            for k in range(8):
                eng.wait_ge(input_ready, pe.nth(input_ready))
                m = mm(bank[4][0:8, 0:SEQ], wk[:, 16 * k:16 * k + 8], U(k), k == 0, k == 7, hold=k == 7)
                if k == 7:
                    m.then_inc(told(4, "scalar"), 1)
            for k in range(8):
                m = mm(bank[5][0:8, 0:SEQ], wk[:, 16 * k + 8:16 * k + 16], U(k), k == 0, k == 7, hold=k == 7)
                if k == 7:
                    m.then_inc(told(5, "scalar"), 1)
            project("gdn_in", 0, 24, 8, U, SEQ, B4, "vector", freed_by="scalar")
            project("gdn_in", 0, 8, 8, U, SEQ, B4, "scalar", n0=24)
            eng.wait_ge(a2p, pe.nth(a2p))
            row_sums(8, 4, "vector", "hsel8", 8)
            row_sums(3, 5, "vector", "hsel8", 8)
            eng.wait_ge(v2p, pe.nth(v2p))
            spread(small[0:8, 2, 0:SEQ], "sel12", 8, B4)
            spread(small[0:8, 1, 0:SEQ], "sel12", 8, B4)
            eng.wait_ge(a2p, pe.nth(a2p))
            for n, (row, c) in enumerate(((0, 0), (0, 1), (4, 0), (4, 1), (5, 0))):
                m = transpose_to(bank[4][:, 8 * n:8 * n + 8], arena[0:8, 9, row, P * c:P * c + P], rows=8,
                                 hold=n == 4)
                if n == 4:
                    m.then_inc(told(4, "vector"), 1)
            eng.wait_ge(v2p, pe.nth(v2p))
            for hp in range(4):
                heads = (2 * hp, 2 * hp + 1)
                gc, beta = arena[0:8, 9, 4], arena[0:8, 9, 0]
                for b in (4, 5, 6, 7):
                    eng.wait_ge(*freed(b))
                for hh, h in enumerate(heads):
                    m = mm(bank[4][:, SEQ * hh:SEQ * hh + SEQ], cm("sel12", P, P * h, 8), gc[:, 0:SEQ], True,
                           True, hold=hh)
                    if hh:
                        m.then_inc(told(4, "scalar"), 1)
                for hh, h in enumerate(heads):
                    m = mm(bank[5][:, SEQ * hh:SEQ * hh + SEQ], cm("sel12", P, P * h, 8), beta[:, 0:SEQ],
                           True, True, hold=hh)
                    if hh:
                        m.then_inc(told(5, "vector"), 1)
                for u in range(4):
                    h, c = heads[u // 2], u % 2
                    o = slice(P * u, P * u + P)
                    mm(bank[6][:, o], cm("sel12", P, P * h, 8), gc[:, P * c:P * c + P], True, False)
                    m = mm(bank[6][:, o], ident, cm("later_neg"), False, True, hold=u == 3)
                    if u == 3:
                        m.then_inc(told(6, "scalar"), 1)
                eng.wait_ge(v2p, pe.nth(v2p))
                for hh, h in enumerate(heads):
                    b = (7, 5)[hh]
                    for c in range(2):
                        cs = slice(P * c, P * c + P)
                        mm(bank[b][:, 2 * P * c:2 * P * c + P], tl(4, h)[:, cs], KB[:, hh, cs], True, True)
                        m = mm(bank[b][:, 2 * P * c + P:2 * P * c + 2 * P], tl(4, h)[:, cs], tl(2, h)[:, cs],
                               True, True, hold=c)
                        if c:
                            m.then_inc(told(b, "vector"), 1)
                eng.wait_ge(a2p, pe.nth(a2p, 2))
                for hh, h in enumerate(heads):
                    b = (4, 6)[hh]
                    for n, (s, c) in enumerate(((5, 0), (5, 1), (4, 0))):
                        m = transpose_to(bank[b][:, P * n:P * n + P], tl(s, h)[:, P * c:P * c + P], hold=n == 2)
                        if n == 2:
                            m.then_inc(told(b, "scalar"), 1)
                for p in range(2):
                    eng.wait_ge(v2p, pe.nth(v2p))
                    eng.wait_ge(*freed(2 + p))
                    for u in (2 * p, 2 * p + 1):
                        m = transpose_to(bank[2 + p][:, P * (u % 2):P * (u % 2) + P], XX[:, u, 1], hold=u % 2)
                        if u % 2:
                            m.then_inc(told(2 + p, "vector"), 1)
                inverse(7)
                eng.wait_ge(v2p, pe.nth(v2p, 2))
                eng.wait_ge(a2p, pe.nth(a2p))
                both = lambda b: [bank[b][:, 0:P], bank[b][:, P:2 * P]]
                for hh in range(2):
                    m = mm(both(4)[hh], XX[:, 2 * hh, 1], TOK[:, hh, 0], True, True, hold=hh)
                    if hh:
                        m.then_inc(told(4, "scalar"), 1)
                eng.wait_ge(a2p, pe.nth(a2p))
                for hh in range(2):
                    m = mm(both(5)[hh], TOK[:, hh, 2], AZ[:, hh, 0], True, True, hold=hh)
                    if hh:
                        m.then_inc(told(5, "scalar"), 1)
                eng.wait_ge(a2p, pe.nth(a2p))
                for hh in range(2):
                    m = mm(both(6)[hh], PP[:, 2 + hh], ZZ[:, 2 * hh], True, True, hold=hh)
                    if hh:
                        m.then_inc(told(6, "vector"), 1)
                eng.wait_ge(v2p, pe.nth(v2p))
                for hh in range(2):
                    m = mm(both(7)[hh], XX[:, 2 * hh + 1, 1], AZ[:, hh, 1], True, True, hold=hh)
                    if hh:
                        m.then_inc(told(7, "scalar"), 1)
                eng.wait_ge(a2p, pe.nth(a2p))
                for hh in range(2):
                    o0, o1 = slice(SEQ * hh, SEQ * hh + P), slice(SEQ * hh + P, SEQ * hh + SEQ)
                    mm(bank[4][:, o0], AZ[:, hh, 0], GM[:, 2 * hh, P:2 * P], True, True)
                    mm(bank[4][:, o1], ZZ[:, 2 * hh], PP[:, hh], True, False)
                    m = mm(bank[4][:, o1], ZZ[:, 2 * hh + 1], GM[:, 2 * hh + 1, P:2 * P], False, True, hold=hh)
                    if hh:
                        m.then_inc(closing(4, "scalar"), 1)
            eng.wait_ge(a2p, pe.nth(a2p))
            row_sums(8, 5, "vector", "hsel8", 8)
            eng.wait_ge(v2p, pe.nth(v2p))
            spread(small[0:8, 2, 0:SEQ], "sel12", 8, B4)
            eng.wait_ge(v2p, pe.nth(v2p))
            out_projection("gdn_out", 0, 8, lambda k: tl(7, k), SEQ)
            norm(SEQ)
            ffn("ffn_in", "ffn_in", "ffn_out", 1, SEQ, FT)
            norm(SEQ)

            T = TALL
            UA = lambda k: tl(US, k, T)
            QT = ((0, 128), (128, 128), (256, 16))

            def by_packed(o, lhs, rhs, hold):
                for i, (s0, sn) in enumerate(QT):
                    m = mm(o[:, s0:T], lhs(i, sn), rhs[0:sn, PK[i]:PK[i] + T - s0], i == 0, i == 2, hold=hold and i == 2)
                return m

            def mixer(l):
                eng.wait_ge(*freed(4))
                wk = w(("dtf", l, 0, 0))
                for k in range(8):
                    eng.wait_ge(input_ready, pe.nth(input_ready))
                    m = mm(bank[4][0:12, 0:T], wk[:, 12 * k:12 * k + 12], UA(k), k == 0, k == 7, hold=k == 7)
                    if k == 7:
                        m.then_inc(told(4, "scalar"), 1)
                project("mix_in", l, 6, 8, UA, T, B4, "vector", freed_by="scalar")
                project("mix_in", l, 13, 8, UA, T, B4, "scalar", n0=6)
                project("kr", l, 2, 8, UA, T, [6, 7], "vector")
                eng.wait_ge(a2p, pe.nth(a2p))
                eng.wait_ge(*freed(4))
                eng.wait_ge(*freed(5))
                for k in range(2):
                    m = mm(bank[4][:, 0:T], cm("ones"), tl(6, k, T), k == 0, k == 1, hold=k)
                    if k:
                        m.then_inc(told(4, "vector"), 1)
                mm(bank[5][:, 0:T], cm("ones"), tl(6, 2, T), True, True, hold=True).then_inc(told(5, "vector"), 1)
                eng.wait_ge(v2p, pe.nth(v2p))
                eng.wait_ge(*freed(6))
                for i, (s0, sn) in enumerate(QT):
                    for n, row in enumerate((4, 5)):
                        o = 24 * i + 12 * n
                        m = transpose_to(bank[6][0:sn, o:o + 12], arena[0:12, 9, row, s0:s0 + sn], rows=12,
                                         hold=i == 2 and n)
                        if i == 2 and n:
                            m.then_inc(told(6, "vector"), 1)
                eng.wait_ge(v2p, pe.nth(v2p))
                project("uq", l, 2, 2, lambda k: tl(4, 4 + k, T), T, [0, 1], "scalar")
                project("uq", l, 2, 2, lambda k: tl(4, 4 + k, T), T, [2, 3], "vector", n0=2)
                project("ukv", l, 4, 1, lambda k: tl(4, 6, T), T, [0, 1, 4, 5], "scalar", final=True)
                eng.wait_ge(a2p, pe.nth(a2p))
                eng.wait_ge(v2p, pe.nth(v2p))
                for i, (s0, sn) in enumerate(QT):
                    b = (2, 3, 6)[i]
                    eng.wait_ge(*freed(b))
                    for j in range(4):
                        m = transpose_to(bank[b][0:sn, P * j:P * j + P], tl(2, j, T)[:, s0:s0 + sn], hold=j == 3)
                        if j == 3:
                            m.then_inc(closing(b, "vector"), 1)
                for i, (s0, sn) in enumerate(QT):
                    b = (7, 0, 1)[i]
                    eng.wait_ge(*freed(b))
                    for n, (s, j) in enumerate(((4, 2), (4, 3), (5, 2), (5, 3))):
                        m = transpose_to(bank[b][0:sn, P * n:P * n + P], tl(s, j, T)[:, s0:s0 + sn], hold=n == 3)
                        if n == 3:
                            m.then_inc(closing(b, "scalar"), 1)
                for g in range(2):
                    for i, (s0, sn) in enumerate(QT):
                        b, o = ((4, 0), (5, 0), (5, 144))[i]
                        if i < 2:
                            eng.wait_ge(*freed(b))
                        m = mm(bank[b][0:sn, o:o + T - s0], tl(8, 4 + g, T)[:, s0:s0 + sn],
                               tl(2, 5, T)[:, s0:T], True, True, hold=i != 1)
                        if i != 1:
                            m.then_inc(closing(b, "vector"), 1)
                def decays(h):
                    cum = arena[0:12, 9, 5]
                    for i, (s0, sn) in enumerate(QT):
                        b, o = ((2 * (h % 2), 0), (2 * (h % 2) + 1, 0), (2 * (h % 2) + 1, 144))[i]
                        if i < 2:
                            eng.wait_ge(*freed(b))
                        mm(bank[b][0:sn, o:o + T - s0], cm("sel12", sn, P * h, 12), cum[:, s0:T], True, False)
                        m = mm(bank[b][0:sn, o:o + sn], con[0:sn, CC["ident"]:CC["ident"] + sn],
                               con[0:sn, CC["later_neg"]:CC["later_neg"] + sn], False, True, hold=i != 1)
                        if i != 1:
                            m.then_inc(told(b, "scalar"), 1)

                eng.wait_ge(*freed(0))
                eng.wait_ge(*freed(1))
                eng.wait_ge(*freed(2))
                eng.wait_ge(*freed(3))
                decays(0)
                for h in range(8):
                    if h < 7:
                        decays(h + 1)
                    eng.wait_ge(v2p, pe.nth(v2p))
                    b = 6 + h // 2 % 2
                    if h % 2 == 0:
                        eng.wait_ge(*freed(b))
                    e = h % 2
                    m = by_packed(bank[b][64 * e:64 * e + 64], lambda i, sn: XD[0:sn, i, 64 * h:64 * h + 64],
                                  PKT[:, h % 2], hold=e)
                    if e:
                        m.then_inc(closing(b, "vector"), 1)
                eng.wait_ge(a2p, pe.nth(a2p))
                eng.wait_ge(*freed(4))
                eng.wait_ge(*freed(5))
                for g in range(2):
                    for k in range(2):
                        m = mm(bank[4 + g][:, 0:T], cm("ones"), tl(2, 2 * g + k, T), k == 0, k == 1, hold=k)
                        if k:
                            m.then_inc(told(4 + g, "vector"), 1)

                def logits(h):
                    for i, (q0, qn) in enumerate(QT):
                        kn = q0 + qn
                        b, o = ((2 * (h % 2), 0), (2 * (h % 2), P), (2 * (h % 2) + 1, 0))[i]
                        dst = bank[b][0:qn, o:o + kn]
                        mm(dst, tl(7, h, T)[:, q0:kn], tl(4 if h < 4 else 5, h % 4 // 2, T)[:, 0:kn], True, False)
                        if h < 4:
                            mm(dst, cm("sel12", qn, P * (8 + h), 12), arena[0:12, 9, 6, 0:kn], False, False)
                        else:
                            mm(dst, tl(8, h - 4, T)[:, q0:kn], tl(4, 7, T)[:, 0:kn], False, False)
                        m = mm(bank[b][0:qn, o + q0:o + kn], con[0:qn, CC["ident"]:CC["ident"] + qn],
                               con[0:qn, CC["key_neg"]:CC["key_neg"] + qn], False, True, hold=i)
                        if i:
                            m.then_inc(told(b, "vector"), 1)

                for b in range(4):
                    eng.wait_ge(*freed(b))
                logits(0)
                for h in range(8):
                    if h < 7:
                        logits(h + 1)
                    eng.wait_ge(v2p, pe.nth(v2p))
                    for i, (q0, qn) in enumerate(QT):
                        for kb in range(i + 1):
                            k0, kn = QT[kb]
                            b, o = ((4, q0), (5, q0 - P), (5, 144))[kb]
                            m = transpose_to(bank[b][0:kn, o:o + qn], prob(h)[0:qn, i, k0:k0 + kn], rows=qn,
                                             hold=(i, kb) == (2, 2))
                            if (i, kb) == (2, 2):
                                m.then_inc(told(5, "scalar"), 1)
                    eng.wait_ge(a2p, pe.nth(a2p))
                    b = 6 + h // 2 % 2
                    if h % 2 == 0:
                        eng.wait_ge(*freed(b))
                    e = h % 2
                    vt = FV if h < 4 else MV
                    m = by_packed(bank[b][64 * e:64 * e + 64], lambda i, sn: vt[0:sn, i, 64 * (h % 4):64 * (h % 4) + 64],
                                  PKT[:, h % 2], hold=e)
                    if e:
                        m.then_inc(closing(b, "scalar"), 1)
                for b in (6, 7):
                    eng.wait_ge(*freed(b))
                eng.wait_ge(v2p, pe.nth(v2p))
                out_projection("mix_out", l, 8, UA, T)

            for l in range(DEPTH):
                ffn("gate1", "up1", "down1", l, T, 0)
                norm(T)
                mixer(l)
                norm(T)
                ffn("gate2", "up2", "down2", l, T, 0)
                norm(T)

        @block.scalar
        def _(eng):
            a = Counts()
            act = na.activation

            def norm(T, last=False):
                t0 = xview(T)
                for q in range(4):
                    eng.wait_ge(centered, a.nth(centered))
                    act(arena[:, 9, 2 * q:2 * q + 2, 0:T], arena[:, XAS, 2 * q:2 * q + 2, t0:t0 + T], ACT.Square).then_inc(a.sig(squared), 1)
                eng.wait_ge(var_ready, a.nth(var_ready))
                act(small[:, 1, 0:T], small[:, 0, 0:T], ACT.Sqrt).then_inc(a.sig(std_ready), 1)

            def norm_out(n, T, signal=input_ready):
                t0 = xview(T)
                for j in range(DT):
                    if j % 2 == 0:
                        eng.wait_ge(normed, a.nth(normed))
                    act(tl(US, j, T, t0), tl(9, j, T), ACT.Identity, bias=lnc[:, n, 1, j:j + 1],
                             scale=lnc[:, n, 0, j:j + 1]).then_inc(a.sig(signal), 1)

            def ffn(T):
                for f in range(FT):
                    eng.wait_ge(gate_full, a.nth(gate_full))
                    act(silu_t[:, f % 2, 0:T], bank[2 * (f % 2)][:, 0:T], ACT.Silu).then_inc(a.sig(silu_ready), 1)

            def copies(n_tiles, banks, dst, func=ACT.Copy, T=SEQ, last=None, **kw):
                for n in range(n_tiles):
                    b = banks[n % len(banks)]
                    eng.wait_ge(full_for_scalar[b], a.nth(full_for_scalar[b]))
                    act(dst(n), bank[b][:, 0:T], func, **{k: v(n) for k, v in kw.items()}).then_inc(a.sig(last if last and n == n_tiles - 1 else free["scalar"][b]), 1)

            eng.wait_ge(inputs_loaded, 80)
            act(cond[:, :], cond[:, :], ACT.Silu).then_inc(a.sig(cond_ready), 1)
            B4 = [0, 1, 2, 3]
            copies(8, B4, lambda n: tl(4, n))
            eng.wait_ge(full_for_scalar[4], a.nth(full_for_scalar[4]))
            act(small[0:64, 0, 0:SEQ], bank[4][0:64, 0:SEQ], ACT.Tanh).then_inc(a.sig(a2p), 1)
            eng.wait_ge(full_for_scalar[5], a.nth(full_for_scalar[5]))
            act(small[64:128, 0, 0:SEQ], bank[5][64:128, 0:SEQ], ACT.Copy).then_inc(a.sig(a2p), 1)
            for n in range(8):
                for half, dst in ((0, 5), (1, 6)):
                    b = 2 * (n % 2) + half
                    eng.wait_ge(full_for_scalar[b], a.nth(full_for_scalar[b]))
                    act(tl(dst, n), bank[b][:, 0:SEQ], ACT.Sigmoid, bias=pc("a0" if half else "w0", n)).then_inc(a.sig(free["scalar"][b]), 1)
            copies(8, B4, lambda n: tl(7, n))
            copies(8, B4, lambda n: tl(8, n))
            eng.wait_ge(full_for_scalar[4], a.nth(full_for_scalar[4]))
            act(small[:, 1, 0:SEQ], bank[4][:, 0:SEQ], ACT.Sigmoid).then_inc(a.sig(a2p), 1)
            copies(8, B4, lambda n: tl(US, n, SEQ, META), last=a2v)
            eng.wait_ge(v2a, a.nth(v2a))
            act(slot(9)[:, :, 0:SEQ], slot(2)[:, :, 0:SEQ], ACT.Square).then_inc(a.sig(a2p), 1)
            eng.wait_ge(v2a, a.nth(v2a))
            act(small[0:16, 2, 0:SEQ], small[0:16, 2, 0:SEQ], ACT.Sqrt).then_inc(a.sig(a2v), 1)
            eng.wait_ge(full_for_scalar[5], a.nth(full_for_scalar[5]))
            act(small[0:16, 1, 0:SEQ], bank[5][0:16, 0:SEQ], ACT.Copy).then_inc(a.sig(free["scalar"][5]), 1)
            eng.wait_ge(v2a, a.nth(v2a))
            act(slot(3)[:, :, 0:SEQ], slot(9)[:, :, 0:SEQ], ACT.Exp, scale=-DECAY_SCALE).then_inc(a.sig(a2v), 1)
            eng.wait_ge(v2a, a.nth(v2a))
            act(slot(5)[:, :, 0:SEQ], slot(5)[:, :, 0:SEQ], ACT.Exp, scale=-DECAY_SCALE).then_inc(a.sig(a2v), 1)
            act(slot(9)[:, :, 0:SEQ], slot(9)[:, :, 0:SEQ], ACT.Exp, scale=DECAY_SCALE).then_inc(a.sig(a2v), 1)
            for j in range(DT):
                if j:
                    pass
                for tau in range(2):
                    b = 4 + tau
                    eng.wait_ge(full_for_scalar[b], a.nth(full_for_scalar[b]))
                    act(TOK[:, tau], bank[b][:, 0:384].rearrange("p (n f) -> p n f", n=3), ACT.Copy).then_inc(a.sig(astep), 1)
                    act(AZ[:, tau, :, 0:64], bank[b][:, 384:512].rearrange("p (n f) -> p n f", n=2), ACT.Copy).then_inc(a.sig(a2p), 1)
                for tau in range(2):
                    b = 4 + tau
                    eng.wait_ge(full_for_scalar[b], a.nth(full_for_scalar[b]))
                    act(AZ[:, tau, :, 64:128], bank[b][:, 0:P].rearrange("p (n f) -> p n f", n=2), ACT.Copy).then_inc(a.sig(a2p), 1)
                for tau in range(2):
                    b = 4 + tau
                    eng.wait_ge(full_for_scalar[b], a.nth(full_for_scalar[b]))
                    act(PP[:, 2 * tau:2 * tau + 2], bank[b][:, 0:256].rearrange("p (n f) -> p n f", n=2), ACT.Copy).then_inc(a.sig(a2p), 1)
            eng.wait_ge(full_for_scalar[4], a.nth(full_for_scalar[4]))
            act(small[0:16, 0, 0:SEQ], bank[4][0:16, 0:SEQ], ACT.Copy, scale=1.0 / 64).then_inc(a.sig(a2p), 1)
            eng.wait_ge(v2a, a.nth(v2a, 4))
            act(slot(3)[:, :, 0:SEQ], slot(5)[:, :, 0:SEQ], ACT.Square).then_inc(a.sig(a2p), 1)
            eng.wait_ge(v2a, a.nth(v2a))
            act(small[0:16, 2, 0:SEQ], small[0:16, 2, 0:SEQ], ACT.Sqrt).then_inc(a.sig(a2v), 1)
            norm(SEQ), norm_out(0, SEQ)
            ffn(SEQ)
            norm(SEQ), norm_out(1, SEQ)
            rows8 = lambda n, T=SEQ, r=8: arena[0:r, 9, n, 0:T]
            eng.wait_ge(full_for_scalar[4], a.nth(full_for_scalar[4]))
            eng.wait_ge(v2a, a.nth(v2a))
            act(rows8(0), bank[4][0:8, 0:SEQ], ACT.Sigmoid).then_inc(a.sig(astep), 1)
            eng.wait_ge(full_for_scalar[5], a.nth(full_for_scalar[5]))
            act(rows8(1), bank[5][0:8, 0:SEQ], ACT.Identity, bias=pc("gdn_dtb", rows=8)).then_inc(a.sig(astep), 1)
            eng.wait_ge(*a.last)

            def soft(r, T, alog):
                act(rows8(2, T, r), rows8(1, T, r), ACT.Abs).then_inc(a.sig(astep), 1)
                eng.wait_ge(*a.last)
                act(cols[0:r, 48:49], pc(alog, rows=r), ACT.Exp).then_inc(a.sig(astep), 1)
                act(rows8(2, T, r), rows8(2, T, r), ACT.Exp, scale=-1.0).then_inc(a.sig(a2v), 1)

            soft(8, SEQ, "gdn_alog")
            for n in range(24):
                b = n % 4
                eng.wait_ge(v2a, a.nth(v2a))
                act(tl((2, 4, 5)[n // 8], n % 8), XX[:, b].rearrange("p a f -> p (a f)"), ACT.Silu).then_inc(a.sig(free["scalar"][b]), 1)
            eng.wait_ge(*a.last)
            act(slot(8)[:, :, 0:SEQ], slot(2)[:, :, 0:SEQ], ACT.Square).then_inc(a.sig(astep), 1)
            act(slot(3)[:, :, 0:SEQ], slot(4)[:, :, 0:SEQ], ACT.Square).then_inc(a.sig(a2p), 1)
            copies(8, B4, lambda n: tl(6, n), ACT.Silu)
            eng.wait_ge(v2a, a.nth(v2a))
            act(small[0:8, 2, 0:SEQ], small[0:8, 2, 0:SEQ], ACT.Sqrt).then_inc(a.sig(astep), 1)
            act(small[0:8, 1, 0:SEQ], small[0:8, 1, 0:SEQ], ACT.Sqrt).then_inc(a.sig(a2v), 1)
            act(rows8(5, P), rows8(4, P), ACT.Exp, scale=-1.0, bias=rows8(4)[:, P - 1:P]).then_inc(a.sig(a2p), 1)
            for hp in range(4):
                eng.wait_ge(full_for_scalar[4], a.nth(full_for_scalar[4]))
                act(EX[:, :, :], bank[4][:, :].rearrange("p (n f) -> p n f", n=2), ACT.Exp).then_inc(a.sig(a2p), 1)
                eng.wait_ge(full_for_scalar[6], a.nth(full_for_scalar[6]))
                for u in range(4):
                    c, h = u % 2, 2 * hp + u // 2
                    act(DC[:, u], bank[6][:, P * u:P * u + P], ACT.Exp, bias=cols[:, 16 + 8 * c + h:17 + 8 * c + h]).then_inc(a.sig(a2p if u == 3 else astep), 1)
                for hh in range(2):
                    h = 2 * hp + hh
                    b = (4, 6)[hh]
                    eng.wait_ge(full_for_scalar[b], a.nth(full_for_scalar[b]))
                    for n, col in enumerate((h, 8 + h, 32 + h)):
                        act(TOK[:, hh, n], bank[b][:, P * n:P * n + P], ACT.Copy, scale=cols[:, col:col + 1]).then_inc(a.sig(a2p if hh and n == 2 else a2v if not hh and n == 0 else astep), 1)
                both = lambda b: bank[b][:, 0:2 * P].rearrange("p (n f) -> p n f", n=2)
                eng.wait_ge(full_for_scalar[4], a.nth(full_for_scalar[4]))
                act(AZ[:, :, 0], both(4), ACT.Copy).then_inc(a.sig(a2p), 1)
                eng.wait_ge(full_for_scalar[5], a.nth(full_for_scalar[5]))
                act(ZZ[:, 0:4:2], both(5), ACT.Copy).then_inc(a.sig(a2p), 1)
                eng.wait_ge(full_for_scalar[7], a.nth(full_for_scalar[7]))
                act(ZZ[:, 1:4:2], both(7), ACT.Copy).then_inc(a.sig(a2p), 1)
                eng.wait_ge(full_for_scalar[4], a.nth(full_for_scalar[4]))
                act(arena[:, 7, 2 * hp:2 * hp + 2, 0:SEQ], bank[4][:, :].rearrange("p (n f) -> p n f", n=2), ACT.Copy).then_inc(a.sig(free["scalar"][4]), 1)
            eng.wait_ge(*a.last)
            act(slot(8)[:, :, 0:SEQ], slot(7)[:, :, 0:SEQ], ACT.Square).then_inc(a.sig(a2p), 1)
            eng.wait_ge(v2a, a.nth(v2a))
            act(small[0:8, 2, 0:SEQ], small[0:8, 2, 0:SEQ], ACT.Sqrt).then_inc(a.sig(a2v), 1)
            norm(SEQ), norm_out(2, SEQ)
            ffn(SEQ)
            norm(SEQ), norm_out(3, SEQ)

            T = TALL
            QT = ((0, 128), (128, 128), (256, 16))

            def mixer(l):
                eng.wait_ge(full_for_scalar[4], a.nth(full_for_scalar[4]))
                eng.wait_ge(v2a, a.nth(v2a))
                act(rows8(1, T, 12), bank[4][0:12, 0:T], ACT.Identity, bias=cols[0:12, 50:51], scale=cm("sign12", 1, 0, 12)).then_inc(a.sig(astep), 1)
                eng.wait_ge(*a.last)
                soft(12, T, f"alog{l}")
                for n in range(6):
                    b = n % 4
                    eng.wait_ge(v2a, a.nth(v2a))
                    act(tl(2, n, T), tl(3, 4 + b, T), ACT.Silu, bias=pc(f"conv_b{l}", n)).then_inc(a.sig(free["scalar"][b]), 1)
                for n in range(13):
                    b = n % 4
                    eng.wait_ge(full_for_scalar[b], a.nth(full_for_scalar[b]))
                    src = bank[b][:, 0:T]
                    if n < 4:
                        act(tl(3, n, T), src, ACT.Silu).then_inc(a.sig(free["scalar"][b]), 1)
                    elif n < 6:
                        for e in range(2):
                            act(tl(7, 2 * (n - 4) + e, T), src, ACT.Copy, scale=cm("half_fox", 1, e)).then_inc(a.sig(free["scalar"][b] if e else astep), 1)
                    elif n < 10:
                        act(tl(4, n - 6, T), src, ACT.Copy).then_inc(a.sig(free["scalar"][b]), 1)
                    else:
                        act(tl(4, n - 6, T), src, ACT.Copy).then_inc(a.sig(free["scalar"][b]), 1)
                eng.wait_ge(*a.last)
                act(arena[:, 6, 0:3, 0:T], arena[:, 4, 4:7, 0:T], ACT.Square).then_inc(a.sig(a2p), 1)
                eng.wait_ge(v2a, a.nth(v2a))
                act(small[:, 0:2, 0:T], small[:, 0:2, 0:T], ACT.Sqrt).then_inc(a.sig(a2v), 1)
                for n in range(2):
                    eng.wait_ge(full_for_scalar[n], a.nth(full_for_scalar[n]))
                    for e in range(2):
                        act(tl(7, 4 + 2 * n + e, T), bank[n][:, 0:T], ACT.Copy, scale=cm("half_mla", 1, e)).then_inc(a.sig(free["scalar"][n] if e else astep), 1)
                for n in range(4):
                    b = (0, 1, 4, 5)[n]
                    eng.wait_ge(full_for_scalar[b], a.nth(full_for_scalar[b]))
                    act(tl(5, n, T), bank[b][:, 0:T], ACT.Copy).then_inc(a.sig(free["scalar"][b] if n < 3 else a2p), 1)
                for i, (s0, sn) in enumerate(QT):
                    b = (7, 0, 1)[i]
                    eng.wait_ge(full_for_scalar[b], a.nth(full_for_scalar[b]))
                    act(FV[0:sn, i], bank[b][0:sn, 0:256], ACT.Copy).then_inc(a.sig(astep), 1)
                    act(MV[0:sn, i], bank[b][0:sn, 256:512], ACT.Copy).then_inc(a.sig(free["scalar"][b]), 1)
                for h in range(8):
                    for i, (s0, sn) in enumerate(QT):
                        b, o = ((2 * (h % 2), 0), (2 * (h % 2) + 1, 0), (2 * (h % 2) + 1, 144))[i]
                        if i < 2:
                            eng.wait_ge(full_for_scalar[b], a.nth(full_for_scalar[b]))
                        act(PKT[0:sn, h % 2, PK[i]:PK[i] + T - s0], bank[b][0:sn, o:o + T - s0], ACT.Exp,
                                 bias=cols[0:sn, 24 * i + 12 + h - 0:24 * i + 13 + h] if 0 else decay_col(i, h, sn)).then_inc(a.sig(a2v if i == 2 else astep), 1)
                eng.wait_ge(v2a, a.nth(v2a))
                act(arena[:, 2, 0:4, 0:T], arena[:, US, 0:4, 0:T], ACT.Square).then_inc(a.sig(a2p), 1)
                eng.wait_ge(v2a, a.nth(v2a))
                act(small[:, 0:2, 0:T], small[:, 0:2, 0:T], ACT.Sqrt).then_inc(a.sig(a2v), 1)
                def turned(h):
                    eng.wait_ge(full_for_scalar[5], a.nth(full_for_scalar[5]))
                    for i, (s0, sn) in enumerate(QT):
                        b, o = ((4, 0), (5, 0), (5, 144))[i]
                        act(PKT[0:sn, h % 2, PK[i]:PK[i] + T - s0], bank[b][0:sn, o:o + T - s0], ACT.Copy).then_inc(a.sig(a2p if i == 2 else astep), 1)
                    if h % 2:
                        b = 6 + h // 2 % 2
                        eng.wait_ge(full_for_scalar[b], a.nth(full_for_scalar[b]))
                        act(tl(US, 4 + h // 2, T), bank[b][:, 0:T], ACT.Copy).then_inc(a.sig(free["scalar"][b]), 1)

                for h in range(8):
                    for i, (q0, qn) in enumerate(QT):
                        b, o = ((2 * (h % 2), 0), (2 * (h % 2), P), (2 * (h % 2) + 1, 0))[i]
                        eng.wait_ge(v2a, a.nth(v2a))
                        act(prob(h)[0:qn, i, 0:q0 + qn], bank[b][0:qn, o:o + q0 + qn], ACT.Exp,
                                 bias=cols[0:qn, 52 + i:53 + i], accum_out=cols[0:qn, 56 + i:57 + i]).then_inc(a.sig(a2v), 1)
                    if h:
                        turned(h - 1)
                turned(7)

            for l in range(DEPTH):
                ffn(T)
                norm(T), norm_out(4 + 3 * l, T)
                mixer(l)
                norm(T), norm_out(5 + 3 * l, T)
                ffn(T)
                norm(T)
                norm_out(6 + 3 * l, T, output_ready if l == DEPTH - 1 else input_ready)

        @block.vector
        def _(eng):
            v = Counts()

            def residual(T, coef=None, scale=1.0):
                t0 = xview(T)
                for j in range(DT):
                    b = 6 + j % 2
                    eng.wait_ge(full_for_vector[b], v.nth(full_for_vector[b]))
                    nv.scalar_tensor_tensor(out=tl(XAS, j, T, t0), in0=bank[b][:, 0:T],
                                                 scalar=coef(j) if coef else scale, in1=tl(XAS, j, T, t0),
                                                 op0=ALU.mult, op1=ALU.add).then_inc(v.sig(resid_ready), 1)

            def over_tiles(ap, n, T):
                return ap.unsqueeze(1).to_broadcast([P, n, T])

            def norm(n, T, done=None):
                t0 = xview(T)
                eng.wait_ge(*v.last)
                eng.wait_ge(full_for_vector[4], v.nth(full_for_vector[4]))
                for q in range(4):
                    x = arena[:, XAS, 2 * q:2 * q + 2, t0:t0 + T]
                    nv.tensor_tensor(x, x, over_tiles(bank[4][:, 0:T], 2, T), ALU.subtract).then_inc(v.sig(centered), 1)
                eng.wait_ge(full_for_vector[5], v.nth(full_for_vector[5]))
                nv.tensor_scalar(small[:, 0, 0:T], bank[5][:, 0:T], 1.0, EPS_LN, ALU.mult, ALU.add).then_inc(v.sig(var_ready), 1)
                eng.wait_ge(std_ready, v.nth(std_ready))
                nv.reciprocal(small[:, 2, 0:T], small[:, 1, 0:T]).then_inc(v.sig(vstep), 1)
                eng.wait_ge(*v.last)
                for q in range(4):
                    nv.tensor_tensor(arena[:, 9, 2 * q:2 * q + 2, 0:T], arena[:, XAS, 2 * q:2 * q + 2, t0:t0 + T],
                                          over_tiles(small[:, 2, 0:T], 2, T), ALU.mult).then_inc(v.sig(normed), 1)
                eng.wait_ge(*v.last)
                for j in range(DT):
                    nv.tensor_scalar(tl(XAS, j, T, t0), tl(9, j, T), lnc[:, n, 2, j:j + 1], lnc[:, n, 3, j:j + 1],
                                          ALU.mult, ALU.add).then_inc(v.sig((done or vstep) if j == DT - 1 else vstep), 1)

            def ffn(T):
                for f in range(FT):
                    eng.wait_ge(silu_ready, v.nth(silu_ready))
                    eng.wait_ge(up_full, v.nth(up_full))
                    nv.tensor_tensor(hidden(f, T), silu_t[:, f % 2, 0:T], bank[2 * (f % 2) + 1][:, 0:T], ALU.mult).then_inc(v.sig(hidden_ready), 1)

            def inverse(levels):
                for l in range(1, levels):
                    for p in range(2):
                        eng.wait_ge(full_for_vector[p], v.nth(full_for_vector[p]))
                        nv.tensor_tensor(ZZ[:, 2 * p:2 * p + 2], bank[p][:, 0:256].rearrange("p (n f) -> p n f", n=2),
                                              over_tiles(cm(f"level{l}"), 2, P), ALU.mult).then_inc(v.sig(v2p), 1)
                    for p in range(2):
                        eng.wait_ge(full_for_vector[2 + p], v.nth(full_for_vector[2 + p]))
                        x = XX[:, 2 * p:2 * p + 2].rearrange("p a b f -> p (a b f)")
                        nv.tensor_tensor(x, x, bank[2 + p][:, 0:512], ALU.add).then_inc(v.sig(v2p), 1)

            eng.wait_ge(inputs_loaded, 80)
            for i in range(DEPTH):
                eng.wait_ge(full_for_vector[i], v.nth(full_for_vector[i]))
                nv.tensor_tensor(mods[:, i], bank[i][:, 0:48], par[:, PC[f"ada_b{i}"]:PC[f"ada_b{i}"] + 48], ALU.add).then_inc(v.sig(free["vector"][i]), 1)
                eng.wait_ge(*v.last)
                nv.tensor_scalar(mod1[:, i], mods[:, i], 1.0, None, ALU.add).then_inc(v.sig(vstep), 1)
            eng.wait_ge(*v.last)
            for n in range(10):
                if n < 4:
                    i, s = n // 2, n % 2
                    g = par[:, PC[f"ln_g{i}{s}"]:PC[f"ln_g{i}{s}"] + 8]
                    b = par[:, PC[f"ln_b{i}{s}"]:PC[f"ln_b{i}{s}"] + 8]
                    nxt = (0, 3) if n == 0 else (1, 0) if n == 1 else (1, 3) if n == 2 else None
                else:
                    i, s = (n - 4) // 3, (n - 4) % 3 + 1
                    g = par[:, PC[f"ln{s}_g{i}"]:PC[f"ln{s}_g{i}"] + 8]
                    b = par[:, PC[f"ln{s}_b{i}"]:PC[f"ln{s}_b{i}"] + 8]
                    nxt = None
                nv.tensor_scalar(lnc[:, n, 2], g, ALPHA, None, ALU.mult).then_inc(v.sig(vstep), 1)
                nv.tensor_scalar(lnc[:, n, 3], b, ALPHA, None, ALU.mult).then_inc(v.sig(vstep), 1)
                if nxt:
                    l, q = nxt
                    sh, sc = slice(8 * q, 8 * q + 8), slice(8 * q + 8, 8 * q + 16)
                    nv.tensor_tensor(lnc[:, n, 0], g, mod1[:, l, sc], ALU.mult).then_inc(v.sig(vstep), 1)
                    nv.tensor_tensor(lnc[:, n, 1], b, mod1[:, l, sc], ALU.mult).then_inc(v.sig(vstep), 1)
                    eng.wait_ge(*v.last)
                    nv.tensor_tensor(lnc[:, n, 1], lnc[:, n, 1], mods[:, l, sh], ALU.add).then_inc(v.sig(vstep), 1)
                else:
                    nv.tensor_copy(lnc[:, n, 0], g).then_inc(v.sig(vstep), 1)
                    nv.tensor_copy(lnc[:, n, 1], b).then_inc(v.sig(vstep), 1)
            for j in range(DT):
                nv.tensor_scalar(tl(US, j, SEQ, META), tl(XAS, j, SEQ, META), mod1[:, 0, 8 + j:9 + j],
                                      mods[:, 0, j:j + 1], ALU.mult, ALU.add).then_inc(v.sig(vstep), 1)
            x = arena[:, XAS, :, META:TALL]
            eng.wait_ge(*v.last)
            nv.tensor_scalar(x, x, ALPHA, None, ALU.mult).then_inc(v.sig(vstep), 1)
            nv.tensor_scalar(arena[:, XAS, :, 0:META], arena[:, US, :, 0:META], ALPHA, None, ALU.mult).then_inc(v.sig(vstep), 1)

            u = arena[:, US, :, META:TALL]
            nv.tensor_tensor(slot(9)[:, :, 1:SEQ], u[:, :, 0:SEQ - 1], u[:, :, 1:SEQ], ALU.subtract).then_inc(v.sig(vstep), 1)
            nv.tensor_scalar(slot(9)[:, :, 0:1], u[:, :, 0:1], -1.0, None, ALU.mult).then_inc(v.sig(vstep), 1)
            eng.wait_ge(*v.last)

            def lerp(i, s):
                for j in range(DT):
                    nv.scalar_tensor_tensor(out=tl(s, j), in0=tl(9, j), scalar=pc("mu", 8 * i + j),
                                                 in1=tl(US, j, SEQ, META), op0=ALU.mult, op1=ALU.add).then_inc(v.sig(lerp_ready), 1)

            lerp(1, 2)
            lerp(3, 3)
            eng.wait_ge(lerp_used, v.nth(lerp_used))
            lerp(4, 2)
            eng.wait_ge(lerp_used, v.nth(lerp_used))
            lerp(0, 3)
            eng.wait_ge(lerp_used, v.nth(lerp_used))
            lerp(2, 2)
            eng.wait_ge(lerp_used, v.nth(lerp_used))
            lerp(5, 3)
            nv.tensor_scalar(cols[:, 8:16], par[:, PC["k_a"]:PC["k_a"] + 8], -1.0, 1.0, ALU.mult, ALU.add).then_inc(v.sig(vstep), 1)
            eng.wait_ge(*v.last)
            eng.wait_ge(a2v, v.nth(a2v))
            S = lambda i: slot(i)[:, :, 0:SEQ]
            for j in range(DT):
                nv.tensor_scalar(tl(2, j), tl(4, j), pc("k_k", j), None, ALU.mult).then_inc(v.sig(v2a if j == 7 else vstep), 1)
            for j in range(DT):
                nv.tensor_scalar(tl(3, j), tl(6, j), pc("k_a", j), cols[:, 8 + j:9 + j], ALU.mult, ALU.add).then_inc(v.sig(vstep), 1)
            eng.wait_ge(*v.last)
            nv.tensor_tensor(S(4), S(4), S(3), ALU.mult).then_inc(v.sig(vstep), 1)
            eng.wait_ge(*v.last)
            for j in range(DT):
                nv.scalar_tensor_tensor(out=tl(3, j), in0=tl(7, j), scalar=pc("r_k", j), in1=tl(4, j),
                                             op0=ALU.mult, op1=ALU.mult).then_inc(v.sig(v2p if j == 7 else vstep), 1)
            eng.wait_ge(full_for_vector[4], v.nth(full_for_vector[4]))
            nv.tensor_scalar(small[0:16, 2, 0:SEQ], bank[4][0:16, 0:SEQ], 1.0, 1e-6, ALU.mult, ALU.add).then_inc(v.sig(v2a), 1)
            eng.wait_ge(a2v, v.nth(a2v))
            nv.reciprocal(small[0:16, 2, 0:SEQ], small[0:16, 2, 0:SEQ]).then_inc(v.sig(v2p), 1)

            def two(s, q, T=SEQ):
                return arena[:, s, 2 * q:2 * q + 2, 0:T]

            def pair(b, w_=512):
                return bank[b][:, 0:w_].rearrange("p (n f) -> p n f", n=2)

            for j in range(DT):
                nv.tensor_tensor_scan(tl(9, j), cm("reset64", SEQ), tl(5, j), 0.0, ALU.mult, ALU.add).then_inc(v.sig(v2a if j == 7 else vstep), 1)
            for q in range(4):
                eng.wait_ge(full_for_vector[q], v.nth(full_for_vector[q]))
                nv.tensor_tensor(two(2, q), two(2, q), pair(q), ALU.mult).then_inc(v.sig(free["vector"][q]), 1)
            eng.wait_ge(*v.last)
            nv.tensor_tensor(S(5), S(9), S(5), ALU.subtract).then_inc(v.sig(v2a), 1)
            eng.wait_ge(a2v, v.nth(a2v))
            nv.tensor_tensor(S(7), S(7), S(3), ALU.mult).then_inc(v.sig(vstep), 1)
            nv.tensor_copy(WL, slot(3)[:, :, 63:SEQ:64]).then_inc(v.sig(vstep), 1)
            eng.wait_ge(a2v, v.nth(a2v))
            nv.scalar_tensor_tensor(out=S(5), in0=S(2), scalar=-1.0, in1=S(5), op0=ALU.mult, op1=ALU.mult).then_inc(v.sig(vstep), 1)
            nv.tensor_tensor(S(2), S(2), S(6), ALU.mult).then_inc(v.sig(vstep), 1)
            eng.wait_ge(*v.last)
            eng.wait_ge(a2v, v.nth(a2v))
            nv.tensor_tensor(S(6), S(2), S(9), ALU.mult).then_inc(v.sig(vstep), 1)
            nv.tensor_tensor(S(4), S(4), S(9), ALU.mult).then_inc(v.sig(v2p), 1)
            eng.wait_ge(*v.last)
            nv.memset(S(9), 0.0).then_inc(v.sig(vstep), 1)
            for j in range(DT):
                for u in range(4):
                    b = 6 + u % 2
                    eng.wait_ge(full_for_vector[b], v.nth(full_for_vector[b]))
                    nv.tensor_tensor(GM[:, u].rearrange("p (n f) -> p n f", n=2), pair(b),
                                          over_tiles(cm("strict64", 256), 2, 256), ALU.mult).then_inc(v.sig(free["vector"][b]), 1)
                eng.wait_ge(*v.last)
                nv.tensor_tensor(XX[:, :, 1], GM[:, :, 0:P], over_tiles(cm("level0T"), 4, P), ALU.mult).then_inc(v.sig(vstep), 1)
                eng.wait_ge(*v.last)
                for p in range(2):
                    x = XX[:, 2 * p:2 * p + 2, 1]
                    nv.tensor_tensor(x, x, over_tiles(ident, 2, P), ALU.add).then_inc(v.sig(v2p), 1)
                for p in range(2):
                    eng.wait_ge(full_for_vector[2 + p], v.nth(full_for_vector[2 + p]))
                    nv.tensor_copy(XX[:, 2 * p:2 * p + 2, 0], pair(2 + p, 256)).then_inc(v.sig(v2p), 1)
                inverse(6)
                for tau in range(2):
                    eng.wait_ge(full_for_vector[tau], v.nth(full_for_vector[tau]))
                    nv.tensor_tensor(tl(7, j)[:, P * tau:P * tau + P], tl(7, j)[:, P * tau:P * tau + P],
                                          bank[tau][:, 0:P], ALU.add).then_inc(v.sig(vstep), 1)
                    nv.tensor_copy(tl(5, j)[:, P * tau:P * tau + P], bank[tau][:, P:2 * P]).then_inc(v.sig(free["vector"][tau]), 1)
                    for cc in range(2):
                        c = 2 * tau + cc
                        if c == 3:
                            continue
                        b = (2, 3, 6)[c]
                        eng.wait_ge(full_for_vector[b], v.nth(full_for_vector[b]))
                        if c:
                            for e in range(2):
                                o = slice(64 * e, 64 * e + 64)
                                nv.tensor_tensor(arena[o, 9, j, P * (c - 1) + 64 * e:P * (c - 1) + 64 * e + 64],
                                                      bank[b][o, 64:128], con[o, CC["ident"] + 64 * e:CC["ident"] + 64 * e + 64],
                                                      ALU.add).then_inc(v.sig(vstep), 1)
                        nv.tensor_copy(arena[:, 2, j, 64 * c:64 * c + 64], bank[b][:, 0:64]).then_inc(v.sig(free["vector"][b]), 1)
            eng.wait_ge(*v.last)
            for s in (3, 4, 6):
                nv.memset(arena[:, s, :, 0:P], 0.0).then_inc(v.sig(vstep), 1)
            H = lambda c: arena[:, 2, :, 64 * c:64 * c + 64]
            state = arena[:, 2, :, 192:256]
            wl = lambda c: WL[:, :, c:c + 1].to_broadcast([P, DT, 64])
            eng.wait_ge(*v.last)
            for c in range(3):
                if c == 0:
                    nv.tensor_tensor(state, H(0), wl(0), ALU.mult).then_inc(v.sig(v2p), 1)
                else:
                    eng.wait_ge(full_for_vector[c], v.nth(full_for_vector[c]))
                    nv.tensor_tensor(H(c), H(c), bank[c][:, :].rearrange("p (n f) -> p n f", n=DT), ALU.add).then_inc(v.sig(free["vector"][c]), 1)
                    eng.wait_ge(*v.last)
                    nv.tensor_tensor(state, H(c), wl(c), ALU.mult).then_inc(v.sig(v2p if c == 1 else vstep), 1)
                eng.wait_ge(*v.last)
                for e in range(2):
                    o = slice(64 * e, 64 * e + 64)
                    nv.tensor_copy(arena[o, (3, 4, 6)[c], :, 64 * e:64 * e + 64], arena[o, 2, :, 192:256]).then_inc(v.sig(v2p if c == 2 and e else vstep), 1)
            for j in range(DT):
                b = j % 4
                eng.wait_ge(full_for_vector[b], v.nth(full_for_vector[b]))
                nv.tensor_tensor(tl(5, j)[:, 64:256], tl(5, j)[:, 64:256], bank[b][:, 64:256], ALU.add).then_inc(v.sig(v2p), 1)
            eng.wait_ge(*v.last)
            for q in range(4):
                eng.wait_ge(full_for_vector[q], v.nth(full_for_vector[q]))
                nv.tensor_tensor(two(5, q), two(5, q), pair(q), ALU.subtract).then_inc(v.sig(v2a), 1)
            eng.wait_ge(full_for_vector[5], v.nth(full_for_vector[5]))
            nv.tensor_scalar(small[0:16, 2, 0:SEQ], bank[5][0:16, 0:SEQ], 1.0 / 64, 64e-5, ALU.mult, ALU.add).then_inc(v.sig(v2a), 1)
            eng.wait_ge(a2v, v.nth(a2v))
            nv.reciprocal(small[0:16, 2, 0:SEQ], small[0:16, 2, 0:SEQ]).then_inc(v.sig(v2p), 1)
            for q in range(4):
                eng.wait_ge(full_for_vector[q], v.nth(full_for_vector[q]))
                nv.tensor_tensor(two(5, q), two(5, q), pair(q), ALU.mult).then_inc(v.sig(free["vector"][q]), 1)
            eng.wait_ge(*v.last)
            for j in range(DT):
                nv.tensor_scalar(tl(5, j), tl(5, j), pc("gn_g", j), pc("gn_b", j), ALU.mult, ALU.add).then_inc(v.sig(vstep), 1)
            for q in range(4):
                eng.wait_ge(full_for_vector[q], v.nth(full_for_vector[q]))
                nv.tensor_tensor(two(3, q), two(8, q), pair(q), ALU.mult).then_inc(v.sig(free["vector"][q]), 1)
            eng.wait_ge(*v.last)
            nv.tensor_tensor(S(5), S(5), S(3), ALU.add).then_inc(v.sig(vstep), 1)
            eng.wait_ge(*v.last)
            nv.tensor_tensor(S(5), S(5), arena[:, US, :, META:TALL], ALU.mult).then_inc(v.sig(v2p), 1)
            residual(SEQ, lambda j: mod1[:, 0, 16 + j:17 + j])
            norm(0, SEQ)
            ffn(SEQ)
            residual(SEQ, lambda j: mod1[:, 0, 40 + j:41 + j])
            norm(1, SEQ, v2a)
            def softplus(r, T):
                R = lambda n: arena[0:r, 9, n, 0:T]
                eng.wait_ge(a2v, v.nth(a2v))
                nv.tensor_scalar(R(3), R(2), 2.0, None, ALU.add).then_inc(v.sig(vstep), 1)
                eng.wait_ge(*v.last)
                nv.reciprocal(R(3), R(3)).then_inc(v.sig(vstep), 1)
                eng.wait_ge(*v.last)
                nv.tensor_tensor(R(3), R(2), R(3), ALU.mult).then_inc(v.sig(vstep), 1)
                eng.wait_ge(*v.last)
                nv.tensor_tensor(R(6), R(3), R(3), ALU.mult).then_inc(v.sig(vstep), 1)
                eng.wait_ge(*v.last)
                nv.tensor_scalar(R(7), R(6), 1.0 / 15, None, ALU.mult).then_inc(v.sig(vstep), 1)
                for n in (13, 11, 9, 7, 5, 3, 1):
                    eng.wait_ge(*v.last)
                    nv.scalar_tensor_tensor(out=R(7), in0=R(7), scalar=1.0 / n, in1=R(6 if n > 1 else 3),
                                                 op0=ALU.add, op1=ALU.mult).then_inc(v.sig(vstep), 1)
                nv.tensor_scalar(R(2), R(1), 0.0, None, ALU.max).then_inc(v.sig(vstep), 1)
                eng.wait_ge(*v.last)
                nv.scalar_tensor_tensor(out=R(7), in0=R(7), scalar=2.0, in1=R(2), op0=ALU.mult, op1=ALU.add).then_inc(v.sig(vstep), 1)
                eng.wait_ge(*v.last)

            def convolve(n, b, dst, T, weights, stride):
                eng.wait_ge(full_for_vector[b], v.nth(full_for_vector[b]))
                tap = lambda t: pc(weights, stride * t + n)
                nv.tensor_scalar(dst, bank[b][:, 0:T], tap(3), None, ALU.mult).then_inc(v.sig(vstep), 1)
                for s in (1, 2, 3):
                    eng.wait_ge(*v.last)
                    nv.scalar_tensor_tensor(out=dst[:, s:T], in0=bank[b][:, 0:T - s], scalar=tap(3 - s),
                                                 in1=dst[:, s:T], op0=ALU.mult, op1=ALU.add).then_inc(v.sig(v2a if s == 3 else vstep), 1)

            def decay_rows():
                softplus(8, SEQ)
                R = lambda n: arena[0:8, 9, n, 0:SEQ]
                nv.tensor_scalar(R(6), R(7), cols[0:8, 48:49], -1.0, ALU.mult, ALU.mult).then_inc(v.sig(vstep), 1)
                eng.wait_ge(*v.last)
                for c in range(2):
                    cs = slice(P * c, P * c + P)
                    nv.tensor_tensor_scan(R(4)[:, cs], cm("ones", P, 0, 8), R(6)[:, cs], 0.0, ALU.mult, ALU.add).then_inc(v.sig(vstep), 1)

            for n in range(24):
                convolve(n, n % 4, XX[:, n % 4].rearrange("p a f -> p (a f)"), SEQ, "gdn_conv", 24)
                if n == 3:
                    decay_rows()
            eng.wait_ge(full_for_vector[4], v.nth(full_for_vector[4]))
            nv.tensor_scalar(small[0:8, 2, 0:SEQ], bank[4][0:8, 0:SEQ], 1.0, 1e-6, ALU.mult, ALU.add).then_inc(v.sig(vstep), 1)
            eng.wait_ge(full_for_vector[5], v.nth(full_for_vector[5]))
            nv.tensor_scalar(small[0:8, 1, 0:SEQ], bank[5][0:8, 0:SEQ], 1.0, 1e-6, ALU.mult, ALU.add).then_inc(v.sig(v2a), 1)
            eng.wait_ge(a2v, v.nth(a2v))
            nv.reciprocal(small[0:8, 2, 0:SEQ], small[0:8, 2, 0:SEQ]).then_inc(v.sig(vstep), 1)
            eng.wait_ge(*v.last)
            nv.tensor_scalar(small[0:8, 2, 0:SEQ], small[0:8, 2, 0:SEQ], P ** -0.5, None, ALU.mult).then_inc(v.sig(vstep), 1)
            nv.reciprocal(small[0:8, 1, 0:SEQ], small[0:8, 1, 0:SEQ]).then_inc(v.sig(v2p), 1)
            for s in (2, 4):
                for q in range(4):
                    eng.wait_ge(full_for_vector[q], v.nth(full_for_vector[q]))
                    nv.tensor_tensor(two(s, q), two(s, q), pair(q), ALU.mult).then_inc(v.sig(free["vector"][q]), 1)
            eng.wait_ge(full_for_vector[4], v.nth(full_for_vector[4]))
            nv.tensor_copy(cols[:, 0:16], bank[4][:, 0:16]).then_inc(v.sig(vstep), 1)
            nv.tensor_scalar(cols[:, 16:32], bank[4][:, 16:32], -1.0, None, ALU.mult).then_inc(v.sig(vstep), 1)
            nv.tensor_copy(cols[:, 32:40], bank[4][:, 32:40]).then_inc(v.sig(v2p), 1)
            for hp in range(4):
                eng.wait_ge(full_for_vector[5], v.nth(full_for_vector[5]))
                nv.tensor_tensor(KB, arena[:, 4, 2 * hp:2 * hp + 2, 0:SEQ], pair(5), ALU.mult).then_inc(v.sig(v2p), 1)
                eng.wait_ge(a2v, v.nth(a2v))
                nv.tensor_tensor(PP[:, 0:2], arena[:, 2, 2 * hp:2 * hp + 2, P:SEQ], EX[:, :, P:SEQ], ALU.mult).then_inc(v.sig(vstep), 1)
                eng.wait_ge(*v.last)
                nv.tensor_tensor(PP[:, 2:4], KB[:, :, P:SEQ], EX[:, :, P:SEQ], ALU.mult).then_inc(v.sig(vstep), 1)
                nv.tensor_tensor(DS, DC, over_tiles(cm("nstrict"), 4, P), ALU.mult).then_inc(v.sig(vstep), 1)
                eng.wait_ge(*v.last)
                for hh in range(2):
                    b = (7, 5)[hh]
                    eng.wait_ge(full_for_vector[b], v.nth(full_for_vector[b]))
                    g = bank[b][:, :].rearrange("p (n f) -> p n f", n=2)
                    us = slice(2 * hh, 2 * hh + 2)
                    nv.tensor_tensor(GM[:, us, 0:P], g[:, :, 0:P], DS[:, us], ALU.mult).then_inc(v.sig(vstep), 1)
                    nv.tensor_tensor(GM[:, us, P:2 * P], g[:, :, P:2 * P], DC[:, us], ALU.mult).then_inc(v.sig(vstep), 1)
                eng.wait_ge(*v.last)
                nv.tensor_tensor(XX[:, :, 1], GM[:, :, 0:P], over_tiles(cm("level0T"), 4, P), ALU.mult).then_inc(v.sig(vstep), 1)
                eng.wait_ge(*v.last)
                for p in range(2):
                    x = XX[:, 2 * p:2 * p + 2, 1]
                    nv.tensor_tensor(x, x, over_tiles(ident, 2, P), ALU.add).then_inc(v.sig(v2p), 1)
                for p in range(2):
                    eng.wait_ge(full_for_vector[2 + p], v.nth(full_for_vector[2 + p]))
                    nv.tensor_copy(XX[:, 2 * p:2 * p + 2, 0], pair(2 + p, 256)).then_inc(v.sig(v2p), 1)
                inverse(7)
                eng.wait_ge(full_for_vector[6], v.nth(full_for_vector[6]))
                nv.tensor_tensor(AZ[:, :, 1], TOK[:, :, 1], pair(6, 256), ALU.subtract).then_inc(v.sig(v2p), 1)
            eng.wait_ge(full_for_vector[5], v.nth(full_for_vector[5]))
            nv.tensor_scalar(small[0:8, 2, 0:SEQ], bank[5][0:8, 0:SEQ], 1.0 / P, 1e-6, ALU.mult, ALU.add).then_inc(v.sig(v2a), 1)
            eng.wait_ge(a2v, v.nth(a2v))
            nv.reciprocal(small[0:8, 2, 0:SEQ], small[0:8, 2, 0:SEQ]).then_inc(v.sig(v2p), 1)
            for q in range(4):
                eng.wait_ge(full_for_vector[q], v.nth(full_for_vector[q]))
                nv.tensor_tensor(two(7, q), two(7, q), pair(q), ALU.mult).then_inc(v.sig(free["vector"][q]), 1)
            eng.wait_ge(*v.last)
            nv.scalar_tensor_tensor(out=S(7), in0=S(7), scalar=pc("gdn_norm"), in1=S(6), op0=ALU.mult, op1=ALU.mult).then_inc(v.sig(v2p), 1)
            residual(SEQ, lambda j: mod1[:, 1, 16 + j:17 + j])
            norm(2, SEQ)
            ffn(SEQ)
            residual(SEQ, lambda j: mod1[:, 1, 40 + j:41 + j])
            norm(3, SEQ)

            T = TALL
            QT = ((0, 128), (128, 128), (256, 16))

            def mixer(l):
                eng.wait_ge(*v.last)
                nv.tensor_tensor(cols[0:12, 50:51], pc(f"dtb{l}", rows=12), cm("sign12", 1, 0, 12), ALU.mult).then_inc(v.sig(v2a), 1)
                R = lambda n: arena[0:12, 9, n, 0:T]
                for n in range(6):
                    convolve(n, n % 4, tl(3, 4 + n % 4, T), T, f"conv_w{l}", 6)
                    if n == 3:
                        softplus(12, T)
                        nv.tensor_copy(R(4), R(7)).then_inc(v.sig(vstep), 1)
                        nv.tensor_scalar(R(6), R(7), cols[0:12, 48:49], -1.0, ALU.mult, ALU.mult).then_inc(v.sig(vstep), 1)
                        eng.wait_ge(*v.last)
                        nv.tensor_tensor_scan(R(5), cm("ones", 1, 0, 12).to_broadcast([12, T]), R(6), 0.0,
                                                   ALU.mult, ALU.add).then_inc(v.sig(vstep), 1)
                        eng.wait_ge(*v.last)
                        nv.tensor_scalar(R(6), R(5), -1.0, None, ALU.mult).then_inc(v.sig(vstep), 1)
                eng.wait_ge(full_for_vector[6], v.nth(full_for_vector[6]))
                nv.tensor_tensor(tl(4, 7, T), bank[6][:, 0:T], cm("cos", T), ALU.mult).then_inc(v.sig(free["vector"][6]), 1)
                eng.wait_ge(full_for_vector[7], v.nth(full_for_vector[7]))
                nv.tensor_tensor(tl(8, 6, T), bank[7][:, 0:T], cm("sin", T), ALU.mult).then_inc(v.sig(free["vector"][7]), 1)
                eng.wait_ge(*v.last)
                nv.tensor_tensor(tl(4, 7, T), tl(4, 7, T), tl(8, 6, T), ALU.add).then_inc(v.sig(v2p), 1)
                eng.wait_ge(full_for_vector[4], v.nth(full_for_vector[4]))
                nv.tensor_scalar(small[:, 0, 0:T], bank[4][:, 0:T], 1.0 / 256, EPS_LN, ALU.mult, ALU.add).then_inc(v.sig(vstep), 1)
                eng.wait_ge(full_for_vector[5], v.nth(full_for_vector[5]))
                nv.tensor_scalar(small[:, 1, 0:T], bank[5][:, 0:T], 1.0 / 128, EPS_LN, ALU.mult, ALU.add).then_inc(v.sig(v2a), 1)
                eng.wait_ge(full_for_vector[6], v.nth(full_for_vector[6]))
                for i, (s0, sn) in enumerate(QT):
                    nv.tensor_copy(TC[0:sn, i, 0:12], bank[6][0:sn, 24 * i:24 * i + 12]).then_inc(v.sig(vstep), 1)
                    nv.tensor_scalar(TC[0:sn, i, 12:24], bank[6][0:sn, 24 * i + 12:24 * i + 24], -1.0, None, ALU.mult).then_inc(v.sig(vstep), 1)
                eng.wait_ge(a2v, v.nth(a2v))
                nv.reciprocal(small[:, 0:2, 0:T], small[:, 0:2, 0:T]).then_inc(v.sig(vstep), 1)
                eng.wait_ge(*v.last)
                for k in range(3):
                    nv.scalar_tensor_tensor(out=tl(4, 4 + k, T), in0=tl(4, 4 + k, T),
                                                 scalar=pc(f"mlaq{l}", k) if k < 2 else pc(f"mlakv{l}"),
                                                 in1=small[:, k // 2, 0:T], op0=ALU.mult, op1=ALU.mult).then_inc(v.sig(v2p if k == 2 else vstep), 1)
                eng.wait_ge(full_for_vector[2], v.nth(full_for_vector[2]))
                nv.tensor_tensor(tl(8, 6, T), bank[2][:, 0:T], cm("cos", T), ALU.mult).then_inc(v.sig(free["vector"][2]), 1)
                eng.wait_ge(full_for_vector[3], v.nth(full_for_vector[3]))
                nv.tensor_tensor(tl(8, 7, T), bank[3][:, 0:T], cm("sin", T), ALU.mult).then_inc(v.sig(free["vector"][3]), 1)
                eng.wait_ge(*v.last)
                nv.tensor_tensor(tl(8, 6, T), tl(8, 6, T), tl(8, 7, T), ALU.add).then_inc(v.sig(vstep), 1)
                for g in range(2):
                    nv.tensor_scalar(tl(8, 4 + g, T), tl(2, 4, T), cm("half", 1, g), None, ALU.mult).then_inc(v.sig(vstep), 1)
                eng.wait_ge(*v.last)
                for h in range(4):
                    nv.tensor_scalar(tl(8, h, T), tl(8, 6, T), cm("quarter_mla", 1, h), None, ALU.mult).then_inc(v.sig(v2p if h == 3 else vstep), 1)
                for i, (s0, sn) in enumerate(QT):
                    b = (2, 3, 6)[i]
                    eng.wait_ge(full_for_vector[b], v.nth(full_for_vector[b]))
                    nv.tensor_tensor(XD[0:sn, i].rearrange("p (h f) -> p h f", h=8),
                                          bank[b][0:sn, :].rearrange("p (h f) -> p h f", h=8),
                                          TC[0:sn, i, 0:8].unsqueeze(2).to_broadcast([sn, 8, 64]), ALU.mult).then_inc(v.sig(free["vector"][b]), 1)
                for g in range(2):
                    for i, (s0, sn) in enumerate(QT):
                        b, o = ((4, 0), (5, 0), (5, 144))[i]
                        if i < 2:
                            eng.wait_ge(full_for_vector[b], v.nth(full_for_vector[b]))
                        nv.tensor_copy(CB[0:sn, g, PK[i]:PK[i] + T - s0], bank[b][0:sn, o:o + T - s0]).then_inc(v.sig(free["vector"][b] if i != 1 else vstep), 1)
                eng.wait_ge(*v.last)
                for h in range(8):
                    eng.wait_ge(a2v, v.nth(a2v))
                    for i, (s0, sn) in enumerate(QT):
                        x = PKT[0:sn, h % 2, PK[i]:PK[i] + T - s0]
                        nv.tensor_tensor(x, x, CB[0:sn, h // 4, PK[i]:PK[i] + T - s0], ALU.mult).then_inc(v.sig(v2p if i == 2 else vstep), 1)
                    if h > 1 and h % 2 == 0:
                        ssd_out(l, h // 2 - 1)
                ssd_out(l, 3)
                for g in range(2):
                    eng.wait_ge(full_for_vector[4 + g], v.nth(full_for_vector[4 + g]))
                    nv.tensor_scalar(small[:, g, 0:T], bank[4 + g][:, 0:T], 1.0 / 256, EPS_LN, ALU.mult, ALU.add).then_inc(v.sig(v2a if g else vstep), 1)
                eng.wait_ge(a2v, v.nth(a2v))
                nv.reciprocal(small[:, 0:2, 0:T], small[:, 0:2, 0:T]).then_inc(v.sig(vstep), 1)
                eng.wait_ge(*v.last)
                for j in range(4):
                    nv.scalar_tensor_tensor(out=tl(US, j, T), in0=tl(US, j, T), scalar=pc(f"ssd_g{l}", j),
                                                 in1=small[:, j // 2, 0:T], op0=ALU.mult, op1=ALU.mult).then_inc(v.sig(vstep), 1)

                def finish(h):
                    eng.wait_ge(a2v, v.nth(a2v, 3))
                    nv.reciprocal(cols[:, 56:58], cols[:, 56:58]).then_inc(v.sig(vstep), 1)
                    nv.reciprocal(cols[0:16, 58:59], cols[0:16, 58:59]).then_inc(v.sig(vstep), 1)
                    eng.wait_ge(*v.last)
                    for i, (q0, qn) in enumerate(QT):
                        x = prob(h)[0:qn, i, 0:q0 + qn]
                        nv.tensor_scalar(x, x, cols[0:qn, 56 + i:57 + i], None, ALU.mult).then_inc(v.sig(v2p if i == 2 else vstep), 1)

                for h in range(8):
                    for i, (q0, qn) in enumerate(QT):
                        b, o = ((2 * (h % 2), 0), (2 * (h % 2), P), (2 * (h % 2) + 1, 0))[i]
                        if i != 1:
                            eng.wait_ge(full_for_vector[b], v.nth(full_for_vector[b]))
                        nv.tensor_reduce(cols[0:qn, 40 + i:41 + i], bank[b][0:qn, o:o + q0 + qn], AX_X, ALU.max).then_inc(v.sig(vstep), 1)
                    eng.wait_ge(*v.last)
                    for i, (q0, qn) in enumerate(QT):
                        nv.tensor_scalar(cols[0:qn, 52 + i:53 + i], cols[0:qn, 40 + i:41 + i], -1.0, None, ALU.mult).then_inc(v.sig(v2a), 1)
                    finish(h)
                nv.memset(cols[:, 60:61], 0.0).then_inc(v.sig(v2p), 1)

            def ssd_out(l, j):
                b = 6 + j % 2
                eng.wait_ge(full_for_vector[b], v.nth(full_for_vector[b]))
                nv.scalar_tensor_tensor(out=tl(US, j, T), in0=tl(2, j, T), scalar=pc(f"dskip{l}", j), in1=bank[b][:, 0:T],
                                             op0=ALU.mult, op1=ALU.add).then_inc(v.sig(free["vector"][b]), 1)
                eng.wait_ge(*v.last)
                nv.tensor_tensor(tl(US, j, T), tl(US, j, T), tl(3, j, T), ALU.mult).then_inc(v.sig(v2a if j == 3 else vstep), 1)

            for l in range(DEPTH):
                ffn(T)
                residual(T, scale=0.5)
                norm(4 + 3 * l, T)
                mixer(l)
                residual(T)
                norm(5 + 3 * l, T)
                ffn(T)
                residual(T, scale=0.5)
                norm(6 + 3 * l, T)


def _pack_stream(x):
    def padded(a, rows=P, width=P):
        full = np.zeros((rows, width), np.float32)
        full[: a.shape[0], : a.shape[1]] = a
        return full

    rk = x["rwkv_w_rkv"][0]
    gin = x["gdn_w_in"][0]
    dense = {
        ("ada", 0): x["ada_w"][0], ("ada", 1): x["ada_w"][1],
        ("rwkv_r", 0): rk[0], ("rwkv_k", 0): rk[1], ("rwkv_v", 0): rk[2],
        ("w1a1", 0): np.concatenate([x["rwkv_w1"][0], x["rwkv_a1"][0]], 1),
        ("w2a2", 0): np.concatenate([x["rwkv_w2"][0], x["rwkv_a2"][0]], 0),
        ("g1", 0): x["rwkv_g1"][0], ("g2", 0): x["rwkv_g2"][0], ("rwkv_out", 0): x["rwkv_w_out"][0],
        ("gdn_in", 0): gin[:, : 4 * D], ("gdn_out", 0): x["gdn_w_out"][0],
        ("gdn_ba", 0): np.concatenate([gin[P * k:P * k + P, 4 * D:] for k in range(8)], 1),
    }
    for i in range(DEPTH):
        dense["ffn_in", i], dense["ffn_out", i] = x["ffn_w_in"][i], x["ffn_w_out"][i]
        for f in (1, 2):
            dense[f"gate{f}", i] = x[f"ffn{f}_w_gate_2"][i]
            dense[f"up{f}", i] = x[f"ffn{f}_w_up_2"][i]
            dense[f"down{f}", i] = x[f"ffn{f}_w_down_2"][i]
        wi = x["w_in_2"][i]
        z, xbc, dt_, fq, fk, fv, f_, cq, ckv, kr = np.split(wi, np.cumsum([512, 768, 8, 256, 256, 256, 4, 256, 128]), 1)
        dense["mix_in", i] = np.concatenate([xbc, z, fq, fk, fv, cq, ckv], 1)
        dtf = np.concatenate([dt_, f_], 1)
        dense["dtf", i] = padded(np.concatenate([dtf[P * k:P * k + P] for k in range(8)], 1))
        swapped = np.concatenate([kr[:, 16:], kr[:, :16]], 1)
        dense["kr", i] = np.concatenate([np.tile(kr, (1, 4)), np.tile(swapped, (1, 4))], 1)
        uq = x["mla_w_uq_2"][i].reshape(256, 4, 96)
        rope = uq[:, :, 64:]
        dense["uq", i] = np.concatenate(
            [uq[:, :, :64].reshape(256, 256), rope.reshape(256, P),
             np.concatenate([rope[:, :, 16:], rope[:, :, :16]], 2).reshape(256, P)], 1)
        ukv = x["mla_w_ukv_2"][i].reshape(P, 4, 128)
        dense["ukv", i] = np.concatenate([ukv[:, :, :64].reshape(P, 256), ukv[:, :, 64:].reshape(P, 256)], 1)
        dense["mix_out", i] = x["w_out_2"][i]
    m = manifest()
    out = np.zeros((-(-len(m) // BLOCKS), P, BLOCKS, P), np.float32)
    for at, (name, layer, n, k) in enumerate(m):
        out[at // BLOCKS, :, at % BLOCKS] = dense[name, layer][P * k:P * k + P, P * n:P * n + P]
    return out


def _pack_params(x):
    cols = param_columns()
    out = np.zeros((P, cols["_n"]), np.float32)

    def put(name, a, width=1):
        a = np.asarray(a).reshape(-1)
        if a.size >= P:
            a = a.reshape(-1, P).T
            out[:, cols[name]:cols[name] + a.shape[1]] = a
        else:
            out[: a.size, cols[name]] = a

    for i in range(DEPTH):
        put(f"ada_b{i}", x["ada_b"][i])
        for s in range(2):
            put(f"ln_g{i}{s}", x["ln_g"][i, s])
            put(f"ln_b{i}{s}", x["ln_b"][i, s])
    put("mu", x["rwkv_mu"][0])
    for n in ("w0", "a0", "k_k", "k_a", "r_k", "gn_g", "gn_b"):
        put(n, x["rwkv_" + n][0])
    put("gdn_conv", x["gdn_conv"][0])
    put("gdn_norm", x["gdn_norm_g"][0])
    put("gdn_alog", x["gdn_a_log"][0])
    put("gdn_dtb", x["gdn_dt_bias"][0])
    for i in range(DEPTH):
        for s in (1, 2, 3):
            put(f"ln{s}_g{i}", x[f"ln{s}_g_2"][i])
            put(f"ln{s}_b{i}", x[f"ln{s}_b_2"][i])
        put(f"conv_w{i}", x["conv_w_2"][i])
        put(f"conv_b{i}", x["conv_b_2"][i])
        put(f"dtb{i}", np.concatenate([x["dt_bias_2"][i], x["fox_f_b_2"][i]]))
        put(f"alog{i}", x["a_log_2"][i])
        put(f"dskip{i}", np.repeat(x["d_skip_2"][i], 64))
        put(f"ssd_g{i}", x["ssd_norm_g_2"][i])
        put(f"mlaq{i}", x["mla_q_norm_g_2"][i])
        put(f"mlakv{i}", x["mla_kv_norm_g_2"][i])
    return out


def _features_first(a):
    return np.ascontiguousarray(a.reshape(a.shape[0], DT, P).transpose(2, 1, 0))


def kernel(**inputs):
    import concourse.bacc as bacc
    from concourse.bass_utils import run_bass_kernel_spmd

    x = {k: np.asarray(v) for k, v in inputs.items()}
    _, const = constants()
    arrays = {
        "stream": _pack_stream(x), "params": _pack_params(x), "consts": const,
        "xin": _features_first(x["x"][0]),
        "cin": np.ascontiguousarray(x["c"].reshape(DT, P).T),
        "meta": _features_first(x["meta_2"]),
    }
    nc = bacc.Bacc("TRN2", target_bir_lowering=False, num_devices=1)
    args = [nc.dram_tensor(n, a.shape, F32, kind="ExternalInput").ap() for n, a in arrays.items()]
    out = nc.dram_tensor("out", (P, DT, SEQ), F32, kind="ExternalOutput").ap()
    first_and_second_block(nc, *args, out)
    r = run_bass_kernel_spmd(nc, [arrays], core_ids=[0])
    y = r.results[0]["out"]
    return np.ascontiguousarray(y.transpose(2, 1, 0)).reshape(1, SEQ, D)
```

```python
from contextlib import ExitStack

import numpy as np

import concourse.bass as bass
from concourse import mybir

ALU = mybir.AluOpType
ACT = mybir.ActivationFunctionType
F32 = mybir.dt.float32
F32R = mybir.dt.float32r
AX_X = mybir.AxisListType.X

P = 128
D = 1024
DT = D // P
SEQ = 256
META = 16
TALL = META + SEQ
DEPTH = 2
ALPHA = (2.0 * DEPTH) ** 0.25
FF = 2816
FT = FF // P
BLOCKS = 16
RING = 5
HIGHS = 3
SLOTS = 10
EPS_LN = 1e-5
NEG = -1e30
DECAY_SCALE = float(np.exp(-0.5))
BANKS = 8


PIECES = [(0, 1), (0, 0)] + [(0, q) for q in range(2, 6)] + [(1, q) for q in range(6)]
FIRST = 2
PIECE_SLABS = 4
ADA_SLABS = len(PIECES) * PIECE_SLABS
PROJ_SLABS = 14


def _dense(name, layer, n_tiles, k_tiles):
    return [(name, layer, n, k) for n in range(n_tiles) for k in range(k_tiles)]


def manifest():
    m = []

    def whole_slab():
        while len(m) % BLOCKS:
            m.append(("pad", 0, 0, 0))

    m += _dense("rwkv_k", 0, 8, 8)
    m += _dense("w1a1", 0, 1, 8)
    m += _dense("w2a2", 0, 8, 1)
    m += _dense("rwkv_r", 0, 8, 8)
    m += _dense("rwkv_v", 0, 8, 8)
    m += _dense("g1", 0, 1, 8)
    m += _dense("g2", 0, 8, 1)
    m += _dense("rwkv_out", 0, 8, 8)
    whole_slab()
    for n in range(FT):
        m += [("ffn_in", 0, n, k) for k in range(8)] + [("ffn_in", 0, FT + n, k) for k in range(8)]
    m += _dense("ffn_out", 0, 8, FT)
    m += [("gdn_ba", 0, 0, 0)]
    m += _dense("gdn_in", 0, 32, 8)
    whole_slab()
    m += _dense("gdn_out", 0, 8, 8)
    whole_slab()
    for n in range(FT):
        m += [("ffn_in", 1, n, k) for k in range(8)] + [("ffn_in", 1, FT + n, k) for k in range(8)]
    m += _dense("ffn_out", 1, 8, FT)
    for i in range(DEPTH):
        for f in (1, 2):
            whole_slab()
            for n in range(FT):
                m += [(f"gate{f}", i, n, k) for k in range(8)] + [(f"up{f}", i, n, k) for k in range(8)]
            m += _dense(f"down{f}", i, 8, FT)
            if f == 1:
                m += [("dtf", i, 0, 0)]
                m += _dense("mix_in", i, 19, 8)
                m += _dense("kr", i, 2, 8)
                whole_slab()
                m += _dense("uq", i, 4, 2)
                m += _dense("ukv", i, 4, 1)
                m += _dense("mix_out", i, 8, 8)
    return m


SPLIT = ("gdn_ba", "gdn_in", "dtf", "mix_in", "kr", "ffn_in", "ffn_out", "gate1", "up1", "down1", "gate2", "up2", "down2")


def split_slabs(m):
    return [s for s in range(-(-len(m) // BLOCKS)) if m[s * BLOCKS][0] in SPLIT]


STAGES = ("ffn", "gdn", "ffn", "ffn", "mixer", "ffn", "ffn", "mixer", "ffn")
STAGE_SLABS = {"ffn": FT * 24 // BLOCKS, "gdn": -(-(1 + 32 * 8) // BLOCKS), "mixer": -(-(1 + 21 * 8) // BLOCKS)}
STAGE_AT = [sum(STAGE_SLABS[x] for x in STAGES[:n]) for n in range(len(STAGES) + 1)]
HIGH_SLOT = {"ffn": 5, "gdn": 7, "mixer": 8}


def low_by_vector_engine(q):
    n = max(i for i in range(len(STAGES)) if STAGE_AT[i] <= q)
    return STAGES[n] == "ffn" and HIGHS <= q - STAGE_AT[n] < HIGHS + FT


def param_columns():
    cols, at = {}, 0

    def add(name, n):
        nonlocal at
        cols[name] = at
        at += n

    for i in range(DEPTH):
        add(f"ada_b{i}", 48)
        for s in range(2):
            add(f"ln_g{i}{s}", 8)
            add(f"ln_b{i}{s}", 8)
    add("mu", 48)
    for n in ("w0", "a0", "k_k", "k_a", "r_k", "gn_g", "gn_b"):
        add(n, 8)
    add("gdn_conv", 4 * 24)
    add("gdn_norm", 1)
    add("gdn_alog", 1)
    add("gdn_dtb", 1)
    for i in range(DEPTH):
        for s in (1, 2, 3):
            add(f"ln{s}_g{i}", 8)
            add(f"ln{s}_b{i}", 8)
        add(f"conv_w{i}", 4 * 6)
        add(f"conv_b{i}", 6)
        add(f"dtb{i}", 1)
        add(f"alog{i}", 1)
        add(f"dskip{i}", 4)
        add(f"ssd_g{i}", 4)
        add(f"mlaq{i}", 2)
        add(f"mlakv{i}", 1)
    cols["_n"] = at
    return cols


def constants():
    parts, cols, at = [], {}, 0

    def add(name, a):
        nonlocal at
        a = np.asarray(a, np.float32)
        full = np.zeros((P, a.shape[1]), np.float32)
        full[: a.shape[0]] = a
        cols[name] = at
        at += a.shape[1]
        parts.append(full)

    i = np.arange(P)
    r, c = i[:, None], i[None, :]
    add("ident", r == c)
    add("ones", np.ones((P, P)))
    chunk = r // 64 == c // 64
    add("strict64", (r < c) & chunk)
    add("incl64", (r <= c) & chunk)
    add("nstrict", -1.0 * (r < c))
    add("later_neg", NEG * (r > c))
    add("key_neg", NEG * (c > r))
    lv = [(r // 2 ** (l + 1) == c // 2 ** (l + 1)) & (r // 2**l % 2 == 1) & (c // 2**l % 2 == 0) for l in range(7)]
    add("level0T", lv[0].T)
    for l in range(1, 7):
        add(f"level{l}", lv[l])
    add("hsel", np.concatenate([(np.arange(16)[None, :] == 2 * j + r // 64) for j in range(8)], 1))
    add("hselT", np.concatenate([(np.arange(16)[:, None] == 2 * j + c // 64) for j in range(8)], 1))
    add("sel12", np.concatenate([np.repeat(np.arange(12)[:, None] == h, P, 1) for h in range(12)], 1))
    add("mean", np.full((P, P), 1.0 / D))
    add("sign12", np.where(np.arange(12) < 8, 1.0, -1.0)[:, None])
    add("hsel8", np.concatenate([np.repeat(np.arange(8)[None, :] == j, P, 0) for j in range(8)], 1))
    add("reset64", np.broadcast_to((np.arange(SEQ) % 64 != 0)[None, :], (P, SEQ)))
    add("half", np.stack([i < 64, i >= 64], 1))
    add("half_fox", 64.0**-0.5 * np.stack([i < 64, i >= 64], 1))
    add("half_mla", 96.0**-0.5 * np.stack([i < 64, i >= 64], 1))
    add("quarter_mla", 96.0**-0.5 * np.stack([i // 32 == q for q in range(4)], 1))
    freq = (10000.0 ** (-np.arange(0, 32, 2, dtype=np.float32) / 32)).astype(np.float32)
    ang = (freq[i % 16][:, None] * np.arange(TALL, dtype=np.float32)[None, :]).astype(np.float32)
    add("cos", np.cos(ang))
    add("sin", np.sin(ang) * np.where(i % 32 < 16, -1.0, 1.0)[:, None])
    cols["_n"] = at
    return cols, np.concatenate(parts, 1)


class Counts:

    def __init__(self):
        self.sent, self.taken, self.last = {}, {}, None

    def sig(self, sem):
        self.sent[sem] = self.sent.get(sem, 0) + 1
        self.last = (sem, self.sent[sem])
        return sem

    def nth(self, sem, n=1):
        self.taken[sem] = self.taken.get(sem, 0) + n
        return self.taken[sem]


def first_and_second_block(nc, stream, ada, params, consts, xin, cin, meta, out):
    M = manifest()
    HL = split_slabs(M)
    assert len(HL) == STAGE_AT[-1]
    PC = param_columns()
    CC, _ = constants()
    nv, na, ng = nc.vector, nc.scalar, nc.gpsimd

    with ExitStack() as ctx:
        def sb(name, shape):
            return ctx.enter_context(nc.sbuf_tensor(name, shape, F32))

        def sem(name):
            return ctx.enter_context(nc.semaphore(name))

        ring_at = -(-nc.sbuf_base // 32) * 32
        high_at = ring_at + 4 * RING * BLOCKS * P
        arena_at = high_at + 4 * HIGHS * BLOCKS * P
        tile_bytes = 4 * TALL
        ctx.enter_context(nc.sbuf_tensor("large", [P, (arena_at - ring_at) // 4 + SLOTS * DT * TALL], F32))

        def over(name, shape, dtype, address):
            return nc.alloc_sbuf_tensor_at(name, shape, dtype, offset=address)

        ring = over("ring", [P, RING, BLOCKS, P], F32, ring_at)
        ring_low = over("ring_low", [P, RING, BLOCKS, P], F32R, ring_at)
        high = over("high", [P, HIGHS, BLOCKS, P], F32R, high_at)
        ada_ring = over("ada_ring", [P, HIGHS, 2, D], F32, high_at)
        arena = over("arena", [P, SLOTS, DT, TALL], F32, arena_at)
        input_parts = {n: over(f"input_{n}", [P, DT, TALL], F32R, arena_at + slot_ * DT * tile_bytes)
                       for n, slot_ in (("low", 1), *HIGH_SLOT.items())}
        hidden_parts = {n: over(f"hidden_{n}", [P, FT, TALL], F32R, arena_at + slot_ * DT * tile_bytes)
                        for n, slot_ in (("high", 2), ("low", 6))}
        par = sb("par", [P, PC["_n"]])
        con = sb("con", [P, CC["_n"]])
        cond = sb("cond", [P, DT])
        one = sb("one", [P, 1])
        acc = sb("acc", [P, 2, D])
        mods = sb("mods", [P, DEPTH, 48])
        mod1 = sb("mod1", [P, DEPTH, 48])
        lnc = sb("lnc", [P, 10, 4, DT])
        small = sb("small", [P, 3, TALL])
        silu_t = sb("silu_t", [P, 2, TALL])
        XX = sb("XX", [P, 4, 2, P])
        ZZ = sb("ZZ", [P, 4, P])
        TOK = sb("TOK", [P, 2, 3, P])
        AZ = sb("AZ", [P, 2, 2, P])
        PP = sb("PP", [P, 4, P])
        cols = sb("cols", [P, 64])
        TC = sb("TC", [P, 3, 24])[:, :, :]
        prob_even = sb("prob_even", [P, 3, TALL])[:, :, :]
        WL = sb("WL", [P, DT, 4])[:, :, :]
        bank = [ctx.enter_context(nc.psum_tensor(f"bank{b}", [P, 512], F32)) for b in range(BANKS)]

        slab_loaded = [sem(f"slab_loaded{s}") for s in range(RING)]
        slab_used = sem("slab_used")
        inputs_loaded, cond_loaded, consts_loaded = sem("inputs_loaded"), sem("cond_loaded"), sem("consts_loaded")
        ada_loaded = [sem(f"ada_loaded{n}") for n in range(HIGHS)]
        ada_used, first_piece, later_piece = sem("ada_used"), sem("first_piece"), sem("later_piece")
        piece_summed, ada_scaled = sem("piece_summed"), sem("ada_scaled")
        stored = sem("stored")
        high_ready = sem("weights_high_ready")
        low_by_gpsimd, low_by_vector = sem("weights_low_by_gpsimd"), sem("weights_low_by_vector")
        hidden_low = sem("hidden_low")
        input_low, input_whole, meta_low, a2g = sem("input_low"), sem("input_whole"), sem("meta_low"), sem("meta_high")
        output_ready = sem("output_ready")
        vstep, astep, pool_step = sem("vector_step"), sem("scalar_step"), sem("pool_step")
        full = {r: [sem(f"bank{b}_full_for_{r}") for b in range(BANKS)] for r in ("vector", "scalar")}
        full_for_vector, full_for_scalar = full["vector"], full["scalar"]
        free = {r: [sem(f"bank{b}_free_by_{r}") for b in range(BANKS)] for r in ("vector", "scalar")}
        cond_ready = sem("cond_ready")
        gate_full, silu_ready = sem("gate_full"), sem("silu_ready")
        up_full, hidden_ready = sem("up_full"), sem("hidden_ready")
        resid_ready = sem("resid_ready")
        centered, squared = sem("centered"), sem("squared")
        var_ready, std_ready = sem("var_ready"), sem("std_ready")
        normed, input_high_ready = sem("normed"), sem("input_high_ready")
        lerp_ready, lerp_used = sem("lerp_ready"), sem("lerp_used")
        v2p, a2p = sem("vector_result_for_tensor"), sem("scalar_result_for_tensor")
        v2a, a2v = sem("vector_result_for_scalar"), sem("scalar_result_for_vector")
        p2v = sem("tensor_done_for_vector")

        XAS, US = 0, 1

        def slot(i):
            return arena[:, i]

        def tl(i, j, T=SEQ, t0=0):
            return arena[:, i, j, t0:t0 + T]

        def pc(name, j=0, rows=P, width=1):
            return par[0:rows, PC[name] + j:PC[name] + j + width]

        def cm(name, w=P, off=0, rows=P, r0=0):
            return con[r0:rows, CC[name] + off:CC[name] + off + w]

        ident = cm("ident")


        def input_high(stage, k, T):
            return input_parts[stage][:, k, TALL - T:TALL]

        def input_rest(k, T):
            return input_parts["low"][:, k, TALL - T:TALL]

        def hidden_high(f, T):
            return hidden_parts["high"][:, f, 0:T]

        def hidden_rest(f, T):
            return hidden_parts["low"][:, f, 0:T]

        PK = (0, TALL, TALL + TALL - P)
        flat = lambda s, a, b: arena[:, s].rearrange("p j t -> p (j t)")[:, a:b]
        EX = flat(8, 0, 512).rearrange("p (n f) -> p n f", n=2)
        KB = flat(8, 512, 1024).rearrange("p (n f) -> p n f", n=2)
        DC = flat(8, 1024, 1536).rearrange("p (n f) -> p n f", n=4)
        DS = flat(8, 1536, 2048).rearrange("p (n f) -> p n f", n=4)
        XD = flat(6, 0, 1536).rearrange("p (n f) -> p n f", n=3)
        FV = flat(5, 4 * TALL, 4 * TALL + 768).rearrange("p (n f) -> p n f", n=3)
        MV = flat(3, 4 * TALL, 4 * TALL + 768).rearrange("p (n f) -> p n f", n=3)
        CB = flat(9, 0, 864).rearrange("p (g f) -> p g f", g=2)
        PKT = XX[:, :, :, :].rearrange("p a b f -> p (a b f)")[:, 0:864].rearrange("p (n f) -> p n f", n=2)

        def prob(h):
            return arena[:, 2, 4:7] if h % 2 else prob_even

        def decay_col(i, h, sn):
            return TC[0:sn, i, 12 + h:13 + h]

        GM = arena[:, 3].rearrange("p j t -> p (j t)")[:, 0:2048].rearrange("p (u f) -> p u f", u=4)

        def xview(T):
            return TALL - T

        norm_of = {"mixer": 0, "ffn": 1}


        block = ctx.enter_context(nc.Block())

        @block.sync
        def _(sp):
            slabs = -(-len(M) // BLOCKS)
            def ada_slab(a):
                if a >= HIGHS:
                    sp.wait_ge(ada_used, a - HIGHS + 1)
                sp.dma_start(ada_ring[:, a % HIGHS], ada[a]).then_inc(ada_loaded[a % HIGHS], 16)

            def slab(s):
                if s >= RING:
                    sp.wait_ge(slab_used, s - RING + 1)
                sp.dma_start(ring[:, s % RING], stream[s]).then_inc(slab_loaded[s % RING], 16)

            sp.dma_start(cond[:, :], cin).then_inc(cond_loaded, 16)
            for a in range(HIGHS):
                ada_slab(a)
            for dst, src in ((par[:, :], params), (arena[:, XAS, :, META:TALL], xin), (arena[:, US, :, 0:META], meta)):
                sp.dma_start(dst, src).then_inc(inputs_loaded, 16)
            for a in range(HIGHS, FIRST * PIECE_SLABS):
                ada_slab(a)
            slab(0)
            sp.dma_start(con[:, :], consts).then_inc(consts_loaded, 16)
            for s in range(1, RING):
                slab(s)
            for s in range(RING, PROJ_SLABS + RING):
                slab(s)
                if s - RING < FIRST * PIECE_SLABS:
                    ada_slab(FIRST * PIECE_SLABS + s - RING)
            for a in range(2 * FIRST * PIECE_SLABS, ADA_SLABS):
                ada_slab(a)
            for s in range(PROJ_SLABS + RING, slabs):
                slab(s)
            for half in range(2):
                js = slice(4 * half, 4 * half + 4)
                sp.wait_ge(output_ready, 4 * half + 4)
                sp.dma_start(out[:, js], arena[:, US, js, META:TALL]).then_inc(stored, 16)
            sp.wait_ge(stored, 32)

        @block.tensor
        def _(eng):
            pe = Counts()
            prev = [None] * BANKS
            at, owed, given_back = [0], [], [0]

            def freed(b):
                r = prev[b] or "vector"
                n = pe.nth(free[r][b], 1 if prev[b] else 0)
                prev[b] = None
                return free[r][b], n

            def mm(o, l, r, start=True, stop_=True, hold=False):
                ins = nc.tensor.matmul(o, l, r, start=start, stop=stop_, skip_group_check=True)
                if owed and not hold:
                    ins.then_inc(owed.pop(0), 1)
                return ins

            def transpose_to(o, x, rows=P, hold=False):
                ins = nc.tensor.transpose(o, x, con[0:rows, CC["ident"]:CC["ident"] + rows])
                if owed and not hold:
                    ins.then_inc(owed.pop(0), 1)
                return ins

            def closing(b, reader):
                prev[b] = reader
                return full[reader][b]

            def told(b, reader):
                return full[reader][b]

            def left(s):
                owed.extend([slab_used] * (s - given_back[0]))
                given_back[0] = s

            def w(key):
                while M[at[0]][0] == "pad":
                    at[0] += 1
                n = at[0]
                assert M[n] == key, (M[n], key)
                s = n // BLOCKS
                if n % BLOCKS == 0:
                    eng.wait_ge(slab_loaded[s % RING], 16 * (s // RING + 1))
                    left(s)
                at[0] += 1
                return ring[:, s % RING, n % BLOCKS, :]

            def split_block(key):
                while M[at[0]][0] == "pad":
                    at[0] += 1
                n = at[0]
                assert M[n] == key, (M[n], key)
                s = n // BLOCKS
                q = HL.index(s)
                if n % BLOCKS == 0:
                    by_vector = sum(low_by_vector_engine(x) for x in range(q + 1))
                    if low_by_vector_engine(q):
                        eng.wait_ge(low_by_vector, by_vector)
                    else:
                        eng.wait_ge(low_by_gpsimd, q + 1 - by_vector)
                    left(s)
                at[0] += 1
                return high[:, q % HIGHS, n % BLOCKS, :], ring_low[:, s % RING, n % BLOCKS, :]

            def by_parts(o, w_high, w_low, x_high, x_low, first, last, signal=None):
                mm(o, w_high, x_high, first, False)
                mm(o, w_low, x_high, False, False)
                m = mm(o, w_high, x_low, False, last, hold=last and signal is not None)
                if last and signal is not None:
                    m.then_inc(signal, 1)

            def split_product(o, key, x_high, x_low, first, last, signal=None):
                w_high, w_low = split_block(key)
                by_parts(o, w_high, w_low, x_high, x_low, first, last, signal)

            def project_by_parts(stage, name, layer, n_tiles, T, banks, reader, n0=0, freed_by=None):
                for n in range(n_tiles):
                    b = banks[n % len(banks)]
                    eng.wait_ge(*freed(b))
                    for k in range(DT):
                        split_product(bank[b][:, 0:T], (name, layer, n0 + n, k), input_high(stage, k, T),
                                      input_rest(k, T), k == 0, k == DT - 1, closing(b, reader))
                    prev[b] = freed_by or reader

            def project(name, layer, n_tiles, k_tiles, rhs, T, banks, reader, n0=0, ready=None, final=False, freed_by=None):
                for n in range(n_tiles):
                    b = banks[n % len(banks)]
                    eng.wait_ge(*freed(b))
                    for k in range(k_tiles):
                        if n == 0 and ready is not None:
                            eng.wait_ge(ready, pe.nth(ready))
                        m = mm(bank[b][:, 0:T], w((name, layer, n0 + n, k)), rhs(k), k == 0,
                               k == k_tiles - 1, hold=k == k_tiles - 1)
                        if k == k_tiles - 1:
                            m.then_inc(closing(b, reader), 1)
                    prev[b] = freed_by or reader
                if final:
                    prev[b] = None

            resid = {"base": 0, "got": 0}

            def residual(n):
                while resid["got"] < n:
                    eng.wait_ge(resid_ready, pe.nth(resid_ready))
                    resid["got"] += 1

            def out_projection(name, layer, k_tiles, rhs, T, n0=0):
                resid["got"] = 0
                for n in range(DT):
                    b = 6 + n % 2
                    eng.wait_ge(*freed(b))
                    residual(n - 1)
                    for k in range(k_tiles):
                        m = mm(bank[b][:, 0:T], w((name, layer, n, k)), rhs(k), k == 0, k == k_tiles - 1,
                               hold=k == k_tiles - 1)
                        if k == k_tiles - 1:
                            m.then_inc(full["vector"][b], 1)

            def norm(T):
                t0 = xview(T)
                eng.wait_ge(*freed(4))
                for j in range(DT):
                    residual(j + 1)
                    m = mm(bank[4][:, 0:T], cm("mean"), tl(XAS, j, T, t0), j == 0, j == DT - 1, hold=j == DT - 1)
                    if j == DT - 1:
                        m.then_inc(told(4, "vector"), 1)
                eng.wait_ge(*freed(5))
                for j in range(DT):
                    if j % 2 == 0:
                        eng.wait_ge(squared, pe.nth(squared))
                    m = mm(bank[5][:, 0:T], cm("mean"), tl(9, j, T), j == 0, j == DT - 1, hold=j == DT - 1)
                    if j == DT - 1:
                        m.then_inc(told(5, "vector"), 1)

            def ffn(name_g, name_u, name_d, layer, T, up0):
                for b in range(4):
                    eng.wait_ge(*freed(b))
                for f in range(FT):
                    if f >= 2:
                        eng.wait_ge(hidden_ready, pe.nth(hidden_ready))
                    g, u = 2 * (f % 2), 2 * (f % 2) + 1
                    for k in range(DT):
                        if f == 0:
                            eng.wait_ge(input_low, pe.nth(input_low))
                        split_product(bank[g][:, 0:T], (name_g, layer, f, k), input_high("ffn", k, T), input_rest(k, T),
                                      k == 0, k == 7, gate_full)
                    for k in range(DT):
                        split_product(bank[u][:, 0:T], (name_u, layer, up0 + f, k), input_high("ffn", k, T),
                                      input_rest(k, T), k == 0, k == 7, up_full)
                pe.nth(hidden_ready, 2)
                resid["got"] = 0
                for n in range(DT):
                    b = 6 + n % 2
                    eng.wait_ge(*freed(b))
                    residual(n - 1)
                    for k in range(FT):
                        if n == 0:
                            eng.wait_ge(hidden_low, pe.nth(hidden_low))
                        split_product(bank[b][:, 0:T], (name_d, layer, n, k), hidden_high(k, T),
                                      hidden_rest(k, T), k == 0, k == FT - 1, full["vector"][b])
                left(at[0] // BLOCKS)

            def row_sums(src_slot, b, reader, sel, width, wait=None):
                eng.wait_ge(*freed(b))
                for j in range(DT):
                    m = mm(bank[b][0:width, 0:SEQ], cm(sel, width, width * j), tl(src_slot, j), j == 0,
                           j == 7, hold=j == 7)
                    if j == 7:
                        m.then_inc(told(b, reader), 1)

            def spread(rows, sel, nrows, banks, close=closing):
                for j in range(DT):
                    b = banks[j // 2]
                    if j % 2 == 0:
                        eng.wait_ge(*freed(b))
                    m = mm(bank[b][:, 256 * (j % 2):256 * (j % 2) + SEQ], cm(sel, P, P * j, nrows), rows,
                           True, True, hold=j % 2)
                    if j % 2:
                        m.then_inc(close(b, "vector"), 1)

            def inverse(levels):
                for b in range(4):
                    eng.wait_ge(*freed(b))
                for l in range(1, levels):
                    for p in range(2):
                        eng.wait_ge(v2p, pe.nth(v2p))
                        for u in (2 * p, 2 * p + 1):
                            m = mm(bank[p][:, P * (u % 2):P * (u % 2) + P], GM[:, u, 0:P], XX[:, u, 0], True,
                                   True, hold=u % 2)
                            if u % 2:
                                m.then_inc(told(p, "vector"), 1)
                    for p in range(2):
                        eng.wait_ge(v2p, pe.nth(v2p))
                        for u in (2 * p, 2 * p + 1):
                            o = 2 * P * (u % 2)
                            if l < levels - 1:
                                mm(bank[2 + p][:, o:o + P], XX[:, u, 1], ZZ[:, u], True, True)
                            m = mm(bank[2 + p][:, o + P:o + 2 * P], ZZ[:, u], XX[:, u, 1], True, True, hold=u % 2)
                            if u % 2:
                                m.then_inc(told(2 + p, "vector"), 1)

            def sum_piece(n, b, ready):
                eng.wait_ge(ready, pe.nth(ready))
                eng.wait_ge(*freed(b))
                for f in range(DT):
                    m = mm(bank[b][:, f:f + 1], acc[:, n % 2, P * f:P * f + P], one[:, :], True, True, hold=f == 7)
                    if f == 7:
                        m.then_inc(piece_summed, 1)
                prev[b] = "vector"

            for n in range(FIRST):
                sum_piece(n, n, first_piece)


            U = lambda k: tl(US, k, SEQ, META)
            L = [lambda k: tl(2, k), lambda k: tl(3, k)]
            B4 = [0, 1, 2, 3]
            project("rwkv_k", 0, 8, 8, L[0], SEQ, B4, "scalar", ready=lerp_ready)
            owed.append(lerp_used)
            eng.wait_ge(*freed(4))
            eng.wait_ge(*freed(5))
            for k in range(8):
                wk = w(("w1a1", 0, 0, k))
                eng.wait_ge(lerp_ready, pe.nth(lerp_ready))
                m = mm(bank[4][0:64, 0:SEQ], wk[:, 0:64], L[1](k), k == 0, k == 7, hold=k == 7)
                if k == 7:
                    m.then_inc(told(4, "scalar"), 1)
            owed.append(lerp_used)
            eng.wait_ge(lerp_ready, pe.nth(lerp_ready, 8))
            for k in range(8):
                wk = ring[:, ((at[0] - 8 + k) // BLOCKS) % RING, (at[0] - 8 + k) % BLOCKS, :]
                m = mm(bank[5][64:128, 0:SEQ], wk[:, 64:128], L[0](k), k == 0, k == 7, hold=k == 7)
                if k == 7:
                    m.then_inc(told(5, "scalar"), 1)
            owed.append(lerp_used)
            eng.wait_ge(a2p, pe.nth(a2p, 2))
            for n in range(8):
                wk = w(("w2a2", 0, n, 0))
                b = 2 * (n % 2)
                eng.wait_ge(*freed(b))
                mm(bank[b][:, 0:SEQ], wk[0:64, :], small[0:64, 0, 0:SEQ], True, True, hold=True).then_inc(closing(b, "scalar"), 1)
                eng.wait_ge(*freed(b + 1))
                mm(bank[b + 1][:, 0:SEQ], wk[64:128, :], small[64:128, 0, 0:SEQ], True, True, hold=True).then_inc(closing(b + 1, "scalar"), 1)
            project("rwkv_r", 0, 8, 8, L[1], SEQ, B4, "scalar", ready=lerp_ready)
            owed.append(lerp_used)
            project("rwkv_v", 0, 8, 8, L[0], SEQ, B4, "scalar", ready=lerp_ready)
            owed.append(lerp_used)
            project("g1", 0, 1, 8, L[1], SEQ, [4], "scalar", ready=lerp_ready, final=True)
            eng.wait_ge(a2p, pe.nth(a2p))
            project("g2", 0, 8, 1, lambda k: small[:, 1, 0:SEQ], SEQ, B4, "scalar", final=True)
            left(PROJ_SLABS)
            eng.wait_ge(consts_loaded, 16)
            eng.wait_ge(a2p, pe.nth(a2p))
            row_sums(9, 4, "vector", "hsel", 16)
            eng.wait_ge(v2p, pe.nth(v2p))
            row_sums(3, 5, "scalar", "hsel", 16)
            eng.wait_ge(v2p, pe.nth(v2p))
            spread(small[0:16, 2, 0:SEQ], "hselT", 16, B4)

            for j in range(DT):
                if j == 0:
                    sum_piece(FIRST, 0, later_piece)
                if j == 0:
                    eng.wait_ge(v2p, pe.nth(v2p))
                for tau in range(2):
                    ts = slice(P * tau, P * tau + P)
                    b = 4 + tau
                    eng.wait_ge(*freed(b))
                    for n, s in enumerate((8, 4, 6, 5)):
                        m = transpose_to(bank[b][:, P * n:P * n + P], arena[:, s, j, ts], hold=n == 3)
                        if n == 3:
                            m.then_inc(told(b, "scalar"), 1)
                for u in range(4):
                    tau, e = u // 2, u % 2
                    ts = slice(P * tau, P * tau + P)
                    b = 6 + e
                    eng.wait_ge(*freed(b))
                    rows = slice(64 * e, 64 * e + 64)
                    ra = arena[rows, 5:8:2, j, ts]
                    mm(bank[b][:, 0:256], arena[rows, 6, j, ts], ra, True, True)
                    mm(bank[b][:, 256:512], arena[rows, 4, j, ts], ra, True, True, hold=True).then_inc(closing(b, "vector"), 1)
                for p in range(2):
                    eng.wait_ge(v2p, pe.nth(v2p))
                    eng.wait_ge(*freed(2 + p))
                    for u in (2 * p, 2 * p + 1):
                        m = transpose_to(bank[2 + p][:, P * (u % 2):P * (u % 2) + P], XX[:, u, 1], hold=u % 2)
                        if u % 2:
                            m.then_inc(told(2 + p, "vector"), 1)
                inverse(6)
                sum_piece(FIRST + 1 + j, 0, later_piece)
                eng.wait_ge(a2p, pe.nth(a2p, 2))
                eng.wait_ge(v2p, pe.nth(v2p, 2))
                for tau in range(2):
                    b = 4 + tau
                    eng.wait_ge(*freed(b))
                    for e in range(2):
                        m = mm(bank[b][:, 64 * e:64 * e + 64], GM[:, 2 * tau + e, 256:384],
                               TOK[:, tau, 0, 64 * e:64 * e + 64], True, True, hold=e)
                        if e:
                            m.then_inc(told(b, "scalar"), 1)
                for tau in range(2):
                    eng.wait_ge(a2p, pe.nth(a2p))
                    b = 4 + tau
                    eng.wait_ge(*freed(b))
                    for e in range(2):
                        m = mm(bank[b][:, P * e:P * e + P], XX[:, 2 * tau + e, 1], AZ[:, tau, e], True, True, hold=e)
                        if e:
                            m.then_inc(told(b, "scalar"), 1)
                for tau in range(2):
                    eng.wait_ge(a2p, pe.nth(a2p))
                    b = tau
                    eng.wait_ge(*freed(b))
                    for e in range(2):
                        u, o = 2 * tau + e, slice(64 * e, 64 * e + 64)
                        mm(bank[b][o, 0:P], PP[:, u, 0:64], GM[:, u, P:2 * P], True, True)
                        mm(bank[b][o, P:2 * P], PP[:, u, 64:128], GM[:, u, P:2 * P], True, False)
                        m = mm(bank[b][o, P:2 * P], TOK[:, tau, 0, o], GM[:, u, 3 * P:4 * P], False, True, hold=e)
                        if e:
                            m.then_inc(closing(b, "vector"), 1)
                    for cc in range(2):
                        c = 2 * tau + cc
                        if c == 3:
                            continue
                        b = (2, 3, 6)[c]
                        eng.wait_ge(*freed(b))
                        rows = slice(64 * cc, 64 * cc + 64)
                        for e in range(2):
                            u, o = 2 * tau + e, slice(64 * e, 64 * e + 64)
                            mm(bank[b][o, 0:64], TOK[rows, tau, 2, o], PP[rows, u, 64:128], True, False)
                            m = mm(bank[b][o, 0:64], TOK[rows, tau, 1, o], TOK[rows, tau, 0, o], False, True,
                                   hold=e and c == 0)
                            if e and c == 0:
                                m.then_inc(closing(b, "vector"), 1)
                            if c:
                                m = mm(bank[b][o, 64:128], PP[rows, u, 0:64], TOK[rows, tau, 2, o], True,
                                       True, hold=e)
                                if e:
                                    m.then_inc(closing(b, "vector"), 1)
            for c in (1, 2):
                eng.wait_ge(v2p, pe.nth(v2p))
                eng.wait_ge(*freed(c))
                for j in range(DT):
                    m = mm(bank[c][:, 64 * j:64 * j + 64], arena[:, 9, j, P * (c - 1):P * c],
                           arena[:, 2, j, 192:256], True, True, hold=j == 7)
                    if j == 7:
                        m.then_inc(closing(c, "vector"), 1)
            eng.wait_ge(v2p, pe.nth(v2p))
            for j in range(DT):
                b = B4[j % 4]
                eng.wait_ge(*freed(b))
                if j >= 4:
                    eng.wait_ge(v2p, pe.nth(v2p))
                for c in (1, 2, 3):
                    m = mm(bank[b][:, 64 * c:64 * c + 64], arena[:, (3, 4, 6)[c - 1], j, 0:P],
                           tl(7, j)[:, 64 * c:64 * c + 64], True, True, hold=c == 3)
                    if c == 3:
                        m.then_inc(told(b, "vector"), 1)
            eng.wait_ge(v2p, pe.nth(v2p, 4))
            row_sums(5, 4, "scalar", "hsel", 16)
            eng.wait_ge(a2p, pe.nth(a2p))
            spread(small[0:16, 0, 0:SEQ], "hselT", 16, B4, told)
            eng.wait_ge(a2p, pe.nth(a2p))
            row_sums(3, 5, "vector", "hsel", 16)
            eng.wait_ge(v2p, pe.nth(v2p))
            spread(small[0:16, 2, 0:SEQ], "hselT", 16, B4)
            spread(small[0:16, 1, 0:SEQ], "hselT", 16, B4)
            eng.wait_ge(v2p, pe.nth(v2p))
            sum_piece(len(PIECES) - 1, 0, later_piece)
            out_projection("rwkv_out", 0, 8, lambda k: tl(5, k), SEQ)
            norm(SEQ)
            ffn("ffn_in", "ffn_in", "ffn_out", 0, SEQ, FT)
            norm(SEQ)
            eng.wait_ge(*freed(4))
            eng.wait_ge(*freed(5))
            w_high, w_low = split_block(("gdn_ba", 0, 0, 0))
            for k in range(8):
                eng.wait_ge(input_low, pe.nth(input_low))
                c = slice(16 * k, 16 * k + 8)
                by_parts(bank[4][0:8, 0:SEQ], w_high[:, c], w_low[:, c], input_high("gdn", k, SEQ),
                         input_rest(k, SEQ), k == 0, k == 7, told(4, "scalar"))
            for k in range(8):
                c = slice(16 * k + 8, 16 * k + 16)
                by_parts(bank[5][0:8, 0:SEQ], w_high[:, c], w_low[:, c], input_high("gdn", k, SEQ),
                         input_rest(k, SEQ), k == 0, k == 7, told(5, "scalar"))
            project_by_parts("gdn", "gdn_in", 0, 24, SEQ, B4, "vector", freed_by="scalar")
            project_by_parts("gdn", "gdn_in", 0, 8, SEQ, B4, "scalar", n0=24)
            left(-(-at[0] // BLOCKS))
            eng.wait_ge(a2p, pe.nth(a2p))
            row_sums(8, 4, "vector", "hsel8", 8)
            row_sums(3, 5, "vector", "hsel8", 8)
            eng.wait_ge(v2p, pe.nth(v2p))
            spread(small[0:8, 2, 0:SEQ], "sel12", 8, B4)
            spread(small[0:8, 1, 0:SEQ], "sel12", 8, B4)
            eng.wait_ge(a2p, pe.nth(a2p))
            for n, (row, c) in enumerate(((0, 0), (0, 1), (4, 0), (4, 1), (5, 0))):
                m = transpose_to(bank[4][:, 8 * n:8 * n + 8], arena[0:8, 9, row, P * c:P * c + P], rows=8,
                                 hold=n == 4)
                if n == 4:
                    m.then_inc(told(4, "vector"), 1)
            eng.wait_ge(v2p, pe.nth(v2p))
            for hp in range(4):
                heads = (2 * hp, 2 * hp + 1)
                gc, beta = arena[0:8, 9, 4], arena[0:8, 9, 0]
                for b in (4, 5, 6, 7):
                    eng.wait_ge(*freed(b))
                for hh, h in enumerate(heads):
                    m = mm(bank[4][:, SEQ * hh:SEQ * hh + SEQ], cm("sel12", P, P * h, 8), gc[:, 0:SEQ], True,
                           True, hold=hh)
                    if hh:
                        m.then_inc(told(4, "scalar"), 1)
                for hh, h in enumerate(heads):
                    m = mm(bank[5][:, SEQ * hh:SEQ * hh + SEQ], cm("sel12", P, P * h, 8), beta[:, 0:SEQ],
                           True, True, hold=hh)
                    if hh:
                        m.then_inc(told(5, "vector"), 1)
                for u in range(4):
                    h, c = heads[u // 2], u % 2
                    o = slice(P * u, P * u + P)
                    mm(bank[6][:, o], cm("sel12", P, P * h, 8), gc[:, P * c:P * c + P], True, False)
                    m = mm(bank[6][:, o], ident, cm("later_neg"), False, True, hold=u == 3)
                    if u == 3:
                        m.then_inc(told(6, "scalar"), 1)
                eng.wait_ge(v2p, pe.nth(v2p))
                for hh, h in enumerate(heads):
                    b = (7, 5)[hh]
                    for c in range(2):
                        cs = slice(P * c, P * c + P)
                        mm(bank[b][:, 2 * P * c:2 * P * c + P], tl(4, h)[:, cs], KB[:, hh, cs], True, True)
                        m = mm(bank[b][:, 2 * P * c + P:2 * P * c + 2 * P], tl(4, h)[:, cs], tl(2, h)[:, cs],
                               True, True, hold=c)
                        if c:
                            m.then_inc(told(b, "vector"), 1)
                eng.wait_ge(a2p, pe.nth(a2p, 2))
                for hh, h in enumerate(heads):
                    b = (4, 6)[hh]
                    for n, (s, c) in enumerate(((5, 0), (5, 1), (4, 0))):
                        m = transpose_to(bank[b][:, P * n:P * n + P], tl(s, h)[:, P * c:P * c + P], hold=n == 2)
                        if n == 2:
                            m.then_inc(told(b, "scalar"), 1)
                for p in range(2):
                    eng.wait_ge(v2p, pe.nth(v2p))
                    eng.wait_ge(*freed(2 + p))
                    for u in (2 * p, 2 * p + 1):
                        m = transpose_to(bank[2 + p][:, P * (u % 2):P * (u % 2) + P], XX[:, u, 1], hold=u % 2)
                        if u % 2:
                            m.then_inc(told(2 + p, "vector"), 1)
                inverse(7)
                eng.wait_ge(v2p, pe.nth(v2p, 2))
                eng.wait_ge(a2p, pe.nth(a2p))
                both = lambda b: [bank[b][:, 0:P], bank[b][:, P:2 * P]]
                for hh in range(2):
                    m = mm(both(4)[hh], XX[:, 2 * hh, 1], TOK[:, hh, 0], True, True, hold=hh)
                    if hh:
                        m.then_inc(told(4, "scalar"), 1)
                eng.wait_ge(a2p, pe.nth(a2p))
                for hh in range(2):
                    m = mm(both(5)[hh], TOK[:, hh, 2], AZ[:, hh, 0], True, True, hold=hh)
                    if hh:
                        m.then_inc(told(5, "scalar"), 1)
                eng.wait_ge(a2p, pe.nth(a2p))
                for hh in range(2):
                    m = mm(both(6)[hh], PP[:, 2 + hh], ZZ[:, 2 * hh], True, True, hold=hh)
                    if hh:
                        m.then_inc(told(6, "vector"), 1)
                eng.wait_ge(v2p, pe.nth(v2p))
                for hh in range(2):
                    m = mm(both(7)[hh], XX[:, 2 * hh + 1, 1], AZ[:, hh, 1], True, True, hold=hh)
                    if hh:
                        m.then_inc(told(7, "scalar"), 1)
                eng.wait_ge(a2p, pe.nth(a2p))
                for hh in range(2):
                    o0, o1 = slice(SEQ * hh, SEQ * hh + P), slice(SEQ * hh + P, SEQ * hh + SEQ)
                    mm(bank[4][:, o0], AZ[:, hh, 0], GM[:, 2 * hh, P:2 * P], True, True)
                    mm(bank[4][:, o1], ZZ[:, 2 * hh], PP[:, hh], True, False)
                    m = mm(bank[4][:, o1], ZZ[:, 2 * hh + 1], GM[:, 2 * hh + 1, P:2 * P], False, True, hold=hh)
                    if hh:
                        m.then_inc(closing(4, "scalar"), 1)
            eng.wait_ge(a2p, pe.nth(a2p))
            row_sums(8, 5, "vector", "hsel8", 8)
            eng.wait_ge(v2p, pe.nth(v2p))
            spread(small[0:8, 2, 0:SEQ], "sel12", 8, B4)
            eng.wait_ge(v2p, pe.nth(v2p))
            out_projection("gdn_out", 0, 8, lambda k: tl(7, k), SEQ)
            norm(SEQ)
            ffn("ffn_in", "ffn_in", "ffn_out", 1, SEQ, FT)
            norm(SEQ)

            T = TALL
            UA = lambda k: tl(US, k, T)
            QT = ((0, 128), (128, 128), (256, 16))

            def by_packed(o, lhs, rhs, hold):
                for i, (s0, sn) in enumerate(QT):
                    m = mm(o[:, s0:T], lhs(i, sn), rhs[0:sn, PK[i]:PK[i] + T - s0], i == 0, i == 2, hold=hold and i == 2)
                return m

            def mixer(l):
                eng.wait_ge(*freed(4))
                w_high, w_low = split_block(("dtf", l, 0, 0))
                for k in range(8):
                    eng.wait_ge(input_low, pe.nth(input_low))
                    c = slice(12 * k, 12 * k + 12)
                    by_parts(bank[4][0:12, 0:T], w_high[:, c], w_low[:, c], input_high("mixer", k, T),
                             input_rest(k, T), k == 0, k == 7, told(4, "scalar"))
                project_by_parts("mixer", "mix_in", l, 6, T, B4, "vector", freed_by="scalar")
                project_by_parts("mixer", "mix_in", l, 13, T, B4, "scalar", n0=6)
                project_by_parts("mixer", "kr", l, 1, T, [6], "vector")
                eng.wait_ge(a2p, pe.nth(a2p))
                eng.wait_ge(*freed(4))
                eng.wait_ge(*freed(5))
                for k in range(2):
                    m = mm(bank[4][:, 0:T], cm("ones"), tl(6, k, T), k == 0, k == 1, hold=k)
                    if k:
                        m.then_inc(told(4, "vector"), 1)
                mm(bank[5][:, 0:T], cm("ones"), tl(6, 2, T), True, True, hold=True).then_inc(told(5, "vector"), 1)
                project_by_parts("mixer", "kr", l, 1, T, [7], "vector", n0=1)
                left(-(-at[0] // BLOCKS))
                eng.wait_ge(v2p, pe.nth(v2p))
                project("uq", l, 2, 2, lambda k: tl(4, 4 + k, T), T, [0, 1], "scalar")
                project("uq", l, 2, 2, lambda k: tl(4, 4 + k, T), T, [2, 3], "vector", n0=2)
                project("ukv", l, 4, 1, lambda k: tl(4, 6, T), T, [0, 1, 4, 5], "scalar", final=True)
                eng.wait_ge(v2p, pe.nth(v2p))
                eng.wait_ge(*freed(6))
                for i, (s0, sn) in enumerate(QT):
                    for n, row in enumerate((4, 5)):
                        o = 24 * i + 12 * n
                        m = transpose_to(bank[6][0:sn, o:o + 12], arena[0:12, 9, row, s0:s0 + sn], rows=12,
                                         hold=i == 2 and n)
                        if i == 2 and n:
                            m.then_inc(told(6, "vector"), 1)
                eng.wait_ge(a2p, pe.nth(a2p))
                eng.wait_ge(v2p, pe.nth(v2p))
                for i, (s0, sn) in enumerate(QT):
                    b = (2, 3, 6)[i]
                    eng.wait_ge(*freed(b))
                    for j in range(4):
                        m = transpose_to(bank[b][0:sn, P * j:P * j + P], tl(2, j, T)[:, s0:s0 + sn], hold=j == 3)
                        if j == 3:
                            m.then_inc(closing(b, "vector"), 1)
                for i, (s0, sn) in enumerate(QT):
                    b = (7, 0, 1)[i]
                    eng.wait_ge(*freed(b))
                    for n, (s, j) in enumerate(((4, 2), (4, 3), (5, 2), (5, 3))):
                        m = transpose_to(bank[b][0:sn, P * n:P * n + P], tl(s, j, T)[:, s0:s0 + sn], hold=n == 3)
                        if n == 3:
                            m.then_inc(closing(b, "scalar"), 1)
                for g in range(2):
                    for i, (s0, sn) in enumerate(QT):
                        b, o = ((4, 0), (5, 0), (5, 144))[i]
                        if i < 2:
                            eng.wait_ge(*freed(b))
                        m = mm(bank[b][0:sn, o:o + T - s0], tl(8, 4 + g, T)[:, s0:s0 + sn],
                               tl(2, 5, T)[:, s0:T], True, True, hold=i != 1)
                        if i != 1:
                            m.then_inc(closing(b, "vector"), 1)
                def decays(h):
                    cum = arena[0:12, 9, 5]
                    for i, (s0, sn) in enumerate(QT):
                        b, o = ((2 * (h % 2), 0), (2 * (h % 2) + 1, 0), (2 * (h % 2) + 1, 144))[i]
                        if i < 2:
                            eng.wait_ge(*freed(b))
                        mm(bank[b][0:sn, o:o + T - s0], cm("sel12", sn, P * h, 12), cum[:, s0:T], True, False)
                        m = mm(bank[b][0:sn, o:o + sn], con[0:sn, CC["ident"]:CC["ident"] + sn],
                               con[0:sn, CC["later_neg"]:CC["later_neg"] + sn], False, True, hold=i != 1)
                        if i != 1:
                            m.then_inc(told(b, "scalar"), 1)

                eng.wait_ge(*freed(0))
                eng.wait_ge(*freed(1))
                eng.wait_ge(*freed(2))
                eng.wait_ge(*freed(3))
                decays(0)
                for h in range(8):
                    if h < 7:
                        decays(h + 1)
                    eng.wait_ge(v2p, pe.nth(v2p))
                    b = 6 + h // 2 % 2
                    if h % 2 == 0:
                        eng.wait_ge(*freed(b))
                    e = h % 2
                    m = by_packed(bank[b][64 * e:64 * e + 64], lambda i, sn: XD[0:sn, i, 64 * h:64 * h + 64],
                                  PKT[:, h % 2], hold=e)
                    if e:
                        m.then_inc(closing(b, "vector"), 1)
                eng.wait_ge(a2p, pe.nth(a2p))
                eng.wait_ge(*freed(4))
                eng.wait_ge(*freed(5))
                for g in range(2):
                    for k in range(2):
                        m = mm(bank[4 + g][:, 0:T], cm("ones"), tl(2, 2 * g + k, T), k == 0, k == 1, hold=k)
                        if k:
                            m.then_inc(told(4 + g, "vector"), 1)

                def logits(h):
                    for i, (q0, qn) in enumerate(QT):
                        kn = q0 + qn
                        b, o = ((2 * (h % 2), 0), (2 * (h % 2), P), (2 * (h % 2) + 1, 0))[i]
                        dst = bank[b][0:qn, o:o + kn]
                        mm(dst, tl(7, h, T)[:, q0:kn], tl(4 if h < 4 else 5, h % 4 // 2, T)[:, 0:kn], True, False)
                        if h < 4:
                            mm(dst, cm("sel12", qn, P * (8 + h), 12), arena[0:12, 9, 6, 0:kn], False, False)
                        else:
                            mm(dst, tl(8, h - 4, T)[:, q0:kn], tl(4, 7, T)[:, 0:kn], False, False)
                        m = mm(bank[b][0:qn, o + q0:o + kn], con[0:qn, CC["ident"]:CC["ident"] + qn],
                               con[0:qn, CC["key_neg"]:CC["key_neg"] + qn], False, True, hold=i)
                        if i:
                            m.then_inc(told(b, "vector"), 1)

                for b in range(4):
                    eng.wait_ge(*freed(b))
                logits(0)
                for h in range(8):
                    if h < 7:
                        logits(h + 1)
                    eng.wait_ge(v2p, pe.nth(v2p))
                    for i, (q0, qn) in enumerate(QT):
                        for kb in range(i + 1):
                            k0, kn = QT[kb]
                            b, o = ((4, q0), (5, q0 - P), (5, 144))[kb]
                            m = transpose_to(bank[b][0:kn, o:o + qn], prob(h)[0:qn, i, k0:k0 + kn], rows=qn,
                                             hold=(i, kb) == (2, 2))
                            if (i, kb) == (2, 2):
                                m.then_inc(told(5, "scalar"), 1)
                    eng.wait_ge(a2p, pe.nth(a2p))
                    b = 6 + h // 2 % 2
                    if h % 2 == 0:
                        eng.wait_ge(*freed(b))
                    e = h % 2
                    vt = FV if h < 4 else MV
                    m = by_packed(bank[b][64 * e:64 * e + 64], lambda i, sn: vt[0:sn, i, 64 * (h % 4):64 * (h % 4) + 64],
                                  PKT[:, h % 2], hold=e)
                    if e:
                        m.then_inc(closing(b, "scalar"), 1)
                for b in (6, 7):
                    eng.wait_ge(*freed(b))
                eng.wait_ge(v2p, pe.nth(v2p))
                out_projection("mix_out", l, 8, UA, T)

            for l in range(DEPTH):
                if l == 0:
                    eng.wait_ge(meta_low, 1)
                ffn("gate1", "up1", "down1", l, T, 0)
                norm(T)
                mixer(l)
                norm(T)
                ffn("gate2", "up2", "down2", l, T, 0)
                norm(T)

        @block.scalar
        def _(eng):
            a = Counts()
            act = na.activation

            def norm(T, last=False):
                t0 = xview(T)
                for q in range(4):
                    eng.wait_ge(centered, a.nth(centered))
                    act(arena[:, 9, 2 * q:2 * q + 2, 0:T], arena[:, XAS, 2 * q:2 * q + 2, t0:t0 + T], ACT.Square).then_inc(a.sig(squared), 1)
                eng.wait_ge(var_ready, a.nth(var_ready))
                act(small[:, 1, 0:T], small[:, 0, 0:T], ACT.Sqrt).then_inc(a.sig(std_ready), 1)

            def weights_high(q):
                s = HL[q]
                eng.wait_ge(slab_loaded[s % RING], 16 * (s // RING + 1))
                if q >= HIGHS:
                    eng.wait_ge(slab_used, HL[q - HIGHS] + 1)
                act(high[:, q % HIGHS], ring[:, s % RING], ACT.Copy).then_inc(a.sig(high_ready), 1)

            def scaled(a_slab):
                at = a_slab % HIGHS
                eng.wait_ge(ada_loaded[at], 16 * (a_slab // HIGHS + 1))
                for half in range(2):
                    k = 2 * (a_slab % PIECE_SLABS) + half
                    piece = a_slab // PIECE_SLABS
                    to = ada_ring[:, at, half] if k else acc[:, piece % 2]
                    if k == 0:
                        eng.wait_ge(piece_summed, piece - 1)
                    act(to, ada_ring[:, at, half], ACT.Copy, scale=cond[:, k:k + 1]).then_inc(a.sig(ada_scaled), 1)

            def norm_out(n, T, signal=input_high_ready):
                t0 = xview(T)
                for j in range(DT):
                    if j % 2 == 0:
                        eng.wait_ge(normed, a.nth(normed))
                    if n < len(STAGES):
                        act(input_high(STAGES[n], j, T), tl(9, j, T), ACT.Identity, bias=lnc[:, n, 1, j:j + 1],
                            scale=lnc[:, n, 0, j:j + 1]).then_inc(a.sig(signal), 1)
                        continue
                    act(tl(US, j, T, t0), tl(9, j, T), ACT.Identity, bias=lnc[:, n, 1, j:j + 1],
                             scale=lnc[:, n, 0, j:j + 1]).then_inc(a.sig(signal), 1)

            def ffn(n, T):
                q0 = STAGE_AT[n]
                for f in range(FT):
                    eng.wait_ge(gate_full, a.nth(gate_full))
                    act(silu_t[:, f % 2, 0:T], bank[2 * (f % 2)][:, 0:T], ACT.Silu).then_inc(a.sig(silu_ready), 1)
                    weights_high(q0 + HIGHS + f)
                for q in range(q0 + HIGHS + FT, STAGE_AT[n + 1]):
                    weights_high(q)

            def first_highs(n):
                for q in range(HIGHS):
                    weights_high(STAGE_AT[n] + q)

            def copies(n_tiles, banks, dst, func=ACT.Copy, T=SEQ, last=None, **kw):
                for n in range(n_tiles):
                    b = banks[n % len(banks)]
                    eng.wait_ge(full_for_scalar[b], a.nth(full_for_scalar[b]))
                    act(dst(n), bank[b][:, 0:T], func, **{k: v(n) for k, v in kw.items()}).then_inc(a.sig(last if last and n == n_tiles - 1 else free["scalar"][b]), 1)

            eng.wait_ge(cond_loaded, 16)
            act(cond[:, :], cond[:, :], ACT.Silu).then_inc(a.sig(cond_ready), 1)
            eng.wait_ge(inputs_loaded, 48)
            B4 = [0, 1, 2, 3]
            copies(8, B4, lambda n: tl(4, n))
            eng.wait_ge(full_for_scalar[4], a.nth(full_for_scalar[4]))
            act(small[0:64, 0, 0:SEQ], bank[4][0:64, 0:SEQ], ACT.Tanh).then_inc(a.sig(a2p), 1)
            eng.wait_ge(full_for_scalar[5], a.nth(full_for_scalar[5]))
            act(small[64:128, 0, 0:SEQ], bank[5][64:128, 0:SEQ], ACT.Copy).then_inc(a.sig(a2p), 1)
            for n in range(8):
                for half, dst in ((0, 5), (1, 6)):
                    b = 2 * (n % 2) + half
                    eng.wait_ge(full_for_scalar[b], a.nth(full_for_scalar[b]))
                    act(tl(dst, n), bank[b][:, 0:SEQ], ACT.Sigmoid, bias=pc("a0" if half else "w0", n)).then_inc(a.sig(free["scalar"][b]), 1)
            for n in range(8):
                b = B4[n % 4]
                eng.wait_ge(full_for_scalar[b], a.nth(full_for_scalar[b]))
                act(tl(7, n), bank[b][:, 0:SEQ], ACT.Copy).then_inc(a.sig(free["scalar"][b]), 1)
                scaled(FIRST * PIECE_SLABS + n)
            copies(8, B4, lambda n: tl(8, n))
            eng.wait_ge(full_for_scalar[4], a.nth(full_for_scalar[4]))
            act(small[:, 1, 0:SEQ], bank[4][:, 0:SEQ], ACT.Sigmoid).then_inc(a.sig(a2p), 1)
            copies(8, B4, lambda n: tl(US, n, SEQ, META), last=a2v)
            eng.wait_ge(consts_loaded, 16)
            eng.wait_ge(v2a, a.nth(v2a))
            act(slot(9)[:, :, 0:SEQ], slot(2)[:, :, 0:SEQ], ACT.Square).then_inc(a.sig(a2p), 1)
            eng.wait_ge(v2a, a.nth(v2a))
            act(small[0:16, 2, 0:SEQ], small[0:16, 2, 0:SEQ], ACT.Sqrt).then_inc(a.sig(a2v), 1)
            eng.wait_ge(full_for_scalar[5], a.nth(full_for_scalar[5]))
            act(small[0:16, 1, 0:SEQ], bank[5][0:16, 0:SEQ], ACT.Copy).then_inc(a.sig(free["scalar"][5]), 1)
            eng.wait_ge(v2a, a.nth(v2a))
            act(slot(3)[:, :, 0:SEQ], slot(9)[:, :, 0:SEQ], ACT.Exp, scale=-DECAY_SCALE).then_inc(a.sig(a2v), 1)
            eng.wait_ge(v2a, a.nth(v2a))
            act(slot(5)[:, :, 0:SEQ], slot(5)[:, :, 0:SEQ], ACT.Exp, scale=-DECAY_SCALE).then_inc(a.sig(a2v), 1)
            act(slot(9)[:, :, 0:SEQ], slot(9)[:, :, 0:SEQ], ACT.Exp, scale=DECAY_SCALE).then_inc(a.sig(a2v), 1)
            for j in range(DT):
                s0 = (2 * FIRST + j) * PIECE_SLABS
                for tau in range(2):
                    b = 4 + tau
                    eng.wait_ge(full_for_scalar[b], a.nth(full_for_scalar[b]))
                    act(TOK[:, tau], bank[b][:, 0:384].rearrange("p (n f) -> p n f", n=3), ACT.Copy).then_inc(a.sig(astep), 1)
                    act(AZ[:, tau, :, 0:64], bank[b][:, 384:512].rearrange("p (n f) -> p n f", n=2), ACT.Copy).then_inc(a.sig(a2p), 1)
                scaled(s0)
                scaled(s0 + 1)
                for tau in range(2):
                    b = 4 + tau
                    eng.wait_ge(full_for_scalar[b], a.nth(full_for_scalar[b]))
                    act(AZ[:, tau, :, 64:128], bank[b][:, 0:P].rearrange("p (n f) -> p n f", n=2), ACT.Copy).then_inc(a.sig(a2p), 1)
                for tau in range(2):
                    b = 4 + tau
                    eng.wait_ge(full_for_scalar[b], a.nth(full_for_scalar[b]))
                    act(PP[:, 2 * tau:2 * tau + 2], bank[b][:, 0:256].rearrange("p (n f) -> p n f", n=2), ACT.Copy).then_inc(a.sig(a2p), 1)
                scaled(s0 + 2)
                scaled(s0 + 3)
            eng.wait_ge(full_for_scalar[4], a.nth(full_for_scalar[4]))
            act(small[0:16, 0, 0:SEQ], bank[4][0:16, 0:SEQ], ACT.Copy, scale=1.0 / 64).then_inc(a.sig(a2p), 1)
            eng.wait_ge(v2a, a.nth(v2a, 4))
            act(slot(3)[:, :, 0:SEQ], slot(5)[:, :, 0:SEQ], ACT.Square).then_inc(a.sig(a2p), 1)
            eng.wait_ge(v2a, a.nth(v2a))
            act(small[0:16, 2, 0:SEQ], small[0:16, 2, 0:SEQ], ACT.Sqrt).then_inc(a.sig(a2v), 1)
            eng.wait_ge(ada_used, ADA_SLABS)
            first_highs(0)
            norm(SEQ), norm_out(0, SEQ)
            ffn(0, SEQ)
            first_highs(1)
            norm(SEQ), norm_out(1, SEQ)
            rows8 = lambda n, T=SEQ, r=8: arena[0:r, 9, n, 0:T]
            eng.wait_ge(full_for_scalar[4], a.nth(full_for_scalar[4]))
            eng.wait_ge(v2a, a.nth(v2a))
            act(rows8(0), bank[4][0:8, 0:SEQ], ACT.Sigmoid).then_inc(a.sig(astep), 1)
            eng.wait_ge(full_for_scalar[5], a.nth(full_for_scalar[5]))
            act(rows8(1), bank[5][0:8, 0:SEQ], ACT.Identity, bias=pc("gdn_dtb", rows=8)).then_inc(a.sig(astep), 1)
            eng.wait_ge(*a.last)

            def soft(r, T, alog):
                act(rows8(2, T, r), rows8(1, T, r), ACT.Abs).then_inc(a.sig(astep), 1)
                eng.wait_ge(*a.last)
                act(cols[0:r, 48:49], pc(alog, rows=r), ACT.Exp).then_inc(a.sig(astep), 1)
                act(rows8(2, T, r), rows8(2, T, r), ACT.Exp, scale=-1.0).then_inc(a.sig(a2v), 1)

            soft(8, SEQ, "gdn_alog")
            for n in range(24):
                b = n % 4
                eng.wait_ge(v2a, a.nth(v2a))
                act(tl((2, 4, 5)[n // 8], n % 8), XX[:, b].rearrange("p a f -> p (a f)"), ACT.Silu).then_inc(a.sig(free["scalar"][b]), 1)
                if n % 2 == 0:
                    weights_high(STAGE_AT[1] + HIGHS + n // 2)
            eng.wait_ge(*a.last)
            act(slot(8)[:, :, 0:SEQ], slot(2)[:, :, 0:SEQ], ACT.Square).then_inc(a.sig(astep), 1)
            act(slot(3)[:, :, 0:SEQ], slot(4)[:, :, 0:SEQ], ACT.Square).then_inc(a.sig(a2p), 1)
            for n in range(24, 32):
                b = n % 4
                eng.wait_ge(full_for_scalar[b], a.nth(full_for_scalar[b]))
                act(tl(6, n - 24), bank[b][:, 0:SEQ], ACT.Silu).then_inc(a.sig(free["scalar"][b]), 1)
                if n % 2 == 0 and HIGHS + n // 2 < STAGE_SLABS["gdn"]:
                    weights_high(STAGE_AT[1] + HIGHS + n // 2)
            eng.wait_ge(v2a, a.nth(v2a))
            act(small[0:8, 2, 0:SEQ], small[0:8, 2, 0:SEQ], ACT.Sqrt).then_inc(a.sig(astep), 1)
            act(small[0:8, 1, 0:SEQ], small[0:8, 1, 0:SEQ], ACT.Sqrt).then_inc(a.sig(a2v), 1)
            act(rows8(5, P), rows8(4, P), ACT.Exp, scale=-1.0, bias=rows8(4)[:, P - 1:P]).then_inc(a.sig(a2p), 1)
            for hp in range(4):
                eng.wait_ge(full_for_scalar[4], a.nth(full_for_scalar[4]))
                act(EX[:, :, :], bank[4][:, :].rearrange("p (n f) -> p n f", n=2), ACT.Exp).then_inc(a.sig(a2p), 1)
                eng.wait_ge(full_for_scalar[6], a.nth(full_for_scalar[6]))
                for u in range(4):
                    c, h = u % 2, 2 * hp + u // 2
                    act(DC[:, u], bank[6][:, P * u:P * u + P], ACT.Exp, bias=cols[:, 16 + 8 * c + h:17 + 8 * c + h]).then_inc(a.sig(a2p if u == 3 else astep), 1)
                for hh in range(2):
                    h = 2 * hp + hh
                    b = (4, 6)[hh]
                    eng.wait_ge(full_for_scalar[b], a.nth(full_for_scalar[b]))
                    for n, col in enumerate((h, 8 + h, 32 + h)):
                        act(TOK[:, hh, n], bank[b][:, P * n:P * n + P], ACT.Copy, scale=cols[:, col:col + 1]).then_inc(a.sig(a2p if hh and n == 2 else a2v if not hh and n == 0 else astep), 1)
                both = lambda b: bank[b][:, 0:2 * P].rearrange("p (n f) -> p n f", n=2)
                eng.wait_ge(full_for_scalar[4], a.nth(full_for_scalar[4]))
                act(AZ[:, :, 0], both(4), ACT.Copy).then_inc(a.sig(a2p), 1)
                eng.wait_ge(full_for_scalar[5], a.nth(full_for_scalar[5]))
                act(ZZ[:, 0:4:2], both(5), ACT.Copy).then_inc(a.sig(a2p), 1)
                eng.wait_ge(full_for_scalar[7], a.nth(full_for_scalar[7]))
                act(ZZ[:, 1:4:2], both(7), ACT.Copy).then_inc(a.sig(a2p), 1)
                eng.wait_ge(full_for_scalar[4], a.nth(full_for_scalar[4]))
                act(arena[:, 7, 2 * hp:2 * hp + 2, 0:SEQ], bank[4][:, :].rearrange("p (n f) -> p n f", n=2), ACT.Copy).then_inc(a.sig(free["scalar"][4]), 1)
            eng.wait_ge(*a.last)
            act(slot(8)[:, :, 0:SEQ], slot(7)[:, :, 0:SEQ], ACT.Square).then_inc(a.sig(a2p), 1)
            eng.wait_ge(v2a, a.nth(v2a))
            act(small[0:8, 2, 0:SEQ], small[0:8, 2, 0:SEQ], ACT.Sqrt).then_inc(a.sig(a2v), 1)
            first_highs(2)
            norm(SEQ), norm_out(2, SEQ)
            ffn(2, SEQ)
            act(input_parts["ffn"][:, :, 0:META], arena[:, US, :, 0:META], ACT.Copy).then_inc(a.sig(a2g), 1)
            first_highs(3)
            norm(SEQ), norm_out(3, SEQ)

            T = TALL
            QT = ((0, 128), (128, 128), (256, 16))

            def mixer(l):
                eng.wait_ge(full_for_scalar[4], a.nth(full_for_scalar[4]))
                eng.wait_ge(v2a, a.nth(v2a))
                act(rows8(1, T, 12), bank[4][0:12, 0:T], ACT.Identity, bias=cols[0:12, 50:51], scale=cm("sign12", 1, 0, 12)).then_inc(a.sig(astep), 1)
                eng.wait_ge(*a.last)
                soft(12, T, f"alog{l}")
                for n in range(6):
                    b = n % 4
                    eng.wait_ge(v2a, a.nth(v2a))
                    act(tl(2, n, T), tl(3, 4 + b, T), ACT.Silu, bias=pc(f"conv_b{l}", n)).then_inc(a.sig(free["scalar"][b]), 1)
                    if n % 2 == 0:
                        weights_high(STAGE_AT[4 + 3 * l] + HIGHS + n // 2)
                for n in range(13):
                    b = n % 4
                    eng.wait_ge(full_for_scalar[b], a.nth(full_for_scalar[b]))
                    src = bank[b][:, 0:T]
                    if n < 4:
                        act(tl(3, n, T), src, ACT.Silu).then_inc(a.sig(free["scalar"][b]), 1)
                    elif n < 6:
                        for e in range(2):
                            act(tl(7, 2 * (n - 4) + e, T), src, ACT.Copy, scale=cm("half_fox", 1, e)).then_inc(a.sig(free["scalar"][b] if e else astep), 1)
                    elif n < 10:
                        act(tl(4, n - 6, T), src, ACT.Copy).then_inc(a.sig(free["scalar"][b]), 1)
                    else:
                        act(tl(4, n - 6, T), src, ACT.Copy).then_inc(a.sig(free["scalar"][b]), 1)
                    if n % 2 == 0 and HIGHS + (n + 6) // 2 < STAGE_SLABS["mixer"]:
                        weights_high(STAGE_AT[4 + 3 * l] + HIGHS + (n + 6) // 2)
                eng.wait_ge(*a.last)
                act(arena[:, 6, 0:3, 0:T], arena[:, 4, 4:7, 0:T], ACT.Square).then_inc(a.sig(a2p), 1)
                eng.wait_ge(v2a, a.nth(v2a))
                act(small[:, 0:2, 0:T], small[:, 0:2, 0:T], ACT.Sqrt).then_inc(a.sig(a2v), 1)
                for n in range(2):
                    eng.wait_ge(full_for_scalar[n], a.nth(full_for_scalar[n]))
                    for e in range(2):
                        act(tl(7, 4 + 2 * n + e, T), bank[n][:, 0:T], ACT.Copy, scale=cm("half_mla", 1, e)).then_inc(a.sig(free["scalar"][n] if e else astep), 1)
                for n in range(4):
                    b = (0, 1, 4, 5)[n]
                    eng.wait_ge(full_for_scalar[b], a.nth(full_for_scalar[b]))
                    act(tl(5, n, T), bank[b][:, 0:T], ACT.Copy).then_inc(a.sig(free["scalar"][b] if n < 3 else a2p), 1)
                for i, (s0, sn) in enumerate(QT):
                    b = (7, 0, 1)[i]
                    eng.wait_ge(full_for_scalar[b], a.nth(full_for_scalar[b]))
                    act(FV[0:sn, i], bank[b][0:sn, 0:256], ACT.Copy).then_inc(a.sig(astep), 1)
                    act(MV[0:sn, i], bank[b][0:sn, 256:512], ACT.Copy).then_inc(a.sig(free["scalar"][b]), 1)
                for h in range(8):
                    for i, (s0, sn) in enumerate(QT):
                        b, o = ((2 * (h % 2), 0), (2 * (h % 2) + 1, 0), (2 * (h % 2) + 1, 144))[i]
                        if i < 2:
                            eng.wait_ge(full_for_scalar[b], a.nth(full_for_scalar[b]))
                        act(PKT[0:sn, h % 2, PK[i]:PK[i] + T - s0], bank[b][0:sn, o:o + T - s0], ACT.Exp,
                                 bias=decay_col(i, h, sn)).then_inc(a.sig(a2v if i == 2 else astep), 1)
                eng.wait_ge(v2a, a.nth(v2a))
                act(arena[:, 2, 0:4, 0:T], arena[:, US, 0:4, 0:T], ACT.Square).then_inc(a.sig(a2p), 1)
                eng.wait_ge(v2a, a.nth(v2a))
                act(small[:, 0:2, 0:T], small[:, 0:2, 0:T], ACT.Sqrt).then_inc(a.sig(a2v), 1)
                def turned(h):
                    eng.wait_ge(full_for_scalar[5], a.nth(full_for_scalar[5]))
                    for i, (s0, sn) in enumerate(QT):
                        b, o = ((4, 0), (5, 0), (5, 144))[i]
                        act(PKT[0:sn, h % 2, PK[i]:PK[i] + T - s0], bank[b][0:sn, o:o + T - s0], ACT.Copy).then_inc(a.sig(a2p if i == 2 else astep), 1)
                    if h % 2:
                        b = 6 + h // 2 % 2
                        eng.wait_ge(full_for_scalar[b], a.nth(full_for_scalar[b]))
                        act(tl(US, 4 + h // 2, T), bank[b][:, 0:T], ACT.Copy).then_inc(a.sig(free["scalar"][b]), 1)

                for h in range(8):
                    for i, (q0, qn) in enumerate(QT):
                        b, o = ((2 * (h % 2), 0), (2 * (h % 2), P), (2 * (h % 2) + 1, 0))[i]
                        eng.wait_ge(v2a, a.nth(v2a))
                        act(prob(h)[0:qn, i, 0:q0 + qn], bank[b][0:qn, o:o + q0 + qn], ACT.Exp,
                                 bias=cols[0:qn, 52 + i:53 + i], accum_out=cols[0:qn, 56 + i:57 + i]).then_inc(a.sig(a2v), 1)
                    if h:
                        turned(h - 1)
                turned(7)

            for l in range(DEPTH):
                ffn(3 + 3 * l, T)
                first_highs(4 + 3 * l)
                norm(T), norm_out(4 + 3 * l, T)
                mixer(l)
                first_highs(5 + 3 * l)
                norm(T), norm_out(5 + 3 * l, T)
                ffn(5 + 3 * l, T)
                if l < DEPTH - 1:
                    first_highs(6 + 3 * l)
                norm(T)
                norm_out(6 + 3 * l, T, output_ready if l == DEPTH - 1 else input_high_ready)

        @block.vector
        def _(eng):
            v = Counts()

            def residual(T, coef=None, scale=1.0):
                t0 = xview(T)
                for j in range(DT):
                    b = 6 + j % 2
                    eng.wait_ge(full_for_vector[b], v.nth(full_for_vector[b]))
                    nv.scalar_tensor_tensor(out=tl(XAS, j, T, t0), in0=bank[b][:, 0:T],
                                                 scalar=coef(j) if coef else scale, in1=tl(XAS, j, T, t0),
                                                 op0=ALU.mult, op1=ALU.add).then_inc(v.sig(resid_ready), 1)

            def over_tiles(ap, n, T):
                return ap.unsqueeze(1).to_broadcast([P, n, T])

            def norm(n, T, done=None):
                t0 = xview(T)
                eng.wait_ge(*v.last)
                eng.wait_ge(full_for_vector[4], v.nth(full_for_vector[4]))
                for q in range(4):
                    x = arena[:, XAS, 2 * q:2 * q + 2, t0:t0 + T]
                    nv.tensor_tensor(x, x, over_tiles(bank[4][:, 0:T], 2, T), ALU.subtract).then_inc(v.sig(centered), 1)
                eng.wait_ge(full_for_vector[5], v.nth(full_for_vector[5]))
                nv.tensor_scalar(small[:, 0, 0:T], bank[5][:, 0:T], 1.0, EPS_LN, ALU.mult, ALU.add).then_inc(v.sig(var_ready), 1)
                eng.wait_ge(std_ready, v.nth(std_ready))
                nv.reciprocal(small[:, 2, 0:T], small[:, 1, 0:T]).then_inc(v.sig(vstep), 1)
                eng.wait_ge(*v.last)
                def normed_pair(q):
                    nv.tensor_tensor(arena[:, 9, 2 * q:2 * q + 2, 0:T], arena[:, XAS, 2 * q:2 * q + 2, t0:t0 + T],
                                     over_tiles(small[:, 2, 0:T], 2, T), ALU.mult).then_inc(v.sig(normed), 1)
                    return v.last

                if n == len(STAGES):
                    for q in range(4):
                        normed_pair(q)
                    return
                after = normed_pair(0)
                for q in range(4):
                    before, after = after, normed_pair(q + 1) if q < 3 else None
                    eng.wait_ge(*before)
                    for j in (2 * q, 2 * q + 1):
                        nv.tensor_scalar(tl(US, j, T, t0), tl(9, j, T), lnc[:, n, 0, j:j + 1], lnc[:, n, 1, j:j + 1],
                                         ALU.mult, ALU.add).then_inc(v.sig(input_whole), 1)
                for j in range(DT):
                    nv.tensor_scalar(tl(XAS, j, T, t0), tl(9, j, T), lnc[:, n, 2, j:j + 1], lnc[:, n, 3, j:j + 1],
                                          ALU.mult, ALU.add).then_inc(v.sig((done or vstep) if j == DT - 1 else vstep), 1)

            def weights_low(q):
                eng.wait_ge(high_ready, q + 1)
                nv.tensor_tensor(ring_low[:, HL[q] % RING], ring[:, HL[q] % RING], high[:, q % HIGHS].bitcast(F32),
                                 ALU.subtract).then_inc(low_by_vector, 1)

            def ffn(n, T):
                q0 = STAGE_AT[n]
                for f in range(FT):
                    eng.wait_ge(silu_ready, v.nth(silu_ready))
                    eng.wait_ge(up_full, v.nth(up_full))
                    nv.tensor_tensor(tl(6 + f // DT, f % DT, T), silu_t[:, f % 2, 0:T], bank[2 * (f % 2) + 1][:, 0:T], ALU.mult).then_inc(v.sig(vstep), 1)
                    nv.tensor_tensor(hidden_high(f, T), silu_t[:, f % 2, 0:T], bank[2 * (f % 2) + 1][:, 0:T], ALU.mult).then_inc(v.sig(hidden_ready), 1)
                    weights_low(q0 + HIGHS + f)

            def inverse(levels):
                for l in range(1, levels):
                    for p in range(2):
                        eng.wait_ge(full_for_vector[p], v.nth(full_for_vector[p]))
                        nv.tensor_tensor(ZZ[:, 2 * p:2 * p + 2], bank[p][:, 0:256].rearrange("p (n f) -> p n f", n=2),
                                              over_tiles(cm(f"level{l}"), 2, P), ALU.mult).then_inc(v.sig(v2p), 1)
                    for p in range(2):
                        eng.wait_ge(full_for_vector[2 + p], v.nth(full_for_vector[2 + p]))
                        first = 0 if l < levels - 1 else 1
                        x = XX[:, 2 * p:2 * p + 2, first:2]
                        y = bank[2 + p][:, 0:512].rearrange("p (a b f) -> p a b f", a=2, b=2)[:, :, first:2]
                        nv.tensor_tensor(x, x, y, ALU.add).then_inc(v.sig(v2p), 1)

            def modulation(n, b):
                i, q = PIECES[n]
                at = slice(8 * q, 8 * q + 8)
                eng.wait_ge(piece_summed, n + 1)
                nv.tensor_tensor(mods[:, i, at], bank[b][:, 0:DT], pc(f"ada_b{i}", 8 * q, width=DT), ALU.add).then_inc(v.sig(free["vector"][b]), 1)
                eng.wait_ge(*v.last)
                nv.tensor_scalar(mod1[:, i, at], mods[:, i, at], 1.0, None, ALU.add).then_inc(v.sig(vstep), 1)

            def gain_and_bias(n):
                i, s = (n // 2, n % 2) if n < 4 else ((n - 4) // 3, (n - 4) % 3 + 1)
                g, b = (f"ln_g{i}{s}", f"ln_b{i}{s}") if n < 4 else (f"ln{s}_g{i}", f"ln{s}_b{i}")
                return pc(g, width=DT), pc(b, width=DT)

            nv.memset(one[:, :], 1.0).then_inc(v.sig(vstep), 1)
            eng.wait_ge(cond_ready, v.nth(cond_ready))
            for n in range(FIRST):
                for k in range(DT):
                    a = PIECE_SLABS * n + k // 2
                    w_k = ada_ring[:, a % HIGHS, k % 2]
                    if k % 2 == 0:
                        eng.wait_ge(ada_loaded[a % HIGHS], 16 * (a // HIGHS + 1))
                    if k == 0:
                        nv.tensor_scalar(acc[:, n], w_k, cond[:, 0:1], None, ALU.mult).then_inc(v.sig(vstep), 1)
                    else:
                        eng.wait_ge(*v.last)
                        nv.scalar_tensor_tensor(out=acc[:, n], in0=w_k, scalar=cond[:, k:k + 1], in1=acc[:, n],
                                                op0=ALU.mult, op1=ALU.add).then_inc(v.sig(ada_used if k % 2 else vstep), 1)
                eng.wait_ge(*v.last)
                nv.tensor_copy(acc[:, n, 0:1], acc[:, n, 0:1]).then_inc(v.sig(first_piece), 1)
            eng.wait_ge(inputs_loaded, 48)
            for n in range(10):
                g, b = gain_and_bias(n)
                nv.tensor_scalar(lnc[:, n, 2], g, ALPHA, None, ALU.mult).then_inc(v.sig(vstep), 1)
                nv.tensor_scalar(lnc[:, n, 3], b, ALPHA, None, ALU.mult).then_inc(v.sig(vstep), 1)
                if n > 2:
                    nv.tensor_copy(lnc[:, n, 0], g).then_inc(v.sig(vstep), 1)
                    nv.tensor_copy(lnc[:, n, 1], b).then_inc(v.sig(vstep), 1)
            for n in range(FIRST):
                modulation(n, n)
            eng.wait_ge(*v.last)
            for j in range(DT):
                nv.tensor_scalar(tl(US, j, SEQ, META), tl(XAS, j, SEQ, META), mod1[:, 0, 8 + j:9 + j],
                                      mods[:, 0, j:j + 1], ALU.mult, ALU.add).then_inc(v.sig(vstep), 1)
            eng.wait_ge(*v.last)

            u = arena[:, US, :, META:TALL]
            nv.tensor_tensor(slot(9)[:, :, 1:SEQ], u[:, :, 0:SEQ - 1], u[:, :, 1:SEQ], ALU.subtract).then_inc(v.sig(vstep), 1)
            nv.tensor_scalar(slot(9)[:, :, 0:1], u[:, :, 0:1], -1.0, None, ALU.mult).then_inc(v.sig(vstep), 1)
            eng.wait_ge(*v.last)

            def lerp(i, s):
                for j in range(DT):
                    nv.scalar_tensor_tensor(out=tl(s, j), in0=tl(9, j), scalar=pc("mu", 8 * i + j),
                                                 in1=tl(US, j, SEQ, META), op0=ALU.mult, op1=ALU.add).then_inc(v.sig(lerp_ready), 1)

            lerp(1, 2)
            lerp(3, 3)
            x = arena[:, XAS, :, META:TALL]
            nv.tensor_scalar(x, x, ALPHA, None, ALU.mult).then_inc(v.sig(vstep), 1)
            nv.tensor_scalar(arena[:, XAS, :, 0:META], arena[:, US, :, 0:META], ALPHA, None, ALU.mult).then_inc(v.sig(vstep), 1)
            eng.wait_ge(lerp_used, v.nth(lerp_used))
            lerp(4, 2)
            eng.wait_ge(lerp_used, v.nth(lerp_used))
            lerp(0, 3)
            eng.wait_ge(lerp_used, v.nth(lerp_used))
            lerp(2, 2)
            eng.wait_ge(lerp_used, v.nth(lerp_used))
            lerp(5, 3)
            nv.tensor_scalar(cols[:, 8:16], par[:, PC["k_a"]:PC["k_a"] + 8], -1.0, 1.0, ALU.mult, ALU.add).then_inc(v.sig(vstep), 1)
            eng.wait_ge(*v.last)
            eng.wait_ge(consts_loaded, 16)
            eng.wait_ge(a2v, v.nth(a2v))
            S = lambda i: slot(i)[:, :, 0:SEQ]
            for j in range(DT):
                nv.tensor_scalar(tl(2, j), tl(4, j), pc("k_k", j), None, ALU.mult).then_inc(v.sig(v2a if j == 7 else vstep), 1)
            for j in range(DT):
                nv.tensor_scalar(tl(3, j), tl(6, j), pc("k_a", j), cols[:, 8 + j:9 + j], ALU.mult, ALU.add).then_inc(v.sig(vstep), 1)
            eng.wait_ge(*v.last)
            nv.tensor_tensor(S(4), S(4), S(3), ALU.mult).then_inc(v.sig(vstep), 1)
            eng.wait_ge(*v.last)
            for j in range(DT):
                nv.scalar_tensor_tensor(out=tl(3, j), in0=tl(7, j), scalar=pc("r_k", j), in1=tl(4, j),
                                             op0=ALU.mult, op1=ALU.mult).then_inc(v.sig(v2p if j == 7 else vstep), 1)
            eng.wait_ge(full_for_vector[4], v.nth(full_for_vector[4]))
            nv.tensor_scalar(small[0:16, 2, 0:SEQ], bank[4][0:16, 0:SEQ], 1.0, 1e-6, ALU.mult, ALU.add).then_inc(v.sig(v2a), 1)
            eng.wait_ge(a2v, v.nth(a2v))
            nv.reciprocal(small[0:16, 2, 0:SEQ], small[0:16, 2, 0:SEQ]).then_inc(v.sig(v2p), 1)

            def two(s, q, T=SEQ):
                return arena[:, s, 2 * q:2 * q + 2, 0:T]

            def pair(b, w_=512):
                return bank[b][:, 0:w_].rearrange("p (n f) -> p n f", n=2)

            for j in range(DT):
                nv.tensor_tensor_scan(tl(9, j), cm("reset64", SEQ), tl(5, j), 0.0, ALU.mult, ALU.add).then_inc(v.sig(v2a if j == 7 else vstep), 1)
            for q in range(4):
                eng.wait_ge(full_for_vector[q], v.nth(full_for_vector[q]))
                nv.tensor_tensor(two(2, q), two(2, q), pair(q), ALU.mult).then_inc(v.sig(free["vector"][q]), 1)
            eng.wait_ge(*v.last)
            nv.tensor_tensor(S(5), S(9), S(5), ALU.subtract).then_inc(v.sig(v2a), 1)
            eng.wait_ge(a2v, v.nth(a2v))
            nv.tensor_tensor(S(7), S(7), S(3), ALU.mult).then_inc(v.sig(vstep), 1)
            nv.tensor_copy(WL, slot(3)[:, :, 63:SEQ:64]).then_inc(v.sig(vstep), 1)
            eng.wait_ge(a2v, v.nth(a2v))
            nv.scalar_tensor_tensor(out=S(5), in0=S(2), scalar=-1.0, in1=S(5), op0=ALU.mult, op1=ALU.mult).then_inc(v.sig(vstep), 1)
            nv.tensor_tensor(S(2), S(2), S(6), ALU.mult).then_inc(v.sig(vstep), 1)
            eng.wait_ge(*v.last)
            eng.wait_ge(a2v, v.nth(a2v))
            nv.tensor_tensor(S(6), S(2), S(9), ALU.mult).then_inc(v.sig(vstep), 1)
            nv.tensor_tensor(S(4), S(4), S(9), ALU.mult).then_inc(v.sig(v2p), 1)
            eng.wait_ge(*v.last)
            nv.memset(S(9), 0.0).then_inc(v.sig(vstep), 1)
            for j in range(DT):
                if j == 0:
                    modulation(FIRST, 0)
                for u in range(4):
                    b = 6 + u % 2
                    eng.wait_ge(full_for_vector[b], v.nth(full_for_vector[b]))
                    nv.tensor_tensor(GM[:, u].rearrange("p (n f) -> p n f", n=2), pair(b),
                                          over_tiles(cm("strict64", 256), 2, 256), ALU.mult).then_inc(v.sig(free["vector"][b]), 1)
                eng.wait_ge(*v.last)
                nv.tensor_tensor(XX[:, :, 1], GM[:, :, 0:P], over_tiles(cm("level0T"), 4, P), ALU.mult).then_inc(v.sig(vstep), 1)
                eng.wait_ge(*v.last)
                for p in range(2):
                    x = XX[:, 2 * p:2 * p + 2, 1]
                    nv.tensor_tensor(x, x, over_tiles(ident, 2, P), ALU.add).then_inc(v.sig(v2p), 1)
                for p in range(2):
                    eng.wait_ge(full_for_vector[2 + p], v.nth(full_for_vector[2 + p]))
                    nv.tensor_copy(XX[:, 2 * p:2 * p + 2, 0], pair(2 + p, 256)).then_inc(v.sig(v2p), 1)
                inverse(6)
                modulation(FIRST + 1 + j, 0)
                for tau in range(2):
                    eng.wait_ge(full_for_vector[tau], v.nth(full_for_vector[tau]))
                    nv.tensor_tensor(tl(7, j)[:, P * tau:P * tau + P], tl(7, j)[:, P * tau:P * tau + P],
                                          bank[tau][:, 0:P], ALU.add).then_inc(v.sig(vstep), 1)
                    nv.tensor_copy(tl(5, j)[:, P * tau:P * tau + P], bank[tau][:, P:2 * P]).then_inc(v.sig(free["vector"][tau]), 1)
                    for cc in range(2):
                        c = 2 * tau + cc
                        if c == 3:
                            continue
                        b = (2, 3, 6)[c]
                        eng.wait_ge(full_for_vector[b], v.nth(full_for_vector[b]))
                        if c:
                            for e in range(2):
                                o = slice(64 * e, 64 * e + 64)
                                nv.tensor_tensor(arena[o, 9, j, P * (c - 1) + 64 * e:P * (c - 1) + 64 * e + 64],
                                                      bank[b][o, 64:128], con[o, CC["ident"] + 64 * e:CC["ident"] + 64 * e + 64],
                                                      ALU.add).then_inc(v.sig(vstep), 1)
                        nv.tensor_copy(arena[:, 2, j, 64 * c:64 * c + 64], bank[b][:, 0:64]).then_inc(v.sig(free["vector"][b]), 1)
            eng.wait_ge(*v.last)
            for n, l, q in ((0, 0, 3), (1, 1, 0), (2, 1, 3)):
                g, b = gain_and_bias(n)
                shift, scale = mods[:, l, 8 * q:8 * q + 8], mod1[:, l, 8 * q + 8:8 * q + 16]
                nv.tensor_tensor(lnc[:, n, 0], g, scale, ALU.mult).then_inc(v.sig(vstep), 1)
                nv.tensor_tensor(lnc[:, n, 1], b, scale, ALU.mult).then_inc(v.sig(vstep), 1)
                eng.wait_ge(*v.last)
                nv.tensor_tensor(lnc[:, n, 1], lnc[:, n, 1], shift, ALU.add).then_inc(v.sig(vstep), 1)
            eng.wait_ge(*v.last)
            for s in (3, 4, 6):
                nv.memset(arena[:, s, :, 0:P], 0.0).then_inc(v.sig(vstep), 1)
            H = lambda c: arena[:, 2, :, 64 * c:64 * c + 64]
            state = arena[:, 2, :, 192:256]
            wl = lambda c: WL[:, :, c:c + 1].to_broadcast([P, DT, 64])
            eng.wait_ge(*v.last)
            for c in range(3):
                if c == 0:
                    nv.tensor_tensor(state, H(0), wl(0), ALU.mult).then_inc(v.sig(v2p), 1)
                else:
                    eng.wait_ge(full_for_vector[c], v.nth(full_for_vector[c]))
                    nv.tensor_tensor(H(c), H(c), bank[c][:, :].rearrange("p (n f) -> p n f", n=DT), ALU.add).then_inc(v.sig(free["vector"][c]), 1)
                    eng.wait_ge(*v.last)
                    nv.tensor_tensor(state, H(c), wl(c), ALU.mult).then_inc(v.sig(v2p if c == 1 else vstep), 1)
                eng.wait_ge(*v.last)
                for e in range(2):
                    o = slice(64 * e, 64 * e + 64)
                    nv.tensor_copy(arena[o, (3, 4, 6)[c], :, 64 * e:64 * e + 64], arena[o, 2, :, 192:256]).then_inc(v.sig(v2p if c == 2 and e else vstep), 1)
            for j in range(DT):
                b = j % 4
                eng.wait_ge(full_for_vector[b], v.nth(full_for_vector[b]))
                nv.tensor_tensor(tl(5, j)[:, 64:256], tl(5, j)[:, 64:256], bank[b][:, 64:256], ALU.add).then_inc(v.sig(v2p), 1)
            eng.wait_ge(*v.last)
            for q in range(4):
                eng.wait_ge(full_for_vector[q], v.nth(full_for_vector[q]))
                nv.tensor_tensor(two(5, q), two(5, q), pair(q), ALU.subtract).then_inc(v.sig(v2a), 1)
            eng.wait_ge(full_for_vector[5], v.nth(full_for_vector[5]))
            nv.tensor_scalar(small[0:16, 2, 0:SEQ], bank[5][0:16, 0:SEQ], 1.0 / 64, 64e-5, ALU.mult, ALU.add).then_inc(v.sig(v2a), 1)
            eng.wait_ge(a2v, v.nth(a2v))
            nv.reciprocal(small[0:16, 2, 0:SEQ], small[0:16, 2, 0:SEQ]).then_inc(v.sig(v2p), 1)
            for q in range(4):
                eng.wait_ge(full_for_vector[q], v.nth(full_for_vector[q]))
                nv.tensor_tensor(two(5, q), two(5, q), pair(q), ALU.mult).then_inc(v.sig(free["vector"][q]), 1)
            eng.wait_ge(*v.last)
            for j in range(DT):
                nv.tensor_scalar(tl(5, j), tl(5, j), pc("gn_g", j), pc("gn_b", j), ALU.mult, ALU.add).then_inc(v.sig(vstep), 1)
            for q in range(4):
                eng.wait_ge(full_for_vector[q], v.nth(full_for_vector[q]))
                nv.tensor_tensor(two(3, q), two(8, q), pair(q), ALU.mult).then_inc(v.sig(free["vector"][q]), 1)
            eng.wait_ge(*v.last)
            nv.tensor_tensor(S(5), S(5), S(3), ALU.add).then_inc(v.sig(vstep), 1)
            eng.wait_ge(*v.last)
            nv.tensor_tensor(S(5), S(5), arena[:, US, :, META:TALL], ALU.mult).then_inc(v.sig(v2p), 1)
            modulation(len(PIECES) - 1, 0)
            residual(SEQ, lambda j: mod1[:, 0, 16 + j:17 + j])
            norm(0, SEQ)
            ffn(0, SEQ)
            residual(SEQ, lambda j: mod1[:, 0, 40 + j:41 + j])
            norm(1, SEQ, v2a)
            def softplus(r, T):
                R = lambda n: arena[0:r, 9, n, 0:T]
                eng.wait_ge(a2v, v.nth(a2v))
                nv.tensor_scalar(R(3), R(2), 2.0, None, ALU.add).then_inc(v.sig(vstep), 1)
                eng.wait_ge(*v.last)
                nv.reciprocal(R(3), R(3)).then_inc(v.sig(vstep), 1)
                eng.wait_ge(*v.last)
                nv.tensor_tensor(R(3), R(2), R(3), ALU.mult).then_inc(v.sig(vstep), 1)
                eng.wait_ge(*v.last)
                nv.tensor_tensor(R(6), R(3), R(3), ALU.mult).then_inc(v.sig(vstep), 1)
                eng.wait_ge(*v.last)
                nv.tensor_scalar(R(7), R(6), 1.0 / 15, None, ALU.mult).then_inc(v.sig(vstep), 1)
                for n in (13, 11, 9, 7, 5, 3, 1):
                    eng.wait_ge(*v.last)
                    nv.scalar_tensor_tensor(out=R(7), in0=R(7), scalar=1.0 / n, in1=R(6 if n > 1 else 3),
                                                 op0=ALU.add, op1=ALU.mult).then_inc(v.sig(vstep), 1)
                nv.tensor_scalar(R(2), R(1), 0.0, None, ALU.max).then_inc(v.sig(vstep), 1)
                eng.wait_ge(*v.last)
                nv.scalar_tensor_tensor(out=R(7), in0=R(7), scalar=2.0, in1=R(2), op0=ALU.mult, op1=ALU.add).then_inc(v.sig(vstep), 1)
                eng.wait_ge(*v.last)

            def convolve(n, b, dst, T, weights, stride):
                eng.wait_ge(full_for_vector[b], v.nth(full_for_vector[b]))
                tap = lambda t: pc(weights, stride * t + n)
                nv.tensor_scalar(dst, bank[b][:, 0:T], tap(3), None, ALU.mult).then_inc(v.sig(vstep), 1)
                for s in (1, 2, 3):
                    eng.wait_ge(*v.last)
                    nv.scalar_tensor_tensor(out=dst[:, s:T], in0=bank[b][:, 0:T - s], scalar=tap(3 - s),
                                                 in1=dst[:, s:T], op0=ALU.mult, op1=ALU.add).then_inc(v.sig(v2a if s == 3 else vstep), 1)

            def decay_rows():
                softplus(8, SEQ)
                R = lambda n: arena[0:8, 9, n, 0:SEQ]
                nv.tensor_scalar(R(6), R(7), cols[0:8, 48:49], -1.0, ALU.mult, ALU.mult).then_inc(v.sig(vstep), 1)
                eng.wait_ge(*v.last)
                for c in range(2):
                    cs = slice(P * c, P * c + P)
                    nv.tensor_tensor_scan(R(4)[:, cs], cm("ones", P, 0, 8), R(6)[:, cs], 0.0, ALU.mult, ALU.add).then_inc(v.sig(vstep), 1)

            for n in range(24):
                convolve(n, n % 4, XX[:, n % 4].rearrange("p a f -> p (a f)"), SEQ, "gdn_conv", 24)
                if n == 3:
                    decay_rows()
            eng.wait_ge(full_for_vector[4], v.nth(full_for_vector[4]))
            nv.tensor_scalar(small[0:8, 2, 0:SEQ], bank[4][0:8, 0:SEQ], 1.0, 1e-6, ALU.mult, ALU.add).then_inc(v.sig(vstep), 1)
            eng.wait_ge(full_for_vector[5], v.nth(full_for_vector[5]))
            nv.tensor_scalar(small[0:8, 1, 0:SEQ], bank[5][0:8, 0:SEQ], 1.0, 1e-6, ALU.mult, ALU.add).then_inc(v.sig(v2a), 1)
            eng.wait_ge(a2v, v.nth(a2v))
            nv.reciprocal(small[0:8, 2, 0:SEQ], small[0:8, 2, 0:SEQ]).then_inc(v.sig(vstep), 1)
            eng.wait_ge(*v.last)
            nv.tensor_scalar(small[0:8, 2, 0:SEQ], small[0:8, 2, 0:SEQ], P ** -0.5, None, ALU.mult).then_inc(v.sig(vstep), 1)
            nv.reciprocal(small[0:8, 1, 0:SEQ], small[0:8, 1, 0:SEQ]).then_inc(v.sig(v2p), 1)
            for s in (2, 4):
                for q in range(4):
                    eng.wait_ge(full_for_vector[q], v.nth(full_for_vector[q]))
                    nv.tensor_tensor(two(s, q), two(s, q), pair(q), ALU.mult).then_inc(v.sig(free["vector"][q]), 1)
            eng.wait_ge(full_for_vector[4], v.nth(full_for_vector[4]))
            nv.tensor_copy(cols[:, 0:16], bank[4][:, 0:16]).then_inc(v.sig(vstep), 1)
            nv.tensor_scalar(cols[:, 16:32], bank[4][:, 16:32], -1.0, None, ALU.mult).then_inc(v.sig(vstep), 1)
            nv.tensor_copy(cols[:, 32:40], bank[4][:, 32:40]).then_inc(v.sig(v2p), 1)
            for hp in range(4):
                eng.wait_ge(full_for_vector[5], v.nth(full_for_vector[5]))
                nv.tensor_tensor(KB, arena[:, 4, 2 * hp:2 * hp + 2, 0:SEQ], pair(5), ALU.mult).then_inc(v.sig(v2p), 1)
                eng.wait_ge(a2v, v.nth(a2v))
                nv.tensor_tensor(PP[:, 0:2], arena[:, 2, 2 * hp:2 * hp + 2, P:SEQ], EX[:, :, P:SEQ], ALU.mult).then_inc(v.sig(vstep), 1)
                eng.wait_ge(*v.last)
                nv.tensor_tensor(PP[:, 2:4], KB[:, :, P:SEQ], EX[:, :, P:SEQ], ALU.mult).then_inc(v.sig(vstep), 1)
                nv.tensor_tensor(DS, DC, over_tiles(cm("nstrict"), 4, P), ALU.mult).then_inc(v.sig(vstep), 1)
                eng.wait_ge(*v.last)
                for hh in range(2):
                    b = (7, 5)[hh]
                    eng.wait_ge(full_for_vector[b], v.nth(full_for_vector[b]))
                    g = bank[b][:, :].rearrange("p (n f) -> p n f", n=2)
                    us = slice(2 * hh, 2 * hh + 2)
                    nv.tensor_tensor(GM[:, us, 0:P], g[:, :, 0:P], DS[:, us], ALU.mult).then_inc(v.sig(vstep), 1)
                    nv.tensor_tensor(GM[:, us, P:2 * P], g[:, :, P:2 * P], DC[:, us], ALU.mult).then_inc(v.sig(vstep), 1)
                eng.wait_ge(*v.last)
                nv.tensor_tensor(XX[:, :, 1], GM[:, :, 0:P], over_tiles(cm("level0T"), 4, P), ALU.mult).then_inc(v.sig(vstep), 1)
                eng.wait_ge(*v.last)
                for p in range(2):
                    x = XX[:, 2 * p:2 * p + 2, 1]
                    nv.tensor_tensor(x, x, over_tiles(ident, 2, P), ALU.add).then_inc(v.sig(v2p), 1)
                for p in range(2):
                    eng.wait_ge(full_for_vector[2 + p], v.nth(full_for_vector[2 + p]))
                    nv.tensor_copy(XX[:, 2 * p:2 * p + 2, 0], pair(2 + p, 256)).then_inc(v.sig(v2p), 1)
                inverse(7)
                eng.wait_ge(full_for_vector[6], v.nth(full_for_vector[6]))
                nv.tensor_tensor(AZ[:, :, 1], TOK[:, :, 1], pair(6, 256), ALU.subtract).then_inc(v.sig(v2p), 1)
            eng.wait_ge(full_for_vector[5], v.nth(full_for_vector[5]))
            nv.tensor_scalar(small[0:8, 2, 0:SEQ], bank[5][0:8, 0:SEQ], 1.0 / P, 1e-6, ALU.mult, ALU.add).then_inc(v.sig(v2a), 1)
            eng.wait_ge(a2v, v.nth(a2v))
            nv.reciprocal(small[0:8, 2, 0:SEQ], small[0:8, 2, 0:SEQ]).then_inc(v.sig(v2p), 1)
            for q in range(4):
                eng.wait_ge(full_for_vector[q], v.nth(full_for_vector[q]))
                nv.tensor_tensor(two(7, q), two(7, q), pair(q), ALU.mult).then_inc(v.sig(free["vector"][q]), 1)
            eng.wait_ge(*v.last)
            nv.scalar_tensor_tensor(out=S(7), in0=S(7), scalar=pc("gdn_norm"), in1=S(6), op0=ALU.mult, op1=ALU.mult).then_inc(v.sig(v2p), 1)
            residual(SEQ, lambda j: mod1[:, 1, 16 + j:17 + j])
            norm(2, SEQ)
            ffn(2, SEQ)
            residual(SEQ, lambda j: mod1[:, 1, 40 + j:41 + j])
            norm(3, SEQ)

            T = TALL
            QT = ((0, 128), (128, 128), (256, 16))

            def mixer(l):
                eng.wait_ge(*v.last)
                nv.tensor_tensor(cols[0:12, 50:51], pc(f"dtb{l}", rows=12), cm("sign12", 1, 0, 12), ALU.mult).then_inc(v.sig(v2a), 1)
                R = lambda n: arena[0:12, 9, n, 0:T]
                for n in range(6):
                    convolve(n, n % 4, tl(3, 4 + n % 4, T), T, f"conv_w{l}", 6)
                    if n == 5:
                        softplus(12, T)
                        nv.tensor_copy(R(4), R(7)).then_inc(v.sig(vstep), 1)
                        nv.tensor_scalar(R(6), R(7), cols[0:12, 48:49], -1.0, ALU.mult, ALU.mult).then_inc(v.sig(vstep), 1)
                        eng.wait_ge(*v.last)
                        nv.tensor_tensor_scan(R(5), cm("ones", 1, 0, 12).to_broadcast([12, T]), R(6), 0.0,
                                                   ALU.mult, ALU.add).then_inc(v.sig(vstep), 1)
                        eng.wait_ge(*v.last)
                        nv.tensor_scalar(R(6), R(5), -1.0, None, ALU.mult).then_inc(v.sig(vstep), 1)
                eng.wait_ge(full_for_vector[6], v.nth(full_for_vector[6]))
                nv.tensor_tensor(tl(4, 7, T), bank[6][:, 0:T], cm("cos", T), ALU.mult).then_inc(v.sig(free["vector"][6]), 1)
                cosines = v.last
                eng.wait_ge(full_for_vector[4], v.nth(full_for_vector[4]))
                nv.tensor_scalar(small[:, 0, 0:T], bank[4][:, 0:T], 1.0 / 256, EPS_LN, ALU.mult, ALU.add).then_inc(v.sig(vstep), 1)
                eng.wait_ge(full_for_vector[5], v.nth(full_for_vector[5]))
                nv.tensor_scalar(small[:, 1, 0:T], bank[5][:, 0:T], 1.0 / 128, EPS_LN, ALU.mult, ALU.add).then_inc(v.sig(v2a), 1)
                eng.wait_ge(a2v, v.nth(a2v))
                nv.reciprocal(small[:, 0:2, 0:T], small[:, 0:2, 0:T]).then_inc(v.sig(vstep), 1)
                eng.wait_ge(*v.last)
                for k in range(3):
                    nv.scalar_tensor_tensor(out=tl(4, 4 + k, T), in0=tl(4, 4 + k, T),
                                                 scalar=pc(f"mlaq{l}", k) if k < 2 else pc(f"mlakv{l}"),
                                                 in1=small[:, k // 2, 0:T], op0=ALU.mult, op1=ALU.mult).then_inc(v.sig(v2p if k == 2 else vstep), 1)
                eng.wait_ge(full_for_vector[7], v.nth(full_for_vector[7]))
                nv.tensor_tensor(tl(8, 6, T), bank[7][:, 0:T], cm("sin", T), ALU.mult).then_inc(v.sig(free["vector"][7]), 1)
                eng.wait_ge(*v.last)
                eng.wait_ge(*cosines)
                nv.tensor_tensor(tl(4, 7, T), tl(4, 7, T), tl(8, 6, T), ALU.add).then_inc(v.sig(v2p), 1)
                eng.wait_ge(*v.last)
                eng.wait_ge(full_for_vector[2], v.nth(full_for_vector[2]))
                nv.tensor_tensor(tl(8, 6, T), bank[2][:, 0:T], cm("cos", T), ALU.mult).then_inc(v.sig(free["vector"][2]), 1)
                eng.wait_ge(full_for_vector[3], v.nth(full_for_vector[3]))
                nv.tensor_tensor(tl(8, 7, T), bank[3][:, 0:T], cm("sin", T), ALU.mult).then_inc(v.sig(free["vector"][3]), 1)
                eng.wait_ge(*v.last)
                nv.tensor_tensor(tl(8, 6, T), tl(8, 6, T), tl(8, 7, T), ALU.add).then_inc(v.sig(vstep), 1)
                for g in range(2):
                    nv.tensor_scalar(tl(8, 4 + g, T), tl(2, 4, T), cm("half", 1, g), None, ALU.mult).then_inc(v.sig(vstep), 1)
                eng.wait_ge(*v.last)
                for h in range(4):
                    nv.tensor_scalar(tl(8, h, T), tl(8, 6, T), cm("quarter_mla", 1, h), None, ALU.mult).then_inc(v.sig(vstep), 1)
                eng.wait_ge(full_for_vector[6], v.nth(full_for_vector[6]))
                for i, (s0, sn) in enumerate(QT):
                    nv.tensor_copy(TC[0:sn, i, 0:12], bank[6][0:sn, 24 * i:24 * i + 12]).then_inc(v.sig(vstep), 1)
                    nv.tensor_scalar(TC[0:sn, i, 12:24], bank[6][0:sn, 24 * i + 12:24 * i + 24], -1.0, None, ALU.mult).then_inc(v.sig(v2p if i == 2 else vstep), 1)
                eng.wait_ge(*v.last)
                for i, (s0, sn) in enumerate(QT):
                    b = (2, 3, 6)[i]
                    eng.wait_ge(full_for_vector[b], v.nth(full_for_vector[b]))
                    nv.tensor_tensor(XD[0:sn, i].rearrange("p (h f) -> p h f", h=8),
                                          bank[b][0:sn, :].rearrange("p (h f) -> p h f", h=8),
                                          TC[0:sn, i, 0:8].unsqueeze(2).to_broadcast([sn, 8, 64]), ALU.mult).then_inc(v.sig(free["vector"][b]), 1)
                for g in range(2):
                    for i, (s0, sn) in enumerate(QT):
                        b, o = ((4, 0), (5, 0), (5, 144))[i]
                        if i < 2:
                            eng.wait_ge(full_for_vector[b], v.nth(full_for_vector[b]))
                        nv.tensor_copy(CB[0:sn, g, PK[i]:PK[i] + T - s0], bank[b][0:sn, o:o + T - s0]).then_inc(v.sig(free["vector"][b] if i != 1 else vstep), 1)
                eng.wait_ge(*v.last)
                for h in range(8):
                    eng.wait_ge(a2v, v.nth(a2v))
                    for i, (s0, sn) in enumerate(QT):
                        x = PKT[0:sn, h % 2, PK[i]:PK[i] + T - s0]
                        nv.tensor_tensor(x, x, CB[0:sn, h // 4, PK[i]:PK[i] + T - s0], ALU.mult).then_inc(v.sig(v2p if i == 2 else vstep), 1)
                    if h > 1 and h % 2 == 0:
                        ssd_out(l, h // 2 - 1)
                ssd_out(l, 3)
                for g in range(2):
                    eng.wait_ge(full_for_vector[4 + g], v.nth(full_for_vector[4 + g]))
                    nv.tensor_scalar(small[:, g, 0:T], bank[4 + g][:, 0:T], 1.0 / 256, EPS_LN, ALU.mult, ALU.add).then_inc(v.sig(v2a if g else vstep), 1)
                eng.wait_ge(a2v, v.nth(a2v))
                nv.reciprocal(small[:, 0:2, 0:T], small[:, 0:2, 0:T]).then_inc(v.sig(vstep), 1)
                eng.wait_ge(*v.last)
                for j in range(4):
                    nv.scalar_tensor_tensor(out=tl(US, j, T), in0=tl(US, j, T), scalar=pc(f"ssd_g{l}", j),
                                                 in1=small[:, j // 2, 0:T], op0=ALU.mult, op1=ALU.mult).then_inc(v.sig(vstep), 1)

                def finish(h):
                    eng.wait_ge(a2v, v.nth(a2v, 3))
                    nv.reciprocal(cols[:, 56:58], cols[:, 56:58]).then_inc(v.sig(vstep), 1)
                    nv.reciprocal(cols[0:16, 58:59], cols[0:16, 58:59]).then_inc(v.sig(vstep), 1)
                    eng.wait_ge(*v.last)
                    for i, (q0, qn) in enumerate(QT):
                        x = prob(h)[0:qn, i, 0:q0 + qn]
                        nv.tensor_scalar(x, x, cols[0:qn, 56 + i:57 + i], None, ALU.mult).then_inc(v.sig(v2p if i == 2 else vstep), 1)

                for h in range(8):
                    for i, (q0, qn) in enumerate(QT):
                        b, o = ((2 * (h % 2), 0), (2 * (h % 2), P), (2 * (h % 2) + 1, 0))[i]
                        if i != 1:
                            eng.wait_ge(full_for_vector[b], v.nth(full_for_vector[b]))
                        nv.tensor_reduce(cols[0:qn, 40 + i:41 + i], bank[b][0:qn, o:o + q0 + qn], AX_X, ALU.max).then_inc(v.sig(vstep), 1)
                    eng.wait_ge(*v.last)
                    for i, (q0, qn) in enumerate(QT):
                        nv.tensor_scalar(cols[0:qn, 52 + i:53 + i], cols[0:qn, 40 + i:41 + i], -1.0, None, ALU.mult).then_inc(v.sig(v2a), 1)
                    finish(h)
                nv.memset(cols[:, 60:61], 0.0).then_inc(v.sig(v2p), 1)

            def ssd_out(l, j):
                b = 6 + j % 2
                eng.wait_ge(full_for_vector[b], v.nth(full_for_vector[b]))
                nv.scalar_tensor_tensor(out=tl(US, j, T), in0=tl(2, j, T), scalar=pc(f"dskip{l}", j), in1=bank[b][:, 0:T],
                                             op0=ALU.mult, op1=ALU.add).then_inc(v.sig(free["vector"][b]), 1)
                eng.wait_ge(*v.last)
                nv.tensor_tensor(tl(US, j, T), tl(US, j, T), tl(3, j, T), ALU.mult).then_inc(v.sig(v2a if j == 3 else vstep), 1)

            for l in range(DEPTH):
                ffn(3 + 3 * l, T)
                residual(T, scale=0.5)
                norm(4 + 3 * l, T)
                mixer(l)
                residual(T)
                norm(5 + 3 * l, T)
                ffn(5 + 3 * l, T)
                residual(T, scale=0.5)
                norm(6 + 3 * l, T)

        @block.gpsimd
        def _(eng):
            g = Counts()
            g.sent[ada_used] = FIRST * PIECE_SLABS

            def rest(out, whole, part, signal):
                ng.tensor_tensor(out, whole, part, ALU.subtract).then_inc(signal, 1)

            def weights_low(q):
                eng.wait_ge(high_ready, q + 1)
                rest(ring_low[:, HL[q] % RING], ring[:, HL[q] % RING], high[:, q % HIGHS].bitcast(F32), low_by_gpsimd)

            def stage(n, T, Tn):
                q0 = STAGE_AT[n]
                weights_low(q0)
                weights_low(q0 + 1)
                for j in range(DT):
                    eng.wait_ge(input_high_ready, g.nth(input_high_ready))
                    eng.wait_ge(input_whole, g.nth(input_whole))
                    rest(input_rest(j, Tn), tl(US, j, Tn, xview(Tn)), input_high(STAGES[n], j, Tn).bitcast(F32), input_low)
                weights_low(q0 + 2)
                if STAGES[n] == "ffn":
                    for f in range(FT):
                        eng.wait_ge(hidden_ready, g.nth(hidden_ready))
                        rest(hidden_rest(f, T), tl(6 + f // DT, f % DT, T), hidden_high(f, T).bitcast(F32), hidden_low)
                for q in range(q0 + HIGHS, STAGE_AT[n + 1]):
                    if not low_by_vector_engine(q):
                        weights_low(q)

            eng.wait_ge(ada_used, FIRST * PIECE_SLABS)
            for n in range(FIRST, len(PIECES)):
                for k in range(DT):
                    a = PIECE_SLABS * n + k // 2
                    w_k = ada_ring[:, a % HIGHS, k % 2]
                    eng.wait_ge(ada_scaled, g.nth(ada_scaled))
                    if k:
                        if k > 1:
                            eng.wait_ge(*g.last)
                        ng.tensor_tensor(acc[:, n % 2], acc[:, n % 2], w_k, ALU.add).then_inc(g.sig(ada_used if k % 2 else pool_step), 1)
                eng.wait_ge(*g.last)
                ng.tensor_copy(acc[:, n % 2, 0:1], acc[:, n % 2, 0:1]).then_inc(later_piece, 1)

            for n in range(len(STAGES)):
                if n == 3:
                    eng.wait_ge(a2g, 1)
                    rest(input_parts["low"][:, :, 0:META], arena[:, US, :, 0:META],
                         input_parts["ffn"][:, :, 0:META].bitcast(F32), meta_low)
                stage(n, SEQ if n < 3 else TALL, SEQ if n < 4 else TALL)


def _pack_stream(x):
    def padded(a, rows=P, width=P):
        full = np.zeros((rows, width), np.float32)
        full[: a.shape[0], : a.shape[1]] = a
        return full

    rk = x["rwkv_w_rkv"][0]
    gin = x["gdn_w_in"][0]
    dense = {
        ("rwkv_r", 0): rk[0], ("rwkv_k", 0): rk[1], ("rwkv_v", 0): rk[2],
        ("w1a1", 0): np.concatenate([x["rwkv_w1"][0], x["rwkv_a1"][0]], 1),
        ("w2a2", 0): np.concatenate([x["rwkv_w2"][0], x["rwkv_a2"][0]], 0),
        ("g1", 0): x["rwkv_g1"][0], ("g2", 0): x["rwkv_g2"][0], ("rwkv_out", 0): x["rwkv_w_out"][0],
        ("gdn_in", 0): gin[:, : 4 * D], ("gdn_out", 0): x["gdn_w_out"][0],
        ("gdn_ba", 0): np.concatenate([gin[P * k:P * k + P, 4 * D:] for k in range(8)], 1),
    }
    for i in range(DEPTH):
        dense["ffn_in", i], dense["ffn_out", i] = x["ffn_w_in"][i], x["ffn_w_out"][i]
        for f in (1, 2):
            dense[f"gate{f}", i] = x[f"ffn{f}_w_gate_2"][i]
            dense[f"up{f}", i] = x[f"ffn{f}_w_up_2"][i]
            dense[f"down{f}", i] = x[f"ffn{f}_w_down_2"][i]
        wi = x["w_in_2"][i]
        z, xbc, dt_, fq, fk, fv, f_, cq, ckv, kr = np.split(wi, np.cumsum([512, 768, 8, 256, 256, 256, 4, 256, 128]), 1)
        dense["mix_in", i] = np.concatenate([xbc, z, fq, fk, fv, cq, ckv], 1)
        dtf = np.concatenate([dt_, f_], 1)
        dense["dtf", i] = padded(np.concatenate([dtf[P * k:P * k + P] for k in range(8)], 1))
        swapped = np.concatenate([kr[:, 16:], kr[:, :16]], 1)
        dense["kr", i] = np.concatenate([np.tile(kr, (1, 4)), np.tile(swapped, (1, 4))], 1)
        uq = x["mla_w_uq_2"][i].reshape(256, 4, 96)
        rope = uq[:, :, 64:]
        dense["uq", i] = np.concatenate(
            [uq[:, :, :64].reshape(256, 256), rope.reshape(256, P),
             np.concatenate([rope[:, :, 16:], rope[:, :, :16]], 2).reshape(256, P)], 1)
        ukv = x["mla_w_ukv_2"][i].reshape(P, 4, 128)
        dense["ukv", i] = np.concatenate([ukv[:, :, :64].reshape(P, 256), ukv[:, :, 64:].reshape(P, 256)], 1)
        dense["mix_out", i] = x["w_out_2"][i]
    m = manifest()
    out = np.zeros((-(-len(m) // BLOCKS), P, BLOCKS, P), np.float32)
    for at, (name, layer, n, k) in enumerate(m):
        if name == "pad":
            continue
        out[at // BLOCKS, :, at % BLOCKS] = dense[name, layer][P * k:P * k + P, P * n:P * n + P]
    return out


def _pack_ada(x):
    out = np.empty((ADA_SLABS, P, 2, D), np.float32)
    for n, (i, q) in enumerate(PIECES):
        piece = x["ada_w"][i][:, D * q:D * q + D].reshape(PIECE_SLABS, 2, P, D)
        out[PIECE_SLABS * n:PIECE_SLABS * (n + 1)] = piece.transpose(0, 2, 1, 3)
    return out


def _pack_params(x):
    cols = param_columns()
    out = np.zeros((P, cols["_n"]), np.float32)

    def put(name, a, width=1):
        a = np.asarray(a).reshape(-1)
        if a.size >= P:
            a = a.reshape(-1, P).T
            out[:, cols[name]:cols[name] + a.shape[1]] = a
        else:
            out[: a.size, cols[name]] = a

    for i in range(DEPTH):
        put(f"ada_b{i}", x["ada_b"][i])
        for s in range(2):
            put(f"ln_g{i}{s}", x["ln_g"][i, s])
            put(f"ln_b{i}{s}", x["ln_b"][i, s])
    put("mu", x["rwkv_mu"][0])
    for n in ("w0", "a0", "k_k", "k_a", "r_k", "gn_g", "gn_b"):
        put(n, x["rwkv_" + n][0])
    put("gdn_conv", x["gdn_conv"][0])
    put("gdn_norm", x["gdn_norm_g"][0])
    put("gdn_alog", x["gdn_a_log"][0])
    put("gdn_dtb", x["gdn_dt_bias"][0])
    for i in range(DEPTH):
        for s in (1, 2, 3):
            put(f"ln{s}_g{i}", x[f"ln{s}_g_2"][i])
            put(f"ln{s}_b{i}", x[f"ln{s}_b_2"][i])
        put(f"conv_w{i}", x["conv_w_2"][i])
        put(f"conv_b{i}", x["conv_b_2"][i])
        put(f"dtb{i}", np.concatenate([x["dt_bias_2"][i], x["fox_f_b_2"][i]]))
        put(f"alog{i}", x["a_log_2"][i])
        put(f"dskip{i}", np.repeat(x["d_skip_2"][i], 64))
        put(f"ssd_g{i}", x["ssd_norm_g_2"][i])
        put(f"mlaq{i}", x["mla_q_norm_g_2"][i])
        put(f"mlakv{i}", x["mla_kv_norm_g_2"][i])
    return out


def _features_first(a):
    return np.ascontiguousarray(a.reshape(a.shape[0], DT, P).transpose(2, 1, 0))


def kernel(**inputs):
    import concourse.bacc as bacc
    from concourse.bass_utils import run_bass_kernel_spmd

    x = {k: np.asarray(v) for k, v in inputs.items()}
    _, const = constants()
    arrays = {
        "stream": _pack_stream(x), "ada": _pack_ada(x), "params": _pack_params(x), "consts": const,
        "xin": _features_first(x["x"][0]),
        "cin": np.ascontiguousarray(x["c"].reshape(DT, P).T),
        "meta": _features_first(x["meta_2"]),
    }
    nc = bacc.Bacc("TRN2", target_bir_lowering=False, num_devices=1)
    args = [nc.dram_tensor(n, a.shape, F32, kind="ExternalInput").ap() for n, a in arrays.items()]
    out = nc.dram_tensor("out", (P, DT, SEQ), F32, kind="ExternalOutput").ap()
    first_and_second_block(nc, *args, out)
    r = run_bass_kernel_spmd(nc, [arrays], core_ids=[0])
    y = r.results[0]["out"]
    return np.ascontiguousarray(y.transpose(2, 1, 0)).reshape(1, SEQ, D)
```
